# Optimizing a Trainium2 kernel written in Bass

```python
import jax, jax.numpy as jnp
from jax import lax
import numpy as np

D_MODEL = 1024
BATCH = 1
SEQ = 512
DEPTH = 1

D_FF = 2816
D_PLE = 256
D_GMLP = D_MODEL
N_SGU_GROUPS = 4
CHUNK = 128
D_POOL = D_MODEL
POOL_WINDOWS = (2, 4, 8, 16)
N_POOL_GROUPS = len(POOL_WINDOWS)
D_IN = 2 * D_GMLP + D_POOL + 2 * D_MODEL
EPS = 1e-6


def _rmsnorm(x, g):
    xf = x.astype(jnp.float32)
    y = xf * lax.rsqrt(jnp.mean(xf * xf, axis=-1, keepdims=True) + EPS)
    return (y * g.astype(jnp.float32)).astype(x.dtype)

def _layernorm(x, g):
    xf = x.astype(jnp.float32)
    mu = jnp.mean(xf, axis=-1, keepdims=True)
    xc = xf - mu
    y = xc * lax.rsqrt(jnp.mean(xc * xc, axis=-1, keepdims=True) + EPS)
    return (y * g.astype(jnp.float32)).astype(x.dtype)

def _swiglu(xn, w_gate, w_up, w_down):
    return (jax.nn.silu(xn @ w_gate) * (xn @ w_up)) @ w_down

def _spatial_gating(u, v, norm_g, w_s, b_s):
    B, S, _ = v.shape
    dg = D_GMLP // N_SGU_GROUPS
    v = _layernorm(v, norm_g)
    vc = v.reshape(B, S // CHUNK, CHUNK, N_SGU_GROUPS, dg)
    causal = jnp.tril(jnp.ones((CHUNK, CHUNK), dtype=bool))
    ws = jnp.where(causal[None], w_s, 0.0).astype(v.dtype)
    sv = jnp.einsum('gts,bcsgd->bctgd', ws, vc) + b_s.T[:, :, None].astype(v.dtype)
    return u * sv.reshape(B, S, D_GMLP)

def _pool_mixer(c, pool_w, pool_scale):
    B, S, _ = c.shape
    dg = D_POOL // N_POOL_GROUPS
    cf = c.astype(jnp.float32)
    cs = jnp.concatenate([jnp.zeros((B, 1, D_POOL), jnp.float32), jnp.cumsum(cf, axis=1)], axis=1)
    t = jnp.arange(S)
    outs = []
    for gi, w in enumerate(POOL_WINDOWS):
        lo = jnp.maximum(t + 1 - w, 0)
        sl = slice(gi * dg, (gi + 1) * dg)
        csg = cs[:, :, sl]
        count = (t + 1 - lo).astype(jnp.float32)[None, :, None]
        mean = (csg[:, 1:] - csg[:, lo]) / count
        diff = (mean - cf[:, :, sl]).astype(c.dtype)
        outs.append(jnp.einsum('bsc,cd->bsd', diff, pool_w[gi]))
    return jnp.concatenate(outs, axis=-1) * pool_scale

def _token_mixer(xn, w_in, sgu_norm_g, sgu_w, sgu_b, pool_w, pool_scale, w_out_a, w_out_b, w_o):
    z = xn @ w_in
    i1 = D_GMLP
    i2 = 2 * D_GMLP
    i3 = i2 + D_POOL
    i4 = i3 + D_MODEL
    u = jax.nn.gelu(z[..., :i1])
    v = jax.nn.gelu(z[..., i1:i2])
    c = z[..., i2:i3]
    ga = z[..., i3:i4]
    gb = z[..., i4:]
    a = _spatial_gating(u, v, sgu_norm_g, sgu_w, sgu_b)
    b = _pool_mixer(c, pool_w, pool_scale)
    y = jax.nn.sigmoid(ga) * (a @ w_out_a) + jax.nn.sigmoid(gb) * (b @ w_out_b)
    return y @ w_o

def _gain(k, shape):
    return 1.0 + 0.02 * jax.random.normal(k, shape, jnp.float32)

def _w(k, shape, fan_in):
    return jax.random.normal(k, shape, jnp.float32) * (fan_in ** -0.5)

def first_inputs(seed: int = 0) -> dict:
    key = jax.random.key(seed)
    ks = jax.random.split(key, 32)
    L = DEPTH
    dgp = D_POOL // N_POOL_GROUPS
    return {
        "x": jax.random.normal(ks[0], (BATCH, SEQ, D_MODEL), jnp.float32),
        "p": jax.random.normal(ks[1], (DEPTH, BATCH, SEQ, D_PLE), jnp.float32),
        "ffn1_pre_g": _gain(ks[2], (L, D_MODEL)),
        "ffn1_w_gate": _w(ks[3], (L, D_MODEL, D_FF), D_MODEL),
        "ffn1_w_up": _w(ks[4], (L, D_MODEL, D_FF), D_MODEL),
        "ffn1_w_down": _w(ks[5], (L, D_FF, D_MODEL), D_FF),
        "ffn1_post_g": _gain(ks[6], (L, D_MODEL)),
        "mix_pre_g": _gain(ks[7], (L, D_MODEL)),
        "w_in": _w(ks[8], (L, D_MODEL, D_IN), D_MODEL),
        "sgu_norm_g": _gain(ks[9], (L, D_GMLP)),
        "sgu_w": _w(ks[10], (L, N_SGU_GROUPS, CHUNK, CHUNK), CHUNK),
        "sgu_b": _gain(ks[11], (L, N_SGU_GROUPS, CHUNK)),
        "pool_w": _w(ks[12], (L, N_POOL_GROUPS, dgp, dgp), dgp),
        "pool_scale": _gain(ks[13], (L, D_POOL)),
        "w_out_a": _w(ks[14], (L, D_GMLP, D_MODEL), D_GMLP),
        "w_out_b": _w(ks[15], (L, D_POOL, D_MODEL), D_POOL),
        "w_o": _w(ks[16], (L, D_MODEL, D_MODEL), D_MODEL),
        "mix_post_g": _gain(ks[17], (L, D_MODEL)),
        "ffn2_pre_g": _gain(ks[18], (L, D_MODEL)),
        "ffn2_w_gate": _w(ks[19], (L, D_MODEL, D_FF), D_MODEL),
        "ffn2_w_up": _w(ks[20], (L, D_MODEL, D_FF), D_MODEL),
        "ffn2_w_down": _w(ks[21], (L, D_FF, D_MODEL), D_FF),
        "ffn2_post_g": _gain(ks[22], (L, D_MODEL)),
        "ple_pre_g": _gain(ks[23], (L, D_MODEL)),
        "ple_w_gate": _w(ks[24], (L, D_MODEL, D_MODEL), D_MODEL),
        "ple_w_proj": _w(ks[25], (L, D_PLE, D_MODEL), D_PLE),
        "ple_post_g": _gain(ks[26], (L, D_MODEL)),
    }

def first_block(x, p, ffn1_pre_g, ffn1_w_gate, ffn1_w_up, ffn1_w_down, ffn1_post_g,
              mix_pre_g, w_in, sgu_norm_g, sgu_w, sgu_b, pool_w, pool_scale,
              w_out_a, w_out_b, w_o, mix_post_g,
              ffn2_pre_g, ffn2_w_gate, ffn2_w_up, ffn2_w_down, ffn2_post_g,
              ple_pre_g, ple_w_gate, ple_w_proj, ple_post_g):
    h = x
    for i in range(DEPTH):
        f = _swiglu(_rmsnorm(h, ffn1_pre_g[i]), ffn1_w_gate[i], ffn1_w_up[i], ffn1_w_down[i])
        h = h + 0.5 * _rmsnorm(f, ffn1_post_g[i])
        m = _token_mixer(_rmsnorm(h, mix_pre_g[i]), w_in[i], sgu_norm_g[i], sgu_w[i], sgu_b[i],
                         pool_w[i], pool_scale[i], w_out_a[i], w_out_b[i], w_o[i])
        h = h + _rmsnorm(m, mix_post_g[i])
        f = _swiglu(_rmsnorm(h, ffn2_pre_g[i]), ffn2_w_gate[i], ffn2_w_up[i], ffn2_w_down[i])
        h = h + 0.5 * _rmsnorm(f, ffn2_post_g[i])
        gate = jax.nn.sigmoid(_rmsnorm(h, ple_pre_g[i]) @ ple_w_gate[i])
        e = p[i] @ ple_w_proj[i]
        h = h + _rmsnorm(gate * e, ple_post_g[i])
    return h


PLE_DIM = 256
D_MIX = D_MODEL
HEAD_DIM = 64
RMS_EPS = 1e-6

CONV_W = D_MIX // 4
CONV_K = 3

NSA_HEADS = 6
NSA_KV_HEADS = 2
NSA_GROUP = NSA_HEADS // NSA_KV_HEADS
NSA_W = NSA_HEADS * HEAD_DIM
NSA_KV_W = NSA_KV_HEADS * HEAD_DIM
CMP_BLOCK = 32
CMP_STRIDE = 16
SLC_BLOCK = 64
SLC_TOPK = 16
WIN = 512
Q_BLOCK = 128
FORCE_SCORE = 1e4

DIL_PAIRS = ((128, 1), (512, 4), (2048, 16))
DIL_HEADS_PER_PAIR = 2
DIL_HEADS = DIL_HEADS_PER_PAIR * len(DIL_PAIRS)
DIL_W = DIL_HEADS * HEAD_DIM
DIL_BLOCK = 128

IN_SIZES = ((CONV_W,) * 4
            + (NSA_W,) + (NSA_KV_W,) * 6
            + (NSA_HEADS * 3, NSA_W)
            + (DIL_W,) * 4)
D_IN_2 = sum(IN_SIZES)


def _rmsnorm_2(x, g):
    x32 = x.astype(jnp.float32)
    y = x32 * lax.rsqrt(jnp.mean(x32 * x32, axis=-1, keepdims=True) + RMS_EPS)
    return (y * g.astype(jnp.float32)).astype(x.dtype)

def _masked_softmax(s, mask):
    s = jnp.where(mask, s.astype(jnp.float32), -jnp.inf)
    m = jnp.max(s, axis=-1, keepdims=True)
    m = jnp.where(jnp.isfinite(m), m, 0.0)
    e = jnp.where(mask, jnp.exp(s - m), 0.0)
    den = jnp.sum(e, axis=-1, keepdims=True)
    return e / jnp.maximum(den, 1e-30), m, den

def _short_conv(u, w, b):
    y = lax.conv_general_dilated(
        u, w[:, None, :].astype(u.dtype), window_strides=(1,), padding=((CONV_K - 1, 0),),
        dimension_numbers=("NWC", "WIO", "NWC"), feature_group_count=u.shape[-1])
    return y + b.astype(u.dtype)

def _nsa(q, kc_raw, vc_raw, ks_raw, vs_raw, kw_raw, vw_raw, gates, pe, w1, w2):
    B, T, G, R, E = q.shape
    scale = E ** -0.5
    n_cmp = (T - CMP_BLOCK) // CMP_STRIDE + 1
    cmp_start = jnp.arange(n_cmp) * CMP_STRIDE
    cmp_idx = cmp_start[:, None] + jnp.arange(CMP_BLOCK)[None, :]

    def compress(a, pe_, w1_, w2_):
        blk = a[:, cmp_idx] + pe_[None, None, :, None, :].astype(a.dtype)
        flat = jnp.moveaxis(blk, 3, 2).reshape(B, n_cmp, G, CMP_BLOCK * E)
        return jax.nn.silu(flat @ w1_) @ w2_

    k_cmp = compress(kc_raw, pe[0], w1[0], w2[0])
    v_cmp = compress(vc_raw, pe[1], w1[1], w2[1])
    cmp_last = cmp_start + CMP_BLOCK - 1
    n_slc = T // SLC_BLOCK
    slc_start = jnp.arange(n_slc) * SLC_BLOCK
    overlap = ((cmp_start[:, None] < slc_start[None, :] + SLC_BLOCK)
               & (cmp_start[:, None] + CMP_BLOCK > slc_start[None, :])).astype(jnp.float32)
    k_slc = ks_raw.reshape(B, n_slc, SLC_BLOCK, G, E).transpose(0, 3, 1, 2, 4)
    v_slc = vs_raw.reshape(B, n_slc, SLC_BLOCK, G, E).transpose(0, 3, 1, 2, 4)
    top = min(SLC_TOPK, n_slc)
    b_ix = jnp.arange(B)[:, None, None, None]
    g_ix = jnp.arange(G)[None, None, :, None]
    k_win = jnp.pad(kw_raw, ((0, 0), (WIN, 0), (0, 0), (0, 0)))
    v_win = jnp.pad(vw_raw, ((0, 0), (WIN, 0), (0, 0), (0, 0)))

    def block(qi):
        q0 = qi * Q_BLOCK
        t = q0 + jnp.arange(Q_BLOCK)
        qb = lax.dynamic_slice_in_dim(q, q0, Q_BLOCK, axis=1)
        gb = lax.dynamic_slice_in_dim(gates, q0, Q_BLOCK, axis=1)
        s_c = jnp.einsum("bqgrd,bngd->bqgrn", qb, k_cmp) * scale
        m_c = (cmp_last[None, :] <= t[:, None])[None, :, None, None, :]
        p_c, _, _ = _masked_softmax(s_c, m_c)
        o_c = jnp.einsum("bqgrn,bngd->bqgrd", p_c.astype(qb.dtype), v_cmp)
        imp = jnp.einsum("bqgrn,ns->bqgs", p_c, overlap)
        blk = jnp.arange(n_slc)[None, :]
        cur = (t // SLC_BLOCK)[:, None]
        forced = (blk == 0) | (blk == cur) | (blk == cur - 1)
        causal = blk * SLC_BLOCK <= t[:, None]
        imp = jnp.where(forced[None, :, None, :], FORCE_SCORE, imp)
        imp = jnp.where(causal[None, :, None, :], imp, -1.0)
        _, sel = lax.top_k(imp, top)
        k_sel = k_slc[b_ix, g_ix, sel]
        v_sel = v_slc[b_ix, g_ix, sel].reshape(B, Q_BLOCK, G, top * SLC_BLOCK, E)
        pos = sel[..., None] * SLC_BLOCK + jnp.arange(SLC_BLOCK)
        m_s = (pos <= t[None, :, None, None, None]).reshape(B, Q_BLOCK, G, 1, top * SLC_BLOCK)
        s_s = jnp.einsum("bqgrd,bqgkld->bqgrkl", qb, k_sel).reshape(
            B, Q_BLOCK, G, R, top * SLC_BLOCK) * scale
        p_s, _, _ = _masked_softmax(s_s, m_s)
        o_s = jnp.einsum("bqgrk,bqgkd->bqgrd", p_s.astype(qb.dtype), v_sel)
        kw = lax.dynamic_slice_in_dim(k_win, q0, WIN + Q_BLOCK, axis=1)
        vw = lax.dynamic_slice_in_dim(v_win, q0, WIN + Q_BLOCK, axis=1)
        kpos = q0 - WIN + jnp.arange(WIN + Q_BLOCK)
        dist = t[:, None] - kpos[None, :]
        m_w = ((dist >= 0) & (dist < WIN) & (kpos[None, :] >= 0))[None, :, None, None, :]
        s_w = jnp.einsum("bqgrd,bkgd->bqgrk", qb, kw) * scale
        p_w, _, _ = _masked_softmax(s_w, m_w)
        o_w = jnp.einsum("bqgrk,bkgd->bqgrd", p_w.astype(qb.dtype), vw)
        return gb[..., 0:1] * o_c + gb[..., 1:2] * o_s + gb[..., 2:3] * o_w

    out = lax.map(block, jnp.arange(T // Q_BLOCK))
    return jnp.moveaxis(out, 0, 1).reshape(B, T, G * R * E)

def _dilated_group(q, k, v, window, dil):
    B, T, H, E = q.shape
    L = T // dil
    Lp = -(-L // DIL_BLOCK) * DIL_BLOCK
    nb = Lp // DIL_BLOCK
    steps = window // dil

    def sub(a):
        a = a.reshape(B, L, dil, H, E).transpose(0, 2, 3, 1, 4)
        a = jnp.pad(a, ((0, 0), (0, 0), (0, 0), (0, Lp - L), (0, 0)))
        return a.reshape(B, dil, H, nb, DIL_BLOCK, E)

    def with_prev(a):
        prev = jnp.concatenate([jnp.zeros_like(a[:, :, :, :1]), a[:, :, :, :-1]], axis=3)
        return jnp.concatenate([prev, a], axis=4)

    qs = sub(q)
    kc = with_prev(sub(k))
    vc = with_prev(sub(v))
    s = jnp.einsum("bdhnqe,bdhnke->bdhnqk", qs, kc) * (E ** -0.5)
    a_i = jnp.arange(DIL_BLOCK)
    c_i = jnp.arange(2 * DIL_BLOCK)
    dist = a_i[:, None] + DIL_BLOCK - c_i[None, :]
    j = jnp.arange(nb)[:, None, None] * DIL_BLOCK - DIL_BLOCK + c_i[None, None, :]
    mask = (dist[None] >= 0) & (dist[None] <= steps) & (j >= 0)
    p, m, den = _masked_softmax(s, mask)
    o = jnp.einsum("bdhnqk,bdhnke->bdhnqe", p.astype(v.dtype), vc)
    lse = (m + jnp.log(den))[..., 0]
    o = o.reshape(B, dil, H, Lp, E)[:, :, :, :L].transpose(0, 3, 1, 2, 4).reshape(B, T, H, E)
    lse = lse.reshape(B, dil, H, Lp)[:, :, :, :L].transpose(0, 3, 1, 2).reshape(B, T, H)
    return o, lse

def _dilated_mixer(q, k, v):
    B, T, _, E = q.shape
    outs, lses = [], []
    for gi, (window, dil) in enumerate(DIL_PAIRS):
        sl = slice(gi * DIL_HEADS_PER_PAIR, (gi + 1) * DIL_HEADS_PER_PAIR)
        o, lse = _dilated_group(q[:, :, sl], k[:, :, sl], v[:, :, sl], window, dil)
        outs.append(o)
        lses.append(lse)
    alpha = jax.nn.softmax(jnp.stack(lses, axis=0), axis=0)
    y = jnp.concatenate([alpha[gi][..., None].astype(outs[gi].dtype) * outs[gi]
                         for gi in range(len(DIL_PAIRS))], axis=2)
    return y.reshape(B, T, DIL_W)

def second_inputs(seed: int = 0) -> dict:
    key = jax.random.key(seed)
    ks = jax.random.split(key, 13)
    f32 = jnp.float32
    x = jax.random.normal(ks[0], (BATCH, SEQ, D_MODEL), f32)
    p = jax.random.normal(ks[1], (DEPTH, BATCH, SEQ, PLE_DIM), f32)
    norm_mix = 1.0 + 0.05 * jax.random.normal(ks[2], (DEPTH, D_MODEL), f32)
    w_in = jax.random.normal(ks[3], (DEPTH, D_MODEL, D_IN_2), f32) * D_MODEL ** -0.5
    conv_w = jax.random.normal(ks[4], (DEPTH, CONV_K, CONV_W), f32) * CONV_K ** -0.5
    conv_b = 0.02 * jax.random.normal(ks[5], (DEPTH, CONV_W), f32)
    cmp_pe = 0.5 * jax.random.normal(ks[6], (DEPTH, 2, CMP_BLOCK, HEAD_DIM), f32)
    cmp_w1 = jax.random.normal(ks[7], (DEPTH, 2, CMP_BLOCK * HEAD_DIM, HEAD_DIM), f32) * (CMP_BLOCK * HEAD_DIM) ** -0.5
    cmp_w2 = jax.random.normal(ks[8], (DEPTH, 2, HEAD_DIM, HEAD_DIM), f32) * HEAD_DIM ** -0.5
    w_out = jax.random.normal(ks[9], (DEPTH, D_MIX, D_MODEL), f32) * D_MIX ** -0.5
    w_ple_gate = jax.random.normal(ks[10], (DEPTH, D_MODEL, D_MODEL), f32) * D_MODEL ** -0.5
    w_ple_proj = jax.random.normal(ks[11], (DEPTH, PLE_DIM, D_MODEL), f32) * PLE_DIM ** -0.5
    norm_final = 1.0 + 0.05 * jax.random.normal(ks[12], (D_MODEL,), f32)
    return {"x": x, "p": p, "norm_mix": norm_mix, "w_in": w_in, "conv_w": conv_w,
            "conv_b": conv_b, "cmp_pe": cmp_pe, "cmp_w1": cmp_w1, "cmp_w2": cmp_w2,
            "w_out": w_out, "w_ple_gate": w_ple_gate, "w_ple_proj": w_ple_proj,
            "norm_final": norm_final}

def second_block(x, p, norm_mix, w_in, conv_w, conv_b, cmp_pe, cmp_w1, cmp_w2,
              w_out, w_ple_gate, w_ple_proj, norm_final):
    B, T, _ = x.shape
    E = HEAD_DIM
    split_points = np.cumsum(IN_SIZES)[:-1].tolist()
    h = x
    for i in range(DEPTH):
        xn = _rmsnorm_2(h, norm_mix[i])
        u = xn @ w_in[i]
        (a_b, a_c, a_h, a_z,
         n_q, n_kc, n_vc, n_ks, n_vs, n_kw, n_vw, n_g, n_z,
         d_q, d_k, d_v, d_z) = jnp.split(u, split_points, axis=-1)
        y_a = a_b * _short_conv(a_c * a_h, conv_w[i], conv_b[i]) * jax.nn.silu(a_z)
        kv = lambda a: a.reshape(B, T, NSA_KV_HEADS, E)
        gates = jax.nn.sigmoid(n_g.astype(jnp.float32)).astype(u.dtype).reshape(
            B, T, NSA_KV_HEADS, NSA_GROUP, 3)
        y_b = _nsa(n_q.reshape(B, T, NSA_KV_HEADS, NSA_GROUP, E), kv(n_kc), kv(n_vc),
                   kv(n_ks), kv(n_vs), kv(n_kw), kv(n_vw), gates,
                   cmp_pe[i], cmp_w1[i], cmp_w2[i]) * jax.nn.silu(n_z)
        hd = lambda a: a.reshape(B, T, DIL_HEADS, E)
        y_c = _dilated_mixer(hd(d_q), hd(d_k), hd(d_v)) * jax.nn.silu(d_z)
        h = h + jnp.concatenate([y_a, y_b, y_c], axis=-1) @ w_out[i]
        gate = jax.nn.sigmoid((h @ w_ple_gate[i]).astype(jnp.float32)).astype(h.dtype)
        h = h + gate * (p[i] @ w_ple_proj[i])
    return _rmsnorm_2(h, norm_final)


def setup_inputs(seed=0):
    out = dict(first_inputs(seed))
    for name, value in second_inputs(seed + 1).items():
        if name != "x":
            out[name + "_2"] = value
    return out


def reference(
    x, p, ffn1_pre_g, ffn1_w_gate, ffn1_w_up, ffn1_w_down, ffn1_post_g, mix_pre_g, w_in,
    sgu_norm_g, sgu_w, sgu_b, pool_w, pool_scale, w_out_a, w_out_b, w_o, mix_post_g, ffn2_pre_g,
    ffn2_w_gate, ffn2_w_up, ffn2_w_down, ffn2_post_g, ple_pre_g, ple_w_gate, ple_w_proj,
    ple_post_g, p_2, norm_mix_2, w_in_2, conv_w_2, conv_b_2, cmp_pe_2, cmp_w1_2, cmp_w2_2,
    w_out_2, w_ple_gate_2, w_ple_proj_2, norm_final_2,
):
    x = first_block(
        x, p, ffn1_pre_g, ffn1_w_gate, ffn1_w_up, ffn1_w_down, ffn1_post_g, mix_pre_g, w_in,
        sgu_norm_g, sgu_w, sgu_b, pool_w, pool_scale, w_out_a, w_out_b, w_o, mix_post_g,
        ffn2_pre_g, ffn2_w_gate, ffn2_w_up, ffn2_w_down, ffn2_post_g, ple_pre_g, ple_w_gate,
        ple_w_proj, ple_post_g,
    )
    return second_block(
        x, p_2, norm_mix_2, w_in_2, conv_w_2, conv_b_2, cmp_pe_2, cmp_w1_2, cmp_w2_2, w_out_2,
        w_ple_gate_2, w_ple_proj_2, norm_final_2,
    )


_drawn_inputs = setup_inputs


def setup_inputs(seed=0):
    import zlib

    import numpy as np

    out = dict(_drawn_inputs(seed))
    spreads = {}
    factors = {'ffn1_pre_g': 4.346,
     'ffn1_post_g': 6.114,
     'mix_pre_g': 3.965,
     'sgu_norm_g': 23.774,
     'sgu_b': 8.0,
     'pool_scale': 6.094,
     'mix_post_g': 4.649,
     'ffn2_pre_g': 7.28,
     'ffn2_post_g': 8.0,
     'ple_pre_g': 8.0,
     'ple_post_g': 5.193,
     'norm_mix_2': 3.697,
     'conv_b_2': 34.098,
     'cmp_pe_2': 3.257,
     'p_2': 4.297,
     'w_ple_gate_2': 6.116,
     'w_ple_proj_2': 4.275}
    for name, (base, spread) in spreads.items():
        noise = np.random.default_rng([zlib.crc32(name.encode()), seed]).standard_normal(out[name].shape)
        drawn = base * np.exp(spread * noise) if base else spread * noise
        out[name] = __import__('jax').numpy.asarray(drawn.astype(out[name].dtype))
    for name, factor in factors.items():
        out[name] = (out[name] * factor).astype(out[name].dtype)
    return out
```

```python
from contextlib import ExitStack

import concourse.bass as bass
from concourse import mybir

F32 = mybir.dt.float32
F32R = mybir.dt.float32r
BF16 = mybir.dt.bfloat16
ALU = mybir.AluOpType
ACT = mybir.ActivationFunctionType
AX = mybir.AxisListType.X

T = 512
D = 1024
FF = 2816
KD = D // 128
NEG = -1.0e30
EPS = 1e-6
NRAW = 3
NSPLIT = 3
AHEAD = 2

COLS = [("ffn1_pre_g", 8), ("ffn1_post_g", 8), ("mix_pre_g", 8), ("sgu_norm_g", 8), ("pool_scale", 8),
        ("mix_post_g", 8), ("ffn2_pre_g", 8), ("ffn2_post_g", 8), ("ple_pre_g", 8), ("ple_post_g", 8),
        ("norm_mix_2", 8), ("norm_final_2", 8), ("conv_w_2", 6), ("conv_b_2", 2)]


class Queue:

    def __init__(self, sem):
        self.sem, self.count, self.items, self.met = sem, 0, [], {}

    def put(self, make, *after, inc=True):
        waits = []
        for tok in flat(after):
            key = tok[0].name
            if self.met.get(key, 0) < tok[1]:
                self.met[key] = tok[1]
                waits.append(tok)
        self.items.append((waits, make, self.sem if inc else None))
        if inc:
            self.count += 1
            return (self.sem, self.count)
        return None

    def run(self, eng):
        for waits, make, sem in self.items:
            for s, v in waits:
                eng.wait_ge(s, v)
            ins = make(eng)
            if sem is not None:
                ins.then_inc(sem, 1)


def flat(toks):
    for t in toks:
        if t is None:
            continue
        if isinstance(t, list):
            yield from flat(t)
        else:
            yield t


def now(*toks):
    last = {}
    for s, v in flat(toks):
        if s.name not in last or last[s.name][1] < v:
            last[s.name] = (s, v)
    return list(last.values())


class Ring:

    def __init__(self, aps):
        self.aps, self.free, self.at = aps, [[] for _ in aps], 0

    def take(self):
        i = self.at % len(self.aps)
        self.at += 1
        return i, self.aps[i], self.free[i]


class Operand:

    def __init__(self, hi, lo, first=0):
        self.hi, self.lo, self.first = hi, lo, first
        n = hi.shape[1]
        self.ready = [[] for _ in range(n)]
        self.war = [[] for _ in range(n)]


def two_blocks(nc, a, out):
    ctx = ExitStack()
    with ctx:
        def sem(name):
            return ctx.enter_context(nc.semaphore(name))

        base, top = 16512, 229344
        place = {"at": base}

        def at(name, shape, dt, offset):
            return nc.alloc_sbuf_tensor_at(name, shape, dt, offset=offset)

        def sb(name, shape, dt):
            n = 1
            for s in shape[1:]:
                n *= s
            n *= 2 if dt == BF16 else 4
            o = place["at"]
            place["at"] = o + (n + 31) // 32 * 32
            assert place["at"] <= top, (name, place["at"] - top)
            return at(name, shape, dt, o), o

        h, _ = sb("h", [128, KD, T], F32)
        xh, _ = sb("xh", [128, KD, T], F32R)
        xl, _ = sb("xl", [128, KD, T], F32R)
        ah, ah_o = sb("ah", [128, KD, T], F32R)
        al, _ = sb("al", [128, KD, T], F32R)
        bh, bh_o = sb("bh", [128, KD, T], F32R)
        bl, _ = sb("bl", [128, KD, T], F32R)
        f, f_o = sb("f", [128, KD, T], F32)
        raw, _ = sb("raw", [128, NRAW, 1024], F32)
        whi, _ = sb("whi", [128, NSPLIT, 1024], F32R)
        wlo, _ = sb("wlo", [128, NSPLIT, 1024], F32R)
        act_t, _ = sb("act_t", [128, 4, T], F32)
        tmp_t, _ = sb("tmp_t", [128, 4, T], F32)
        sq_t, _ = sb("sq_t", [128, 2, T], F32)
        rstd, _ = sb("rstd", [128, T], F32)
        m_o = place["at"]
        place["at"] += 12 * 1024
        vnt, _ = sb("vnt", [128, 4, 256], F32)
        ident, _ = sb("ident", [128, 128], F32)
        identb, _ = sb("identb", [128, 128], BF16)
        ones, _ = sb("ones", [128, 128], F32)
        cols, _ = sb("cols", [128, 104], F32)
        half, _ = sb("half", [128, 16], F32)
        mcaus, _ = sb("mcaus", [128, 128], BF16)
        mband, _ = sb("mband", [128, 2, 128], BF16)
        md4, _ = sb("md4", [128, 2, 128], BF16)
        md16, _ = sb("md16", [128, 2, 128], BF16)
        mcmp, _ = sb("mcmp", [128, 4, 31], F32)
        eps, _ = sb("eps", [128, 1], F32)
        inv, _ = sb("inv", [128, 16], F32)
        gates, _ = sb("gates", [128, 4, 18], F32)
        mv, _ = sb("mv", [128, 4, 2], F32)
        bnst, _ = sb("bnst", [128, 4, 2, 6], F32)
        lnr, _ = sb("lnr", [128, 4], F32)
        poolw = at("poolw", [128, 4, 2, 256], F32, m_o)
        wst = at("wst", [128, 4, 128], F32, m_o + 8192)
        sgub = at("sgub", [128, 4, 128], F32, m_o + 10240)
        vtok = f[:, :, :].rearrange("p k t -> p (k t)").rearrange("p (i c) -> p i c", i=4)
        cpad = at("cpad", [128, 2, 528], F32, f_o)
        csum = at("csum", [128, 2, 528], F32, f_o + 4224)
        prow = at("prow", [128, 4, 256], F32, bh_o + 6 * 2048)
        qn = at("qn", [128, 3, T], F32, bh_o)
        kvn = at("kvn", [128, 4, T], F32, bh_o + 6144)
        dq = at("dq", [128, 3, T], F32, bh_o + 14336)
        dk = at("dk", [128, 3, T], F32, bh_o + 20480)
        cab = at("cab", [128, 2, T], F32, bh_o + 14336)
        cac = at("cac", [128, 2, T], F32, bh_o + 18432)
        ccv = at("ccv", [128, 2, T], F32, bh_o + 22528)
        blk = at("blk", [128, 31, 32], F32, bh_o + 26624)
        pcmp = at("pcmp", [128, 24, 32], F32, bh_o + 26624)
        vcs = at("vcs", [31, 128], F32, bh_o + 26624 + 4096)
        kcs = at("kcs", [128, 32], F32, bh_o + 26624 + 4608)
        hcs = at("hcs", [128, 32], F32, bh_o + 26624 + 4736)
        pes = at("pes", [128, 2, 32], F32, bh_o + 26624 + 4864)
        pcs = at("pcs", [128, 3, 24], F32, bh_o + 26624 + 5120)
        w2s = at("w2s", [128, 2, 64], F32, bh_o + 26624 + 5408)
        dv = at("dv", [128, 4, 384], F32, ah_o)
        odil = at("odil", [128, 3, T], F32, m_o)
        nz = at("nz", [128, 3, T], F32, m_o + 6144)
        ptr = at("ptr", [128, 4, T], F32, f_o)
        prb = at("prb", [128, 3, T], F32, f_o + 8192)
        stat = at("stat", [128, 256], F32, f_o + 14336)
        w1s = at("w1s", [128, 2, 32, 64], F32, f_o)
        perow = at("perow", [32, 2, 2, 64], F32, ah_o + 8192)

        G = [ctx.enter_context(nc.psum_tensor(f"G{i}", [128, T], F32)) for i in range(4)]
        X = [ctx.enter_context(nc.psum_tensor(f"X{i}", [128, T], F32)) for i in range(4)]
        gfree = [[] for _ in range(4)]
        xfree = [[] for _ in range(4)]

        pe, dve, sca, pool, sp = (Queue(sem(n)) for n in ("s_pe", "s_dve", "s_act", "s_pool", "s_sp"))
        raw_sem = [sem(f"s_raw{i}") for i in range(NRAW)]
        s_out = sem("s_out")
        n_sem = [0]

        def load(q, dst, src, *after, waits=1):
            n_sem[0] += 1
            s = sem(f"s_ld{n_sem[0]}")
            q.put(lambda e: e.dma_start(dst, src).then_inc(s, 16), *after, inc=False)
            return (s, 16)

        def mm(o, lhs, rhs, start, stop, *after, inc=False):
            return pe.put(lambda e: e.matmul(o, lhs, rhs, start=start, stop=stop), *after, inc=inc)

        def tr(o, i, idn, *after, inc=False):
            return pe.put(lambda e: e.transpose(o, i, idn), *after, inc=inc)

        def act(o, i, fn, *after, **kw):
            return sca.put(lambda e: e.activation(o, i, fn, **kw), *after)

        def copy(q, o, i, *after):
            if q is sca:
                return act(o, i, ACT.Copy, *after)
            return q.put(lambda e: e.tensor_copy(o, i), *after)

        def tt(q, o, i0, i1, op, *after):
            return q.put(lambda e: e.tensor_tensor(o, i0, i1, op), *after)

        def stt(o, i0, s, i1, op0, op1, *after):
            return dve.put(lambda e: e.scalar_tensor_tensor(o, i0, s, i1, op0, op1), *after)

        def ts(q, o, i, s1, s2, op0, op1, *after):
            if s2 is None:
                return q.put(lambda e: e.tensor_scalar(o, i, s1, None, op0), *after)
            return q.put(lambda e: e.tensor_scalar(o, i, s1, s2, op0, op1), *after)

        def red(o, i, op, *after, **kw):
            return dve.put(lambda e: e.tensor_reduce(o, i, AX, op, **kw), *after)

        def rec(o, i, *after):
            return dve.put(lambda e: e.reciprocal(o, i), *after)

        acts = Ring([act_t[:, i, :] for i in range(4)])
        tmps = Ring([tmp_t[:, i, :] for i in range(4)])
        sqs = Ring([sq_t[:, i, :] for i in range(2)])

        units = []
        split_done, pe_done = [], []
        sent = [0]
        raw_count = [0] * NRAW
        raw_tok = []

        def add_units(pieces_of, nk, wid):
            first = len(units)
            for k0 in range(0, nk, 2):
                units.append((pieces_of(k0, min(2, nk - k0)), min(2, nk - k0), wid))
            return (first, nk, wid)

        def plain(w, parts, row0=0):
            def pieces(k0, n):
                o, got = 0, []
                for c0, c1 in parts:
                    src = w[row0 + k0 * 128:row0 + (k0 + n) * 128, c0:c1].rearrange("(k p) c -> p k c", p=128)
                    got.append((0, 128, 0, n, o, c1 - c0, src))
                    o += c1 - c0
                return got
            return pieces

        def send(j):
            pieces, nk, wid = units[j]
            s = j % NRAW
            after = split_done[j - NRAW] if j >= NRAW else []
            v = raw[:, s, 0:nk * wid].rearrange("p (k c) -> p k c", k=nk)
            for p0, p1, k0, n, o, c, src in pieces:
                dst = v[p0:p1, k0:k0 + n, o:o + c] if o is not None else c(v[p0:p1, k0])
                sp.put(lambda e, dst=dst, src=src: e.dma_start(dst, src).then_inc(raw_sem[s], 16), after, inc=False)
                raw_count[s] += 16
            raw_tok.append((raw_sem[s], raw_count[s]))

        def split(j):
            pieces, nk, wid = units[j]
            n = nk * wid
            r, d = j % NRAW, j % NSPLIT
            used = pe_done[j - NSPLIT] if j >= NSPLIT else None
            hi = act(whi[:, d, 0:n], raw[:, r, 0:n], ACT.Copy, raw_tok[j], used)
            lo = tt(dve, wlo[:, d, 0:n], raw[:, r, 0:n], whi[:, d, 0:n].bitcast(F32), ALU.subtract, hi, raw_tok[j], used)
            split_done.append([hi, lo])

        def ahead(n):
            while len(split_done) <= min(n + AHEAD, len(units) - 1):
                while sent[0] <= min(len(split_done) + NRAW - 1, len(units) - 1):
                    send(sent[0])
                    sent[0] += 1
                split(len(split_done))

        background = []

        def pump():
            while background:
                try:
                    next(background[0])
                    return
                except StopIteration:
                    background.pop(0)

        def drain_background():
            while background:
                pump()

        def gemm(group, x, tiles, by_token=False, order=None, pumps=()):
            first, nk, wid = group
            done = [None] * tiles
            order = order or list(range(tiles))
            for u in range(0, nk, 2):
                n = first + u // 2
                ahead(n)
                d = n % NSPLIT
                kn = min(2, nk - u)
                tok = None
                for ti, m in enumerate(order):
                    for kk in range(kn):
                        k = u + kk
                        wv = [w[:, d, kk * wid:(kk + 1) * wid] for w in (whi, wlo)]
                        xv = [v[:, x.first + k, :] for v in (x.hi, x.lo)]
                        for wi, xi in ((0, 0), (0, 1), (1, 0)):
                            if by_token:
                                o, lhs, rhs = G[m][:, 0:wid], xv[xi][:, m * 128:(m + 1) * 128], wv[wi]
                            else:
                                lhs = wv[wi][:, m * 128:(m + 1) * 128]
                                o, rhs = G[m][:, :], xv[xi]
                            s, e = k == 0 and wi + xi == 0, k == nk - 1 and wi == 1
                            inc = (kk == kn - 1 and wi == 1) and (k == nk - 1 or ti == tiles - 1)
                            tok = mm(o, lhs, rhs, s, e, split_done[n], x.ready[x.first + k],
                                     gfree[m] if s else None, inc=inc)
                            if e:
                                done[m] = tok
                    if ti in pumps:
                        pump()
                pe_done.append(tok)
            for k in range(nk):
                x.war[x.first + k] = [pe_done[-1]]
            return done

        turn = [0]

        def split_tile(i, t, tok, x, k):
            hi = act(x.hi[:, k, :], t, ACT.Copy, tok, x.war[k])
            lo = tt(pool, x.lo[:, k, :], t, x.hi[:, k, :].bitcast(F32), ALU.subtract, hi, x.war[k])
            x.ready[k] = [hi, lo]
            if i is not None:
                tmps.free[i] = [lo]

        XO, AO, BO = Operand(xh, xl), Operand(ah, al), Operand(bh, bl)
        PO = Operand(bh, bl, 4)

        A = a
        plan = {}

        def ffn_units(name, wg, wu, wd):
            for hf, (g0, g1) in enumerate(((0, 6), (6, 11))):
                for g in range(g0, g1):
                    c = g * 256

                    def pieces(k0, n, c=c):
                        return [(0, 128, 0, n, o, 256,
                                 w[k0 * 128:(k0 + n) * 128, c:c + 256].rearrange("(k p) c -> p k c", p=128))
                                for o, w in ((0, wg), (256, wu))]
                    plan[name, "gu", g] = add_units(pieces, KD, 512)
                for c in range(2):
                    plan[name, "dn", hf, c] = add_units(plain(wd, [(c * 512, c * 512 + 512)], g0 * 256),
                                                        2 * (g1 - g0), 512)

        def two(name, w, nk, c0=0):
            for c in range(2):
                plan[name, c] = add_units(plain(w, [(c0 + c * 512, c0 + c * 512 + 512)]), nk, 512)

        def inter(names):
            for c in range(2):
                for name, w, nk, c0 in names:
                    plan[name, c] = add_units(plain(w, [(c0 + c * 512, c0 + c * 512 + 512)]), nk, 512)

        ffn_units("ffn1", A["ffn1_w_gate"][0], A["ffn1_w_up"][0], A["ffn1_w_down"][0])
        win = A["w_in"][0]
        two("v", win, KD, D)
        two("u", win, KD, 0)
        two("c", win, KD, 2 * D)
        inter([("ga", win, KD, 3 * D), ("oa", A["w_out_a"][0], KD, 0)])
        inter([("gb", win, KD, 4 * D), ("ob", A["w_out_b"][0], KD, 0)])
        two("wo", A["w_o"][0], KD)
        ffn_units("ffn2", A["ffn2_w_gate"][0], A["ffn2_w_up"][0], A["ffn2_w_down"][0])
        inter([("pg", A["ple_w_gate"][0], KD, 0), ("pp", A["ple_w_proj"][0], 2, 0)])
        w2 = A["w_in_2"][0]

        def by_pair(c0, rest):
            def pieces(k0, n):
                got = []
                for k in range(n):
                    rows = w2[(k0 + k) * 128:(k0 + k + 1) * 128]
                    for g in range(2):
                        src = rows[:, c0 + 192 * g:c0 + 192 * g + 192].rearrange("p (r e) -> p r e", r=3)
                        got.append((0, 128, k, 1, None,
                                    lambda v, g=g: v[:, 0:384].rearrange("p (r g e) -> p r g e", r=3, g=2)[:, :, g], src))
                    if rest:
                        got.append((0, 128, k, 1, None, lambda v: v[:, 384:384 + rest],
                                    rows[:, c0 + 384:c0 + 384 + rest]))
                return got
            return pieces

        for name, parts in (("dq", [(2578, 2962)]), ("dk", [(2962, 3346)]), ("dv", [(3346, 3730)]),
                            ("qkc", [(1024, 1536)]), ("vcks", [(1536, 1792), (1920, 2048)]),
                            ("vg", [(1792, 1920), (2048, 2194)]), ("nz", [(2194, 2578)]), ("dz", [(3730, 4114)]),
                            ("bc", [(0, 512)]), ("hz", [(512, 1024)])):
            pieces = by_pair(parts[0][0], parts[0][1] - 384 - parts[0][0]) if name in ("qkc", "nz") else plain(w2, parts)
            plan[name] = add_units(pieces, KD, sum(c1 - c0 for c0, c1 in parts))
        wout2 = A["w_out_2"][0]

        def wout_pieces(c0):
            def rows(p0, p1, k, n, r0):
                src = wout2[r0:r0 + n * (p1 - p0), c0:c0 + 512].rearrange("(k p) c -> p k c", p=p1 - p0)
                return (p0, p1, k, n, 0, 512, src)

            def pieces(k0, n):
                if k0 == 2:
                    return [rows(64 * g, 64 * g + 64, 0, 2, 256 + 192 * g) for g in range(2)]
                if k0 == 4:
                    return [rows(64 * g, 64 * g + 64, 0, 1, 256 + 192 * g + 128) for g in range(2)] + \
                           [rows(0, 128, 1, 1, 640)]
                return [rows(0, 128, 0, 2, k0 * 128)]
            return pieces

        for c in range(2):
            plan["out2", c] = add_units(wout_pieces(c * 512), KD, 512)
        inter([("pg2", A["w_ple_gate_2"][0], KD, 0), ("pp2", A["w_ple_proj_2"][0], 2, 0)])

        xrow = f[:, :, :].rearrange("p k t -> p (k t)").rearrange("p (i c) -> p i c", i=4)
        x_tok = [load(sp, xrow[:, i, :], A["x"][0, i * 128:(i + 1) * 128, :]) for i in range(4)]
        grow = tmp_t[:, 3, 0:128]
        g_tok, r = [], 0
        colat = {}
        for name, n in COLS:
            src = A[name][0].rearrange("k (a c) -> (k a) c", c=128) if name == "conv_w_2" else \
                (A[name] if name == "norm_final_2" else A[name][0]).rearrange("(a c) -> a c", c=128)
            g_tok.append(load(sca, tmp_t[r:r + n, 3, 0:128], src))
            colat[name] = r
            r += n

        def col(name, m):
            return cols[:, colat[name] + m:colat[name] + m + 1]

        k1 = pool.put(lambda e: e.memset(ident[:, :], 0.0))
        k_id = pool.put(lambda e: e.affine_select(out=ident[:, :], in_=ident[:, :], compare_op=ALU.not_equal, fill=1.0,
                                                  base=0, pattern=[[-1, 128]], channel_multiplier=1), k1)
        k_idb = copy(pool, identb[:, :], ident[:, :], k_id)
        k_ones = pool.put(lambda e: e.memset(ones[:, :], 1.0))
        k_eps = pool.put(lambda e: e.memset(eps[:, :], EPS))
        for t in range(15):
            k_inv = pool.put(lambda e, t=t: e.memset(inv[:, t:t + 1], 1.0 / (t + 1)))
        zero = sq_t[:, 0, 0:128]
        k_z = pool.put(lambda e: e.memset(zero, 0.0))
        keep = dict(compare_op=ALU.is_ge, fill=NEG, base=0)
        k_mc = pool.put(lambda e: e.affine_select(out=mcaus[:, :], in_=zero, pattern=[[-1, 128]],
                                                  channel_multiplier=1, **keep), k_z)
        k_mb = pool.put(lambda e: e.affine_select(out=mband[:, 0, :], in_=zero, pattern=[[1, 128]],
                                                  channel_multiplier=-1, **keep), k_z)
        k_mb = copy(pool, mband[:, 1, :], mcaus[:, :], k_mc)
        zc = sq_t[:, 0, 0:124].rearrange("p (i n) -> p i n", i=4)
        k_cm = pool.put(lambda e: e.affine_select(out=mcmp[:, :, :], in_=zc, pattern=[[128, 4], [-16, 31]],
                                                  channel_multiplier=1, compare_op=ALU.is_ge, fill=NEG, base=-31), k_z)
        k_md = []
        for n, (d, md) in enumerate(((4, md4), (16, md16))):
            o = sq_t[0:d, 1, n * 128:n * 128 + 128].rearrange("p (a b) -> p a b", b=d)
            kz = pool.put(lambda e, o=o: e.memset(o, 0.0))
            ko = pool.put(lambda e, o=o, d=d: e.affine_select(out=o, in_=o, compare_op=ALU.not_equal, fill=1.0, base=0,
                                                              pattern=[[0, 128 // d], [1, d]],
                                                              channel_multiplier=-1), kz)
            oh = sq_t[0:d, 1, n * 128:n * 128 + 128]
            kp = mm(X[3][:, n * 128:n * 128 + 128], oh, oh, True, True, ko, inc=True)
            mt = sq_t[:, 0, 128 + n * 128:256 + n * 128]
            kd = ts(dve, mt, X[3][:, n * 128:n * 128 + 128], -1.0, -NEG, ALU.add, ALU.mult, kp)
            k0 = copy(pool, md[:, 0, :], mt, kd)
            k_md.append(pool.put(lambda e, md=md, mt=mt: e.affine_select(
                out=md[:, 1, :], in_=mt, pattern=[[-1, 128]], channel_multiplier=1, **keep), kd))
            xfree[3] = [kd]
        sqs.free = [[k_cm, k_md], [kp]]

        k_g = tr(X[2][:, 0:104], tmp_t[0:104, 3, 0:128], ident[0:104, 0:104], g_tok, k_id, inc=True)
        k_cols = copy(dve, cols[:, :], X[2][:, 0:104], k_g)
        xfree[2] = [k_cols]
        tmps.free[3] = [k_g]
        k_half = [ts(dve, half[:, 8 * n:8 * n + 8], cols[:, colat[w]:colat[w] + 8], 0.5, None, ALU.mult, None, k_cols)
                  for n, w in enumerate(("ffn1_post_g", "ffn2_post_g"))]

        h_tok = [None] * KD
        for k in range(KD):
            b = (0, 1)[k % 2]
            for i in range(4):
                t = tr(X[b][:, i * 128:(i + 1) * 128], xrow[:, i, k * 128:(k + 1) * 128], ident[:, :],
                       x_tok[i], k_id, xfree[b], inc=(i == 3))
            h_tok[k] = copy(dve, h[:, k, :], X[b][:, :], t)
            xfree[b] = [h_tok[k]]
        f_tok = [[t] for _ in range(KD)]

        rstd_free = [[]]

        def rstd_of(tiles, toks):
            n = len(tiles)
            for m in range(n):
                i, s, fr = sqs.take()
                k = act(s, tiles[m], ACT.Square, toks[m], fr)
                t = mm(X[0][:, :], ones[:, :], s, m == 0, m == n - 1, k, k_ones, xfree[0] if m == 0 else None, inc=True)
                sqs.free[i] = [t]
            i, s, fr = sqs.take()
            k = act(s, X[0][:, :], ACT.Sqrt, t, k_eps, fr, bias=eps[:, 0:1], scale=1.0 / D)
            xfree[0] = [k]
            k = rec(rstd[:, :], s, k, rstd_free[0])
            sqs.free[i] = [k]
            return k

        hs = [h[:, m, :] for m in range(KD)]
        fs = [f[:, m, :] for m in range(KD)]

        def pre_norm(name):
            k = rstd_of(hs, h_tok)
            for m in range(KD):
                i, t, fr = tmps.take()
                s = stt(t, hs[m], col(name, m), rstd[:, :], ALU.mult, ALU.mult, k, h_tok[m], k_cols, fr)
                split_tile(i, t, s, XO, m)
            rstd_free[0] = [s]

        def post_norm(gain, toks):
            k = rstd_of(fs, toks)
            for m in range(KD):
                s = stt(fs[m], fs[m], gain(m), rstd[:, :], ALU.mult, ALU.mult, k, toks[m], k_half)
                h_tok[m] = tt(pool, hs[m], hs[m], fs[m], ALU.add, s, h_tok[m])
                f_tok[m] = [h_tok[m]]
            rstd_free[0] = [s]

        def ffn(name, pre, post_n):
            pre_norm(pre)
            hid = lambda i: (AO, i) if i < 8 else (BO, i - 8)
            toks = [None] * KD
            for hf, (g0, g1) in enumerate(((0, 6), (6, 11))):
                for g in range(g0, g1):
                    done = gemm(plan[name, "gu", g], XO, 4, order=[0, 2, 1, 3])
                    for p in range(2):
                        si, s, fr = acts.take()
                        k = act(s, G[p][:, :], ACT.Silu, done[p], fr)
                        gfree[p] = [k]
                        i, t, fr = tmps.take()
                        k = tt(dve, t, G[2 + p][:, :], s, ALU.mult, k, done[2 + p], fr)
                        gfree[2 + p] = [k]
                        acts.free[si] = [k]
                        split_tile(i, t, k, *hid(2 * (g - g0) + p))
                nk = 2 * (g1 - g0)
                both = Both(AO, BO, nk)
                for c in range(2):
                    done = gemm(plan[name, "dn", hf, c], both, 4)
                    for m in range(4):
                        j = 4 * c + m
                        if hf == 0:
                            toks[j] = act(fs[j], G[m][:, :], ACT.Copy, done[m], f_tok[j])
                        else:
                            toks[j] = tt(dve, fs[j], G[m][:, :], fs[j], ALU.add, done[m], toks[j])
                        gfree[m] = [toks[j]]
                both.close()
            post_norm(lambda m: half[:, 8 * post_n + m:8 * post_n + m + 1], toks)

        class Both:

            def __init__(self, p, q, n):
                self.p, self.q, self.n, self.first = p, q, n, 0
                self.ready = p.ready + q.ready
                self.war = [None] * 16
                self.hi, self.lo = Pair(p.hi, q.hi), Pair(p.lo, q.lo)

            def close(self):
                for k in range(self.n):
                    (self.p if k < 8 else self.q).war[k % 8] = self.war[k]

        class Pair:
            def __init__(self, p, q):
                self.p, self.q = p, q

            def __getitem__(self, at):
                return self.p[at] if at[1] < 8 else self.q[:, at[1] - 8, :]

        ffn("ffn1", "ffn1_pre_g", 0)

        ws_t = [load(pool, tmp_t[:, 2, 0:512].rearrange("p (g s) -> p g s", g=4),
                     A["sgu_w"][0].rearrange("g t s -> t g s"), tmps.free[2])]
        w_ws = tmp_t[:, 2, 0:512].rearrange("p (g s) -> p g s", g=4)
        sgb_t = load(pool, sgub[:, :, :].rearrange("p g t -> p (g t)"),
                     A["sgu_b"][0:1].rearrange("a g t -> a (g t)").to_broadcast([128, 512])
                     if False else A["sgu_b"].rearrange("a g t -> a (g t)").partition_broadcast(128))
        pw_t = load(pool, poolw[:, :, :, :], A["pool_w"][0].rearrange("g (k p) d -> p g k d", p=128))
        for g in range(4):
            k_ws = pool.put(lambda e, g=g: e.affine_select(out=w_ws[:, g, :], in_=w_ws[:, g, :], pattern=[[-1, 128]],
                                                           channel_multiplier=1, compare_op=ALU.is_ge, fill=0.0,
                                                           base=0), ws_t)
        for g in range(4):
            t = tr(X[1][:, g * 128:(g + 1) * 128], w_ws[:, g, :], ident[:, :], k_ws, xfree[1], inc=(g == 3))
        k_wst = copy(dve, wst[:, :, :].rearrange("p g s -> p (g s)"), X[1][:, :], t)
        xfree[1] = [k_wst]
        tmps.free[2] = [t]

        pre_norm("mix_pre_g")

        k_ln = [None] * 4
        v_tok = [[None, None] for _ in range(4)]
        for c in range(2):
            done = gemm(plan["v", c], XO, 4, by_token=True)
            for i in range(4):
                v = vtok[:, i, c * 512:(c + 1) * 512]
                v_tok[i][c] = act(v, G[i][:, :], ACT.Gelu_apprx_tanh, done[i], f_tok)
                gfree[i] = [v_tok[i][c]]
                k_bn = dve.put(lambda e, i=i, c=c, v=v: e.bn_stats(bnst[:, i, c, :], v), v_tok[i][c])
        for i in range(4):
            k_ag = dve.put(lambda e, i=i: e.bn_aggr(mv[:, i, :], bnst[:, i, :, :]), k_bn)
        k = act(lnr[:, :], mv[:, :, 1], ACT.Sqrt, k_ag, k_eps, bias=eps[:, 0:1])
        k_lr = rec(lnr[:, :], lnr[:, :], k)
        for i in range(4):
            k_ln[i] = ts(dve, vtok[:, i, :], vtok[:, i, :], mv[:, i, 0:1], lnr[:, i:i + 1], ALU.subtract, ALU.mult,
                         k_lr, v_tok[i])

        for c in range(2):
            done = gemm(plan["u", c], XO, 4)
            for m in range(4):
                j = 4 * c + m
                si, u, fr = acts.take()
                k_u = act(u, G[m][:, :], ACT.Gelu_apprx_tanh, done[m], fr)
                gfree[m] = [k_u]
                b = j % 2
                for i in range(4):
                    t = mm(X[b][:, i * 128:(i + 1) * 128], vtok[:, i, j * 128:(j + 1) * 128], wst[:, j // 2, :],
                           True, True, k_ln, k_wst, xfree[b], inc=(i == 3))
                ti, s, fr = tmps.take()
                bb = sgub[:, j // 2, :].unsqueeze(1).to_broadcast([128, 4, 128])
                k = stt(s.rearrange("p (i t) -> p i t", i=4), X[b][:, :].rearrange("p (i t) -> p i t", i=4),
                        col("sgu_norm_g", j), bb, ALU.mult, ALU.add, t, sgb_t, fr)
                xfree[b] = [k]
                k = tt(pool, s, s, u, ALU.mult, k, k_u)
                acts.free[si] = [k]
                split_tile(ti, s, k, AO, j)
        k_sgu = t

        k_pad = pool.put(lambda e: e.memset(cpad[:, :, 0:16], 0.0), k_sgu)
        k_c = [[k_pad], [k_pad]]
        diff = []
        k_csum = [None, None]
        for c in range(2):
            done = gemm(plan["c", c], XO, 4)
            for m in range(4):
                j = 4 * c + m
                gi, b = j // 2, j % 2
                w = 2 << gi
                cur = cpad[:, b, :]
                k0 = act(cpad[:, b, 16:528], G[m][:, :], ACT.Copy, done[m], k_c[b], k_sgu)
                gfree[m] = [k0]
                lo, src, k = 0, cur, [k0, k_csum]
                for n in range(gi + 1):
                    dst, sh = csum[:, n % 2, :], 1 << n
                    lo += sh
                    k = [tt(pool, dst[:, lo:528], src[:, lo:528], src[:, lo - sh:528 - sh], ALU.add, k)]
                    src = dst
                ti, t, fr = tmps.take()
                k2 = stt(t, src[:, 16:528], 1.0 / w, cpad[:, b, 16:528], ALU.mult, ALU.subtract, k, fr)
                k3 = tt(dve, src[:, 16:15 + w], src[:, 16:15 + w], inv[:, 0:w - 1], ALU.mult, k2, k_inv)
                k4 = tt(dve, t[:, 0:w - 1], src[:, 16:15 + w], cpad[:, b, 16:15 + w], ALU.subtract, k3)
                k_csum = [k4, k4]
                k_c[b] = [k4]
                diff.append((ti, t, k4))
                if b == 1:
                    for dt_ in range(2):
                        xb = 2 + dt_
                        for kk in range(2):
                            t = mm(X[xb][:, :], poolw[:, gi, kk, dt_ * 128:dt_ * 128 + 128], diff[kk][1], kk == 0,
                                   kk == 1, diff[kk][2], pw_t, xfree[xb], inc=(kk == 1))
                        if dt_ == 1:
                            for kk in range(2):
                                tmps.free[diff[kk][0]] = [t]
                        di = gi * 2 + dt_
                        ti, s, fr = tmps.take()
                        k = act(s, X[xb][:, :], ACT.Copy, t, fr, scale=col("pool_scale", di))
                        xfree[xb] = [k]
                        split_tile(ti, s, k, BO, di)
                    diff = []
        k_cend = [k_c, k_csum]

        y_tok = [None] * KD

        def gated(gname, oname, x, use, func=ACT.Sigmoid):
            for c in range(2):
                done = gemm(plan[gname, c], XO, 4)
                sg = []
                for m in range(4):
                    si, s, fr = acts.take()
                    k = act(s, G[m][:, :], func, done[m], fr)
                    gfree[m] = [k]
                    sg.append((si, s, k))
                done = gemm(plan[oname, c], x, 4)
                for m in range(4):
                    si, s, k = sg[m]
                    k = use(4 * c + m, G[m][:, :], s, [k, done[m]])
                    gfree[m] = [k]
                    acts.free[si] = [k]

        def use_a(j, ps, s, toks):
            y_tok[j] = tt(dve, fs[j], ps, s, ALU.mult, toks, k_cend, k_sgu)
            return y_tok[j]

        def use_b(j, ps, s, toks):
            ti, t, fr = tmps.take()
            k0 = tt(dve, t, ps, s, ALU.mult, toks, fr)
            k = tt(pool, t, t, fs[j], ALU.add, k0, y_tok[j])
            f_tok[j] = [k]
            split_tile(ti, t, k, AO, j)
            return k0

        gated("ga", "oa", AO, use_a)
        gated("gb", "ob", BO, use_b)
        toks = [None] * KD
        for c in range(2):
            done = gemm(plan["wo", c], AO, 4)
            for m in range(4):
                j = 4 * c + m
                toks[j] = act(fs[j], G[m][:, :], ACT.Copy, done[m], f_tok)
                gfree[m] = [toks[j]]
        post_norm(lambda m: col("mix_post_g", m), toks)

        def embed(src, *after):
            k_p = load(pool, prow[:, :, :], src.rearrange("(i p) c -> p i c", p=128), *after)
            for k in range(2):
                for i in range(4):
                    t = tr(X[3][:, i * 128:(i + 1) * 128], prow[:, i, k * 128:(k + 1) * 128], ident[:, :],
                           k_p, xfree[3], inc=(i == 3))
                ti, s, fr = tmps.take()
                kc = copy(dve, s, X[3][:, :], t, fr)
                xfree[3] = [kc]
                PO.war[4 + k] = now(BO.war, *after)
                split_tile(ti, s, kc, PO, 4 + k)
            return t

        k_e = embed(A["p"][0, 0], now(BO.war))
        BO.war[6] = BO.war[7] = [k_e]
        ffn("ffn2", "ffn2_pre_g", 1)

        pre_norm("ple_pre_g")
        toks = [None] * KD

        def use_p(j, ps, s, tk):
            toks[j] = tt(dve, fs[j], ps, s, ALU.mult, tk, f_tok)
            return toks[j]

        gated("pg", "pp", PO, use_p)
        post_norm(lambda m: col("ple_post_g", m), toks)

        k_b2 = now(PO.war, BO.war, AO.war)
        pre_norm("norm_mix_2")

        def store(done, dst, *after, tiles=None, scale=None, fn=ACT.Copy, wid=T):
            got = []
            for m, d in enumerate(dst):
                kw = {} if scale is None or scale[m] is None else {"scale": scale[m]}
                got.append(act(d, G[m][:, 0:wid], fn, done[m], *after, **kw))
                gfree[m] = [got[-1]]
            return got

        k_dq = store(gemm(plan["dq"], XO, 3), [dq[:, m, :] for m in range(3)], k_b2, scale=[0.125] * 3)
        k_dk = store(gemm(plan["dk"], XO, 3), [dk[:, m, :] for m in range(3)], k_b2)
        k_dv = store(gemm(plan["dv"], XO, 4, by_token=True), [dv[:, i, :] for i in range(4)], k_b2, wid=384)

        ptrs = Ring([ptr[:, i, :] for i in range(4)])
        prbs = Ring([prb[:, i, :] for i in range(3)])
        for r_ in (ptrs, prbs):
            r_.free = [now(f_tok) for _ in r_.aps]
        n_stat = [0]
        k_stat = [pool.put(lambda e: e.memset(stat[:, :], 0.0), f_tok)]

        def stats(n):
            o = n_stat[0]
            n_stat[0] += n
            assert o + n <= 256
            return stat[:, o:o + n]

        def qk(bank, q, k, k0, i, masks, nm, den, *after):
            n = (i + 1) * 128 - k0
            qt = q[:, i * 128:(i + 1) * 128]
            mm(X[bank][:, 0:n], qt, k[:, k0:k0 + n], True, False, xfree[bank], *after)
            for mi, (o, mw, m) in enumerate(masks):
                t = mm(X[bank][:, o:o + mw], identb[:, :], m, False, mi == len(masks) - 1,
                       k_idb, k_mc, k_mb, k_md, inc=(mi == len(masks) - 1))
            k1 = red(nm, X[bank][:, 0:n], ALU.max, t, k_stat, negate=True)
            pi, p, fr = prbs.take()
            k2 = act(p[:, 0:n], X[bank][:, 0:n], ACT.Exp, k1, fr, bias=nm, accum_out=den)
            xfree[bank] = [k2]
            return pi, p[:, 0:n], n // 128, k2

        def turn_p(pi, p, nb, k, q):
            for b in range(nb):
                t = tr(X[2][:, b * 128:(b + 1) * 128], p[:, b * 128:(b + 1) * 128], ident[:, :], k, xfree[2],
                       inc=(b == nb - 1))
            prbs.free[pi] = [t]
            ti, o, fr = ptrs.take()
            kc = copy(q, o[:, 0:nb * 128], X[2][:, 0:nb * 128], t, fr)
            xfree[2] = [kc]
            return ti, o, kc

        k_od = [None] * 4

        def dilated():
            steps = [(i, j) for i in range(4) for j in range(2)]
            state = {}

            def scores(s, gi):
                i, j = steps[s]
                if gi == 0:
                    state[s] = {"nm": stats(3), "den": stats(3), "w": stats(3), "dw": stats(3), "s": stats(2), "p": []}
                st = state[s]
                q, k = (v[64 * j:64 * j + 64, gi, :] for v in (dq, dk))
                if gi == 0:
                    k0 = 128 * max(i - 1, 0)
                    masks = [(0, 256, mband[:, :, :].rearrange("p a c -> p (a c)"))] if i else [(0, 128, mband[:, 1, :])]
                else:
                    k0 = 0
                    md = md4 if gi == 1 else md16
                    masks = [(128 * b, 128, md[:, 0, :]) for b in range(i)] + [(128 * i, 128, md[:, 1, :])]
                st["p"].append(qk(gi % 2, q, k, k0, i, masks, st["nm"][:, gi:gi + 1], st["den"][:, gi:gi + 1],
                                  k_dq, k_dk))

            for gi in range(3):
                scores(0, gi)
            yield
            for s, (i, j) in enumerate(steps):
                st = state[s]
                k = st["p"][2][3]
                nM, r_ = st["s"][:, 0:1], st["s"][:, 1:2]
                k = red(nM, st["nm"], ALU.min, k)
                k = act(st["w"], st["nm"], ACT.Exp, k, bias=nM, scale=-1.0)
                k = tt(dve, st["dw"], st["den"], st["w"], ALU.mult, k)
                k = red(r_, st["dw"], ALU.add, k)
                k = rec(r_, r_, k)
                k = ts(dve, st["w"], st["w"], r_, None, ALU.mult, None, k)
                kp = [ts(dve, st["p"][gi][1], st["p"][gi][1], st["w"][:, gi:gi + 1], None, ALU.mult, None, k,
                         st["p"][gi][3]) for gi in range(3)]

                def weigh(gi, ti, o, kc):
                    nb = st["p"][gi][2]
                    for b in range(nb):
                        kt = i + 1 - nb + b
                        t = mm(X[3][64 * j:64 * j + 64, gi * 128:gi * 128 + 128],
                               dv[:, kt, 128 * gi + 64 * j:128 * gi + 64 * j + 64], o[:, b * 128:(b + 1) * 128],
                               b == 0, b == nb - 1, kc, k_dv, xfree[3] if j == 0 else None, inc=(b == nb - 1))
                    ptrs.free[ti] = [t]
                    return t

                last = None
                for gi in range(3):
                    pi, p, nb, _ = st["p"][gi]
                    now = turn_p(pi, p, nb, kp[gi], dve if gi == 1 else sca)
                    if s + 1 < len(steps):
                        scores(s + 1, gi)
                    if last:
                        weigh(*last)
                    last = (gi, *now)
                    yield
                t = weigh(*last)
                if j == 1:
                    k_od[i] = copy(sca, odil[:, :, i * 128:(i + 1) * 128],
                                   X[3][:, 0:384].rearrange("p (g t) -> p g t", g=3), t, k_b2)
                    xfree[3] = [k_od[i]]
                state.pop(s)

        background.append(dilated())

        k_q = store(gemm(plan["qkc"], XO, 4, pumps=(1, 3)),
                    [qn[:, m, :] for m in range(3)] + [kvn[:, 0, :]], k_b2, scale=[0.125] * 3 + [None])
        k_kv = [k_q[3]] + store(gemm(plan["vcks"], XO, 3, pumps=(0, 2)), [kvn[:, 1 + m, :] for m in range(3)], k_b2)
        done = gemm(plan["vg"], XO, 4, by_token=True, pumps=(1, 3))
        k_v, k_gt = [], []
        for i in range(4):
            k_v.append(act(vnt[:, i, :], G[i][:, 0:256], ACT.Copy, done[i]))
            k_gt.append(copy(dve, gates[:, i, :], G[i][:, 256:274], k_v[i]))
            gfree[i] = [k_v[i], k_gt[i]]
        drain_background()
        k_gt = act(gates[:, :, :], gates[:, :, :], ACT.Sigmoid, k_gt)
        k_dil = now(prbs.free, ptrs.free)

        k_w1 = [load(pool, w1s[64 * g:64 * g + 64, kv, :, :], A["cmp_w1_2"][0, kv].rearrange("(l e) o -> e l o", e=64),
                     k_dil) for kv in range(2) for g in range(2)]
        k_w2 = [load(pool, w2s[64 * g:64 * g + 64, :, :], A["cmp_w2_2"][0].rearrange("v e o -> e v o"), k_b2)
                for g in range(2)]
        k_pe = [load(pool, perow[:, :, g, :], A["cmp_pe_2"][0].rearrange("v l e -> l v e"), k_b2) for g in range(2)]
        k_pc = [None]

        def compress():
            for kv in range(2):
                t = tr(X[2][:, kv * 32:kv * 32 + 32], perow[:, kv, :, :].rearrange("l g e -> l (g e)"),
                       ident[0:32, 0:32], k_pe, xfree[2], inc=True)
            k = copy(dve, pes[:, :, :].rearrange("p v l -> p (v l)"), X[2][:, 0:64], t, k_b2)
            xfree[2] = [k]
            t2 = None
            for kv in range(2):
                src = kvn[:, kv, :]
                win_ = bass.AP(tensor=src.tensor, offset=src.offset, ap=[list(src.ap[0]), [16, 31], [1, 32]])
                kb = tt(dve, blk[:, :, :], win_, pes[:, kv, :].unsqueeze(1).to_broadcast([128, 31, 32]), ALU.add,
                        k, k_kv[kv], t2)
                for l in range(32):
                    for g in range(2):
                        sl = slice(64 * g, 64 * g + 64)
                        t = mm(X[0][sl, 0:31], w1s[sl, kv, l, :], blk[sl, :, l], l == 0, l == 31, kb, k_w1, xfree[0],
                               inc=(l == 31 and g == 1))
                    if l == 15:
                        yield
                t2 = t
                kh = act(hcs[:, 0:31], X[0][:, 0:31], ACT.Silu, t, k_pc[0])
                xfree[0] = [kh]
                for g in range(2):
                    sl = slice(64 * g, 64 * g + 64)
                    if kv == 0:
                        t = mm(X[1][sl, 0:31], w2s[sl, kv, :], hcs[sl, 0:31], True, True, kh, k_w2, xfree[1],
                               inc=True)
                    else:
                        t = mm(X[1][0:31, 64 * g:64 * g + 64], hcs[sl, 0:31], w2s[sl, kv, :], True, True, kh, k_w2,
                               xfree[1], t, inc=True)
                    if g == 1 and kv == 0:
                        k_pc[0] = copy(dve, kcs[:, 0:31], X[1][:, 0:31], t)
                        xfree[1] = [k_pc[0]]
                if kv == 1:
                    k_vc = copy(dve, vcs[:, :], X[1][0:31, 0:128], t)
                    xfree[1] = [k_vc]
                yield
            k_s = []
            for g in range(2):
                v = X[g][:, 0:384].rearrange("p (a n) -> p a n", n=32)
                sl = slice(64 * g, 64 * g + 64)
                for i in range(4):
                    for r_ in range(3):
                        t = mm(v[:, i * 3 + r_, 0:31], qn[sl, r_, i * 128:(i + 1) * 128], kcs[sl, 0:31], True, True,
                               k_q, k_pc[0], xfree[g], inc=(i == 3 and r_ == 2))
                for i in range(4):
                    k = tt(dve, pcmp[:, i * 6 + g * 3:i * 6 + g * 3 + 3, 0:31], v[:, i * 3:i * 3 + 3, 0:31],
                           mcmp[:, i, :].unsqueeze(1).to_broadcast([128, 3, 31]), ALU.add, t, t2, k_cm)
                    k_s.append(k)
                xfree[g] = [k]
            pc = pcmp[:, :, 0:31]
            mx, dn = pcs[:, 0, :], pcs[:, 1, :]
            bc = lambda v: v.unsqueeze(2).to_broadcast([128, 24, 31])
            k = red(mx, pc, ALU.max, k_s)
            k = ts(dve, mx, mx, -1.0e20, None, ALU.max, None, k)
            k = tt(dve, pc, pc, bc(mx), ALU.subtract, k)
            k = act(pc, pc, ACT.Exp, k)
            k = red(dn, pc, ALU.add, k)
            k = ts(dve, dn, dn, 1e-30, None, ALU.max, None, k)
            k = rec(dn, dn, k)
            gc = gates[:, :, :].rearrange("p i (n b) -> p (i n) b", b=3)[:, :, 0]
            k = tt(dve, dn, dn, gc, ALU.mult, k, k_gt)
            k_pc[0] = [tt(dve, pc, pc, bc(dn), ALU.mult, k), k_vc]
            yield

        def sparse():
            steps = [(r_, i, g) for r_ in range(3) for i in range(4) for g in range(2)]
            state = {}
            pct_free = [now(sqs.free), now(sqs.free)]
            pct_tok = [None, None]

            def scores(s, b):
                r_, i, g = steps[s]
                if b == 0:
                    state[s] = {"nm": stats(2), "den": stats(2), "p": []}
                st = state[s]
                sl = slice(64 * g, 64 * g + 64)
                st["p"].append(qk(b, qn[sl, r_, :], kvn[sl, 2 + b, :], 0, i, [(128 * i, 128, mcaus[:, :])],
                                  st["nm"][:, b:b + 1], st["den"][:, b:b + 1], k_q, k_kv))

            n_stat[0] = 0
            k_stat[0] = pool.put(lambda e: e.memset(stat[:, :], 0.0), k_pc[0])
            for b in range(2):
                scores(0, b)
            yield
            for s, (r_, i, g) in enumerate(steps):
                st = state[s]
                if i == 0:
                    for ii in range(4):
                        t = tr(X[2][0:31, ii * 128:(ii + 1) * 128], pcmp[:, ii * 6 + g * 3 + r_, 0:31], ident[:, :],
                               k_pc[0], xfree[2], inc=(ii == 3))
                    pct_tok[g] = copy(sca, sq_t[0:31, g, :], X[2][0:31, :], t, pct_free[g])
                    xfree[2] = [pct_tok[g]]
                k = [p[3] for p in st["p"]]
                k = rec(st["den"], st["den"], k)
                kp = []
                for b in range(2):
                    gc = gates[:, i, (g * 3 + r_) * 3 + 1 + b:(g * 3 + r_) * 3 + 2 + b]
                    kp.append(ts(dve, st["p"][b][1], st["p"][b][1], st["den"][:, b:b + 1], gc, ALU.mult, ALU.mult, k,
                                 k_gt))
                o = X[3][64 * g:64 * g + 64, i * 128:(i + 1) * 128]
                sl = slice(64 * g, 64 * g + 64)
                t0 = turn_p(*st["p"][0][:3], kp[0], sca)
                if s + 1 < len(steps):
                    scores(s + 1, 0)
                t = mm(o, vcs[:, sl], sq_t[0:31, g, i * 128:(i + 1) * 128], True, False, k_pc[0], pct_tok[g],
                       xfree[3] if i == 0 else None, inc=True)
                if i == 3:
                    pct_free[g] = [t]
                t1 = turn_p(*st["p"][1][:3], kp[1], dve)
                for b in range(i + 1):
                    t = mm(o, vnt[:, b, sl], t0[1][:, b * 128:(b + 1) * 128], False, False, t0[2], k_v, inc=(b == i))
                ptrs.free[t0[0]] = [t]
                yield
                if s + 1 < len(steps):
                    scores(s + 1, 1)
                for b in range(i + 1):
                    t = mm(o, vnt[:, b, 128 + 64 * g:192 + 64 * g], t1[1][:, b * 128:(b + 1) * 128], False, b == i,
                           t1[2], inc=(b == i))
                ptrs.free[t1[0]] = [t]
                if i == 3 and g == 1:
                    ti, y, fr = tmps.take()
                    k = tt(dve, y, X[3][:, :], nz[:, r_, :], ALU.mult, t, k_nz, fr)
                    xfree[3] = [k]
                    split_tile(ti, y, k, AO, 2 + r_)
                state.pop(s)
                yield
            sqs.free = [pct_free[0], pct_free[1]]

        ptrs.free = [now(k_w1, k_dil) for _ in range(4)]
        prbs.free = [now(k_w1, k_dil) for _ in range(3)]
        for k in range(KD):
            AO.war[k] = now(k_od, k_b2, k_pe)

        def nsa():
            yield from compress()
            for r_ in (ptrs, prbs):
                for n in range(len(r_.aps)):
                    r_.free[n] = now(r_.free[n], k_pc[0])
            for k in range(KD):
                AO.war[k] = now(AO.war[k], k_pc[0])
            yield from sparse()

        done = gemm(plan["nz"], XO, 3)
        k_nz = store(done, [nz[:, m, :] for m in range(3)], k_b2, fn=ACT.Silu)
        background.append(nsa())
        pump()
        done = gemm(plan["dz"], XO, 3, pumps=(0, 1, 2))
        for m in range(3):
            si, s, fr = acts.take()
            k = act(s, G[m][:, :], ACT.Silu, done[m], fr)
            gfree[m] = [k]
            ti, t, fr = tmps.take()
            k = tt(pool, t, s, odil[:, m, :], ALU.mult, k, k_od, fr)
            acts.free[si] = [k]
            split_tile(ti, t, k, AO, 5 + m)
        done = gemm(plan["bc"], XO, 4, pumps=(0, 1, 2, 3))
        k_bc = store(done, [cab[:, 0, :], cab[:, 1, :], cac[:, 0, :], cac[:, 1, :]], k_dil, k_od)
        done = gemm(plan["hz"], XO, 4, order=[0, 2, 1, 3], pumps=(0, 1, 2, 3))
        for m in range(2):
            u, cv = cac[:, m, :], ccv[:, m, :]
            w = lambda n: cols[:, colat["conv_w_2"] + 2 * n + m:colat["conv_w_2"] + 2 * n + m + 1]
            k0 = tt(dve, u, G[m][:, :], u, ALU.mult, k_bc, done[m])
            gfree[m] = [k0]
            k = ts(dve, cv, u, w(2), col("conv_b_2", m), ALU.mult, ALU.add, k0, k_dil, k_od)
            k = stt(cv[:, 1:], u[:, :T - 1], w(1), cv[:, 1:], ALU.mult, ALU.add, k)
            k = stt(cv[:, 2:], u[:, :T - 2], w(0), cv[:, 2:], ALU.mult, ALU.add, k)
            k = tt(pool, cv, cv, cab[:, m, :], ALU.mult, k)
            si, s, fr = acts.take()
            kz = act(s, G[2 + m][:, :], ACT.Silu, done[2 + m], fr)
            gfree[2 + m] = [kz]
            ti, t, fr = tmps.take()
            k = tt(pool, t, cv, s, ALU.mult, k, kz, fr)
            acts.free[si] = [k]
            split_tile(ti, t, k, AO, m)
        drain_background()

        k_e = embed(A["p_2"][0, 0], now(k_pc[0], AO.ready, k_bc, k))

        for c in range(2):
            done = gemm(plan["out2", c], AO, 4)
            for m in range(4):
                j = 4 * c + m
                h_tok[j] = tt(dve, hs[j], G[m][:, :], hs[j], ALU.add, done[m], h_tok[j])
                gfree[m] = [h_tok[j]]
                split_tile(None, hs[j], h_tok[j], XO, j)

        def use_p2(j, ps, s, tk):
            ti, t, fr = tmps.take()
            k0 = tt(dve, t, ps, s, ALU.mult, tk, fr)
            h_tok[j] = tt(pool, hs[j], hs[j], t, ALU.add, k0, h_tok[j], XO.ready[j])
            tmps.free[ti] = [h_tok[j]]
            return k0

        gated("pg2", "pp2", PO, use_p2)
        k = rstd_of(hs, h_tok)
        orow = vtok
        k_o = []
        for m in range(KD):
            ti, t, fr = tmps.take()
            s = stt(t, hs[m], col("norm_final_2", m), rstd[:, :], ALU.mult, ALU.mult, k, h_tok[m], fr)
            b = m % 4
            for i in range(4):
                q = tr(X[b][:, i * 128:(i + 1) * 128], t[:, i * 128:(i + 1) * 128], ident[:, :], s, xfree[b],
                       inc=(i == 3))
            tmps.free[ti] = [q]
            kc = copy(sca, orow[:, :, m * 128:(m + 1) * 128], X[b][:, :].rearrange("p (i c) -> p i c", i=4), q,
                      f_tok, ptrs.free, prbs.free)
            xfree[b] = [kc]
            sp.put(lambda e, m=m: e.dma_start(out[0].rearrange("(i p) c -> p i c", p=128)[:, :, m * 128:(m + 1) * 128],
                                              orow[:, :, m * 128:(m + 1) * 128]).then_inc(s_out, 16), kc, inc=False)

        block = ctx.enter_context(nc.Block())

        @block.sync
        def _(e):
            sp.run(e)
            e.wait_ge(s_out, 16 * KD)

        @block.gpsimd
        def _(e):
            pool.run(e)

        @block.vector
        def _(e):
            dve.run(e)

        @block.scalar
        def _(e):
            sca.run(e)

        @block.tensor
        def _(e):
            pe.run(e)


_INS = ["x", "p", "ffn1_pre_g", "ffn1_w_gate", "ffn1_w_up", "ffn1_w_down", "ffn1_post_g", "mix_pre_g", "w_in",
        "sgu_norm_g", "sgu_w", "sgu_b", "pool_w", "pool_scale", "w_out_a", "w_out_b", "w_o", "mix_post_g", "ffn2_pre_g",
        "ffn2_w_gate", "ffn2_w_up", "ffn2_w_down", "ffn2_post_g", "ple_pre_g", "ple_w_gate", "ple_w_proj",
        "ple_post_g", "p_2", "norm_mix_2", "w_in_2", "conv_w_2", "conv_b_2", "cmp_pe_2", "cmp_w1_2", "cmp_w2_2",
        "w_out_2", "w_ple_gate_2", "w_ple_proj_2", "norm_final_2"]
_OUTS = [((1, 512, 1024), "float32")]


def kernel(**inputs):
    import numpy as _np
    import concourse.bacc as _bacc
    from concourse import mybir as _mybir
    from concourse.bass_utils import run_bass_kernel_spmd as _run

    nc = _bacc.Bacc("TRN2", target_bir_lowering=False, num_devices=1)
    arrays, args = {}, {}
    for name in _INS:
        v = _np.ascontiguousarray(inputs[name])
        arrays[f"in_{name}_dram"] = v
        args[name] = nc.dram_tensor(f"in_{name}_dram", v.shape, _mybir.dt.from_np(v.dtype), kind="ExternalInput").ap()
    outs = []
    for i, (shape, dtype) in enumerate(_OUTS):
        dt = _mybir.dt.from_np(_np.dtype(dtype))
        outs.append(nc.dram_tensor(f"out_{i}_dram", shape, dt, kind="ExternalOutput").ap())
    two_blocks(nc, args, outs[0])
    r = _run(nc, [arrays], core_ids=[0])
    return r.results[0]["out_0_dram"]
```

```python
from contextlib import ExitStack

import concourse.bass as bass
from concourse import mybir

F32 = mybir.dt.float32
F32R = mybir.dt.float32r
BF16 = mybir.dt.bfloat16
ALU = mybir.AluOpType
ACT = mybir.ActivationFunctionType
AX = mybir.AxisListType.X

T = 512
D = 1024
FF = 2816
KD = D // 128
NEG = -1.0e30
EPS = 1e-6
NRAW = 3
NSPLIT = 3
AHEAD = 2

COLS = [("ffn1_pre_g", 8), ("ffn1_post_g", 8), ("mix_pre_g", 8), ("sgu_norm_g", 8), ("pool_scale", 8),
        ("mix_post_g", 8), ("ffn2_pre_g", 8), ("ffn2_post_g", 8), ("ple_pre_g", 8), ("ple_post_g", 8),
        ("norm_mix_2", 8), ("norm_final_2", 8), ("conv_w_2", 6), ("conv_b_2", 2)]


class Queue:

    def __init__(self, sem):
        self.sem, self.count, self.items, self.met = sem, 0, [], {}

    def put(self, make, *after, inc=True):
        waits = []
        for tok in flat(after):
            key = tok[0].name
            if self.met.get(key, 0) < tok[1]:
                self.met[key] = tok[1]
                waits.append(tok)
        self.items.append((waits, make, self.sem if inc else None))
        if inc:
            self.count += 1
            return (self.sem, self.count)
        return None

    def run(self, eng):
        for waits, make, sem in self.items:
            for s, v in waits:
                eng.wait_ge(s, v)
            ins = make(eng)
            if sem is not None:
                ins.then_inc(sem, 1)


def flat(toks):
    for t in toks:
        if t is None:
            continue
        if isinstance(t, list):
            yield from flat(t)
        else:
            yield t


def now(*toks):
    last = {}
    for s, v in flat(toks):
        if s.name not in last or last[s.name][1] < v:
            last[s.name] = (s, v)
    return list(last.values())


class Ring:

    def __init__(self, aps):
        self.aps, self.free, self.at = aps, [[] for _ in aps], 0

    def take(self):
        i = self.at % len(self.aps)
        self.at += 1
        return i, self.aps[i], self.free[i]


class Operand:

    def __init__(self, hi, lo, first=0):
        self.hi, self.lo, self.first = hi, lo, first
        n = hi.shape[1]
        self.ready = [[] for _ in range(n)]
        self.war = [[] for _ in range(n)]


def two_blocks(nc, a, out):
    ctx = ExitStack()
    with ctx:
        def sem(name):
            return ctx.enter_context(nc.semaphore(name))

        base, top = 16512, 229344
        place = {"at": base}

        def at(name, shape, dt, offset):
            return nc.alloc_sbuf_tensor_at(name, shape, dt, offset=offset)

        def sb(name, shape, dt):
            n = 1
            for s in shape[1:]:
                n *= s
            n *= 2 if dt == BF16 else 4
            o = place["at"]
            place["at"] = o + (n + 31) // 32 * 32
            assert place["at"] <= top, (name, place["at"] - top)
            return at(name, shape, dt, o), o

        h, _ = sb("h", [128, KD, T], F32)
        xh, _ = sb("xh", [128, KD, T], F32R)
        xl, _ = sb("xl", [128, KD, T], F32R)
        ah, ah_o = sb("ah", [128, KD, T], F32R)
        al, al_o = sb("al", [128, KD, T], F32R)
        bh, bh_o = sb("bh", [128, KD, T], F32R)
        bl, bl_o = sb("bl", [128, KD, T], F32R)
        f, f_o = sb("f", [128, KD, T], F32)
        raw, _ = sb("raw", [128, NRAW, 1024], F32)
        whi, _ = sb("whi", [128, NSPLIT, 1024], F32R)
        wlo, _ = sb("wlo", [128, NSPLIT, 1024], F32R)
        act_t, _ = sb("act_t", [128, 4, T], F32)
        tmp_t, _ = sb("tmp_t", [128, 4, T], F32)
        sq_t, _ = sb("sq_t", [128, 2, T], F32)
        rpre, _ = sb("rpre", [128, T], F32)
        rtok, _ = sb("rtok", [128, 4], F32)
        m_o = place["at"]
        place["at"] += 12 * 1024
        vnt, _ = sb("vnt", [128, 4, 256], F32)
        ident, _ = sb("ident", [128, 128], F32)
        identb, _ = sb("identb", [128, 128], BF16)
        ones, _ = sb("ones", [128, 128], F32)
        cols, _ = sb("cols", [128, 104], F32)
        half, _ = sb("half", [128, 16], F32)
        mcaus, _ = sb("mcaus", [128, 128], BF16)
        mband, _ = sb("mband", [128, 2, 128], BF16)
        md4, _ = sb("md4", [128, 2, 128], BF16)
        md16, _ = sb("md16", [128, 2, 128], BF16)
        mcmp, _ = sb("mcmp", [128, 4, 31], F32)
        eps, _ = sb("eps", [128, 1], F32)
        inv, _ = sb("inv", [128, 16], F32)
        gates, _ = sb("gates", [128, 4, 18], F32)
        mv, _ = sb("mv", [128, 4, 2], F32)
        bnst, _ = sb("bnst", [128, 4, 2, 6], F32)
        lnr, _ = sb("lnr", [128, 4], F32)
        poolw = at("poolw", [128, 4, 2, 256], F32, m_o)
        wst = at("wst", [128, 4, 128], F32, m_o + 8192)
        sgub = at("sgub", [128, 4, 128], F32, m_o + 10240)
        wsr = at("wsr", [128, 4, 128], F32, bh_o)
        vtok = f[:, :, :].rearrange("p k t -> p (k t)").rearrange("p (i c) -> p i c", i=4)
        cpad = at("cpad", [128, 2, 528], F32, f_o)
        csum = at("csum", [128, 2, 528], F32, f_o + 4224)
        diff = at("diff", [128, KD, T], F32, bl_o)
        prow = at("prow", [128, 4, 256], F32, bh_o + 6 * 2048)
        qn = at("qn", [128, 3, T], F32, bh_o)
        kvn = at("kvn", [128, 4, T], F32, bh_o + 6144)
        dq = at("dq", [128, 3, T], F32, bh_o + 14336)
        dk = at("dk", [128, 3, T], F32, bh_o + 20480)
        cab = at("cab", [128, 2, T], F32, bh_o + 14336)
        cac = at("cac", [128, 2, T], F32, bh_o + 18432)
        ccv = at("ccv", [128, 2, T], F32, bh_o + 22528)
        blk = at("blk", [128, 31, 32], F32, bh_o + 26624)
        pcmp = at("pcmp", [128, 24, 32], F32, bh_o + 26624)
        vcs = at("vcs", [31, 128], F32, bh_o + 26624 + 4096)
        kcs = at("kcs", [128, 32], F32, bh_o + 26624 + 4608)
        hcs = at("hcs", [128, 32], F32, bh_o + 26624 + 4736)
        pes = at("pes", [128, 2, 32], F32, bh_o + 26624 + 4864)
        pcs = at("pcs", [128, 3, 24], F32, bh_o + 26624 + 5120)
        w2s = at("w2s", [128, 2, 64], F32, bh_o + 26624 + 5408)
        dv = at("dv", [128, 4, 384], F32, ah_o)
        odil = at("odil", [128, 3, T], F32, m_o)
        nz = at("nz", [128, 3, T], F32, m_o + 6144)
        ptr = at("ptr", [128, 3, T], F32, f_o)
        prb = at("prb", [128, 4, T], F32, f_o + 6144)
        stat = at("stat", [128, 256], F32, f_o + 14336)
        w1s = at("w1s", [128, 2, 32, 64], F32, al_o)
        perow = at("perow", [32, 2, 2, 64], F32, ah_o + 8192)

        G = [ctx.enter_context(nc.psum_tensor(f"G{i}", [128, T], F32)) for i in range(4)]
        X = [ctx.enter_context(nc.psum_tensor(f"X{i}", [128, T], F32)) for i in range(4)]
        gfree = [[] for _ in range(4)]
        xfree = [[] for _ in range(4)]

        pe, dve, sca, pool, sp = (Queue(sem(n)) for n in ("s_pe", "s_dve", "s_act", "s_pool", "s_sp"))
        raw_sem = [sem(f"s_raw{i}") for i in range(NRAW)]
        s_out = sem("s_out")
        n_sem = [0]

        def load(q, dst, src, *after, waits=1):
            n_sem[0] += 1
            s = sem(f"s_ld{n_sem[0]}")
            q.put(lambda e: e.dma_start(dst, src).then_inc(s, 16), *after, inc=False)
            return (s, 16)

        def mm(o, lhs, rhs, start, stop, *after, inc=False):
            return pe.put(lambda e: e.matmul(o, lhs, rhs, start=start, stop=stop), *after, inc=inc)

        def tr(o, i, idn, *after, inc=False):
            return pe.put(lambda e: e.transpose(o, i, idn), *after, inc=inc)

        def act(o, i, fn, *after, **kw):
            return sca.put(lambda e: e.activation(o, i, fn, **kw), *after)

        def copy(q, o, i, *after):
            if q is sca:
                return act(o, i, ACT.Copy, *after)
            return q.put(lambda e: e.tensor_copy(o, i), *after)

        def tt(q, o, i0, i1, op, *after):
            return q.put(lambda e: e.tensor_tensor(o, i0, i1, op), *after)

        def stt(o, i0, s, i1, op0, op1, *after):
            return dve.put(lambda e: e.scalar_tensor_tensor(o, i0, s, i1, op0, op1), *after)

        def ts(q, o, i, s1, s2, op0, op1, *after):
            if s2 is None:
                return q.put(lambda e: e.tensor_scalar(o, i, s1, None, op0), *after)
            return q.put(lambda e: e.tensor_scalar(o, i, s1, s2, op0, op1), *after)

        def red(o, i, op, *after, **kw):
            return dve.put(lambda e: e.tensor_reduce(o, i, AX, op, **kw), *after)

        def rec(o, i, *after):
            return dve.put(lambda e: e.reciprocal(o, i), *after)

        acts = Ring([act_t[:, i, :] for i in range(4)])
        tmps = Ring([tmp_t[:, i, :] for i in range(4)])
        sqs = Ring([sq_t[:, i, :] for i in range(2)])

        units = []
        split_done, pe_done = [], []
        sent = [0]
        raw_count = [0] * NRAW
        raw_tok = []

        def add_units(pieces_of, nk, wid):
            first = len(units)
            for k0 in range(0, nk, 2):
                units.append((pieces_of(k0, min(2, nk - k0)), min(2, nk - k0), wid))
            return (first, nk, wid)

        def plain(w, parts, row0=0):
            def pieces(k0, n):
                o, got = 0, []
                for c0, c1 in parts:
                    src = w[row0 + k0 * 128:row0 + (k0 + n) * 128, c0:c1].rearrange("(k p) c -> p k c", p=128)
                    got.append((0, 128, 0, n, o, c1 - c0, src))
                    o += c1 - c0
                return got
            return pieces

        def send(j):
            pieces, nk, wid = units[j]
            s = j % NRAW
            after = split_done[j - NRAW] if j >= NRAW else []
            v = raw[:, s, 0:nk * wid].rearrange("p (k c) -> p k c", k=nk)
            for p0, p1, k0, n, o, c, src in pieces:
                dst = v[p0:p1, k0:k0 + n, o:o + c] if o is not None else c(v[p0:p1, k0])
                sp.put(lambda e, dst=dst, src=src: e.dma_start(dst, src).then_inc(raw_sem[s], 16), after, inc=False)
                raw_count[s] += 16
            raw_tok.append((raw_sem[s], raw_count[s]))

        def split(j):
            pieces, nk, wid = units[j]
            n = nk * wid
            r, d = j % NRAW, j % NSPLIT
            used = pe_done[j - NSPLIT] if j >= NSPLIT else None
            hi = act(whi[:, d, 0:n], raw[:, r, 0:n], ACT.Copy, raw_tok[j], used)
            lo = tt(dve, wlo[:, d, 0:n], raw[:, r, 0:n], whi[:, d, 0:n].bitcast(F32), ALU.subtract, hi, raw_tok[j], used)
            split_done.append([hi, lo])

        def ahead(n):
            while len(split_done) <= min(n + AHEAD, len(units) - 1):
                while sent[0] <= min(len(split_done) + NRAW - 1, len(units) - 1):
                    send(sent[0])
                    sent[0] += 1
                split(len(split_done))

        background = []

        def pump():
            while background:
                try:
                    next(background[0])
                    return
                except StopIteration:
                    background.pop(0)

        def drain_background():
            while background:
                pump()

        def gemm(group, x, tiles, by_token=False, order=None, pumps=(), hooks=None, ks=None):
            first, nk, wid = group
            done = [None] * tiles
            order = order or list(range(tiles))
            for u in range(0, nk, 2):
                n = first + u // 2
                ahead(n)
                d = n % NSPLIT
                kn = min(2, nk - u)
                tok = None
                for ti, m in enumerate(order):
                    for kk in range(kn):
                        k = ks[u + kk] if ks else u + kk
                        wv = [w[:, d, kk * wid:(kk + 1) * wid] for w in (whi, wlo)]
                        xv = [v[:, x.first + k, :] for v in (x.hi, x.lo)]
                        for wi, xi in ((0, 0), (0, 1), (1, 0)):
                            if by_token:
                                o, lhs, rhs = G[m][:, 0:wid], xv[xi][:, m * 128:(m + 1) * 128], wv[wi]
                            else:
                                lhs = wv[wi][:, m * 128:(m + 1) * 128]
                                o, rhs = G[m][:, :], xv[xi]
                            s, e = u + kk == 0 and wi + xi == 0, u + kk == nk - 1 and wi == 1
                            inc = (kk == kn - 1 and wi == 1) and (u + kk == nk - 1 or ti == tiles - 1)
                            tok = mm(o, lhs, rhs, s, e, split_done[n], x.ready[x.first + k],
                                     gfree[m] if s else None, inc=inc)
                            if e:
                                done[m] = tok
                    if ti in pumps:
                        pump()
                    if hooks and (u, ti) in hooks:
                        hooks[u, ti]()
                pe_done.append(tok)
            for k in range(nk):
                x.war[x.first + k] = [pe_done[-1]]
            return done

        at_bank = [0]

        def gemm_tile(n):
            b = at_bank[0] % 2
            at_bank[0] += 1
            ahead(n)
            d = n % NSPLIT
            for k in range(KD):
                for wi, xi in ((0, 0), (0, 1), (1, 0)):
                    w, x = (whi, wlo)[wi][:, d, k * 128:(k + 1) * 128], (XO.hi, XO.lo)[xi][:, k, :]
                    s, e = k == 0 and wi + xi == 0, k == KD - 1 and wi == 1
                    t = mm(G[b][:, :], w, x, s, e, split_done[n], XO.ready[k], gfree[b] if s else None, inc=e)
                if k % 2:
                    pump()
            pe_done.append(t)
            for k in range(KD):
                XO.war[k] = [t]
            return b, t

        def split_tile(i, t, tok, x, k):
            hi = act(x.hi[:, k, :], t, ACT.Copy, tok, x.war[k])
            lo = tt(dve, x.lo[:, k, :], t, x.hi[:, k, :].bitcast(F32), ALU.subtract, hi, x.war[k])
            x.ready[k] = [hi, lo]
            if i is not None:
                tmps.free[i] = [lo]

        XO, AO, BO = Operand(xh, xl), Operand(ah, al), Operand(bh, bl)
        PO = Operand(bh, bl, 4)

        A = a
        plan = {}

        def ffn_units(name, wg, wu, wd):
            for hf, (g0, g1) in enumerate(((0, 6), (6, 11))):
                for g in range(g0, g1):
                    c = g * 256

                    def pieces(k0, n, c=c):
                        return [(0, 128, 0, n, o, 256,
                                 w[k0 * 128:(k0 + n) * 128, c:c + 256].rearrange("(k p) c -> p k c", p=128))
                                for o, w in ((0, wg), (256, wu))]
                    plan[name, "gu", g] = add_units(pieces, KD, 512)
                for c in range(2):
                    plan[name, "dn", hf, c] = add_units(plain(wd, [(c * 512, c * 512 + 512)], g0 * 256),
                                                        2 * (g1 - g0), 512)

        def two(name, w, nk, c0=0):
            for c in range(2):
                plan[name, c] = add_units(plain(w, [(c0 + c * 512, c0 + c * 512 + 512)]), nk, 512)

        def inter(names):
            for c in range(2):
                for name, w, nk, c0 in names:
                    plan[name, c] = add_units(plain(w, [(c0 + c * 512, c0 + c * 512 + 512)]), nk, 512)

        ffn_units("ffn1", A["ffn1_w_gate"][0], A["ffn1_w_up"][0], A["ffn1_w_down"][0])
        win = A["w_in"][0]
        two("v", win, KD, D)
        two("u", win, KD, 0)
        two("c", win, KD, 2 * D)
        inter([("ga", win, KD, 3 * D), ("oa", A["w_out_a"][0], KD, 0)])
        inter([("gb", win, KD, 4 * D), ("ob", A["w_out_b"][0], KD, 0)])
        two("wo", A["w_o"][0], KD)
        ffn_units("ffn2", A["ffn2_w_gate"][0], A["ffn2_w_up"][0], A["ffn2_w_down"][0])
        inter([("pg", A["ple_w_gate"][0], KD, 0), ("pp", A["ple_w_proj"][0], 2, 0)])
        w2 = A["w_in_2"][0]

        for name, parts in (("dq", [(2578, 2962)]), ("dk", [(2962, 3346)]), ("dv", [(3346, 3730)]),
                            ("vg", [(1792, 1920), (2048, 2194)])):
            plan[name] = add_units(plain(w2, parts), KD, sum(c1 - c0 for c0, c1 in parts))

        def column(*parts):
            o, got = 0, []
            for c0, c1 in parts:
                got.append((0, 128, 0, KD, o, c1 - c0, w2[:, c0:c1].rearrange("(k p) c -> p k c", p=128)))
                o += c1 - c0
            units.append((got, KD, 128))
            return len(units) - 1

        def pair_column(c0, r_):
            return column(*[(c0 + 192 * g + 64 * r_, c0 + 192 * g + 64 * r_ + 64) for g in range(2)])

        tiles_in = [(("q", r_), pair_column(1024, r_)) for r_ in range(3)]
        tiles_in += [(("kv", n), column((c, c + 128))) for n, c in enumerate((1408, 1536, 1664, 1920))]
        tiles_in += [(("nz", r_), pair_column(2194, r_)) for r_ in range(3)]
        tiles_in += [((n, m), column((c + 128 * m, c + 128 * m + 128))) for n, c in (("b", 0), ("c", 256))
                     for m in range(2)]
        tiles_in += [((n, m), column((c + 128 * m, c + 128 * m + 128))) for m in range(2)
                     for n, c in (("h", 512), ("z", 768))]
        tiles_in += [(("dz", m), column((3730 + 128 * m, 3858 + 128 * m))) for m in range(3)]
        wout2 = A["w_out_2"][0]

        out2_k = [0, 1, 2, 3, 5, 6, 7, 4]

        def wout_pieces(c0):
            def rows(p0, p1, k, r0):
                return (p0, p1, k, 1, 0, 512, wout2[r0:r0 + p1 - p0, c0:c0 + 512].rearrange("p (k c) -> p k c", k=1))

            def pieces(k0, n):
                got = []
                for i, k in enumerate(out2_k[k0:k0 + n]):
                    if 2 <= k < 5:
                        got += [rows(64 * g, 64 * g + 64, i, 256 + 192 * g + 64 * (k - 2)) for g in range(2)]
                    else:
                        got.append(rows(0, 128, i, k * 128))
                return got
            return pieces

        for c in range(2):
            plan["out2", c] = add_units(wout_pieces(c * 512), KD, 512)
        inter([("pg2", A["w_ple_gate_2"][0], KD, 0), ("pp2", A["w_ple_proj_2"][0], 2, 0)])

        xrow = f[:, :, :].rearrange("p k t -> p (k t)").rearrange("p (i c) -> p i c", i=4)
        x_tok = [load(sp, xrow[:, i, :], A["x"][0, i * 128:(i + 1) * 128, :]) for i in range(4)]
        grow = tmp_t[:, 3, 0:128]
        g_tok, r = [], 0
        colat = {}
        for name, n in COLS:
            src = A[name][0].rearrange("k (a c) -> (k a) c", c=128) if name == "conv_w_2" else \
                (A[name] if name == "norm_final_2" else A[name][0]).rearrange("(a c) -> a c", c=128)
            g_tok.append(load(sca, tmp_t[r:r + n, 3, 0:128], src))
            colat[name] = r
            r += n

        def col(name, m):
            return cols[:, colat[name] + m:colat[name] + m + 1]

        k1 = pool.put(lambda e: e.memset(ident[:, :], 0.0))
        k_id = pool.put(lambda e: e.affine_select(out=ident[:, :], in_=ident[:, :], compare_op=ALU.not_equal, fill=1.0,
                                                  base=0, pattern=[[-1, 128]], channel_multiplier=1), k1)
        k_idb = copy(pool, identb[:, :], ident[:, :], k_id)
        k_ones = pool.put(lambda e: e.memset(ones[:, :], 1.0))
        k_eps = pool.put(lambda e: e.memset(eps[:, :], EPS))
        for t in range(15):
            k_inv = pool.put(lambda e, t=t: e.memset(inv[:, t:t + 1], 1.0 / (t + 1)))
        zero = sq_t[:, 0, 0:128]
        k_z = pool.put(lambda e: e.memset(zero, 0.0))
        keep = dict(compare_op=ALU.is_ge, fill=NEG, base=0)
        k_mc = pool.put(lambda e: e.affine_select(out=mcaus[:, :], in_=zero, pattern=[[-1, 128]],
                                                  channel_multiplier=1, **keep), k_z)
        k_mb = pool.put(lambda e: e.affine_select(out=mband[:, 0, :], in_=zero, pattern=[[1, 128]],
                                                  channel_multiplier=-1, **keep), k_z)
        k_mb = copy(pool, mband[:, 1, :], mcaus[:, :], k_mc)
        zc = sq_t[:, 0, 0:124].rearrange("p (i n) -> p i n", i=4)
        k_cm = pool.put(lambda e: e.affine_select(out=mcmp[:, :, :], in_=zc, pattern=[[128, 4], [-16, 31]],
                                                  channel_multiplier=1, compare_op=ALU.is_ge, fill=NEG, base=-31), k_z)
        k_md = []
        for n, (d, md) in enumerate(((4, md4), (16, md16))):
            o = sq_t[0:d, 1, n * 128:n * 128 + 128].rearrange("p (a b) -> p a b", b=d)
            kz = pool.put(lambda e, o=o: e.memset(o, 0.0))
            ko = pool.put(lambda e, o=o, d=d: e.affine_select(out=o, in_=o, compare_op=ALU.not_equal, fill=1.0, base=0,
                                                              pattern=[[0, 128 // d], [1, d]],
                                                              channel_multiplier=-1), kz)
            oh = sq_t[0:d, 1, n * 128:n * 128 + 128]
            kp = mm(X[3][:, n * 128:n * 128 + 128], oh, oh, True, True, ko, inc=True)
            mt = sq_t[:, 0, 128 + n * 128:256 + n * 128]
            kd = ts(dve, mt, X[3][:, n * 128:n * 128 + 128], -1.0, -NEG, ALU.add, ALU.mult, kp)
            k0 = copy(pool, md[:, 0, :], mt, kd)
            k_md.append(pool.put(lambda e, md=md, mt=mt: e.affine_select(
                out=md[:, 1, :], in_=mt, pattern=[[-1, 128]], channel_multiplier=1, **keep), kd))
            xfree[3] = [kd]
        sqs.free = [[k_cm, k_md], [kp]]

        k_g = tr(X[2][:, 0:104], tmp_t[0:104, 3, 0:128], ident[0:104, 0:104], g_tok, k_id, inc=True)
        k_cols = copy(dve, cols[:, :], X[2][:, 0:104], k_g)
        xfree[2] = [k_cols]
        tmps.free[3] = [k_g]
        k_half = [ts(dve, half[:, 8 * n:8 * n + 8], cols[:, colat[w]:colat[w] + 8], 0.5, None, ALU.mult, None, k_cols)
                  for n, w in enumerate(("ffn1_post_g", "ffn2_post_g"))]

        h_tok = [None] * KD
        for k in range(KD):
            b = (0, 1)[k % 2]
            for i in range(4):
                t = tr(X[b][:, i * 128:(i + 1) * 128], xrow[:, i, k * 128:(k + 1) * 128], ident[:, :],
                       x_tok[i], k_id, xfree[b], inc=(i == 3))
            h_tok[k] = copy(dve, h[:, k, :], X[b][:, :], t)
            xfree[b] = [h_tok[k]]
        f_tok = [[t] for _ in range(KD)]

        ws_t = load(pool, wsr[:, :, :], A["sgu_w"][0].rearrange("g t s -> t g s"))
        for g in range(4):
            k_ws = pool.put(lambda e, g=g: e.affine_select(out=wsr[:, g, :], in_=wsr[:, g, :], pattern=[[-1, 128]],
                                                           channel_multiplier=1, compare_op=ALU.is_ge, fill=0.0,
                                                           base=0), ws_t)
        sgb_t = load(pool, sgub[:, :, :].rearrange("p g t -> p (g t)"),
                     A["sgu_b"].rearrange("a g t -> a (g t)").partition_broadcast(128))
        pw_t = load(pool, poolw[:, :, :, :], A["pool_w"][0].rearrange("g (k p) d -> p g k d", p=128))

        hs = [h[:, m, :] for m in range(KD)]
        fs = [f[:, m, :] for m in range(KD)]

        def sqrt_soon():
            act(lnr[:, 0:1], eps[:, 0:1], ACT.Sqrt, k_eps)

        class Sums:

            def __init__(self):
                self.n, self.pend = 0, []

            def square(self, tile, tok, ring=sqs):
                i, s, fr = ring.take()
                self.pend.append((ring, i, s, act(s, tile, ACT.Square, tok, fr)))
                ring.free[i] = None

            def add(self, count=2):
                now_, self.pend = self.pend[:count], self.pend[count:]
                for ring, si, s, k in now_:
                    for i in range(4):
                        t = mm(X[0][:, i:i + 1], s[:, i * 128:(i + 1) * 128], ones[:, 0:1], self.n == 0 and i == 0,
                               self.n == KD - 1 and i == 3, k, k_ones, xfree[0] if self.n == 0 else None, inc=(i == 3))
                    ring.free[si] = [t]
                    self.n += 1
                self.t = t

            def factor(self):
                k = act(rtok[:, :], X[0][:, 0:4], ACT.Sqrt, self.t, k_eps, rtok_free[0], bias=eps[:, 0:1],
                        scale=1.0 / D)
                xfree[0] = [k]
                self.rt = rec(rtok[:, :], rtok[:, :], k)
                rtok_free[0] = [self.rt]

            def diagonal(self):
                self.si, self.s, fr = sqs.take()
                self.dg = []
                for i in range(4):
                    o, r = self.s[:, i * 128:(i + 1) * 128], rtok[:, i:i + 1]
                    if i % 2:
                        self.dg.append(act(o, ident[:, :], ACT.Copy, self.rt, fr, scale=r))
                    else:
                        self.dg.append(ts(dve, o, ident[:, :], r, None, ALU.mult, None, self.rt, fr))
                rtok_free[0] = now(self.dg)

            def spread(self):
                for i in range(4):
                    t = mm(X[1][:, i * 128:(i + 1) * 128], ones[:, :], self.s[:, i * 128:(i + 1) * 128], True, True,
                           self.dg[i], xfree[1], inc=(i == 3))
                sqs.free[self.si] = [t]
                return t

        rtok_free = [None]

        class Stats(Sums):

            def tile(self, m):
                self.square(hs[m], h_tok[m], (sqs, acts, acts, tmps)[m // 2])

            def hooks(self):
                def last():
                    self.add(4)
                    self.factor()
                    self.diagonal()

                def end():
                    t = self.spread()
                    self.k = copy(dve, rpre[:, :], X[1][:, :], t)
                    xfree[1] = [self.k]
                return {(4, 2): lambda: self.add(4), (6, 0): last, (6, 2): end}

        def operand_hi(m, gain, tok):
            XO.ready[m] = [act(XO.hi[:, m, :], hs[m], ACT.Copy, tok, k_cols, XO.war[m], scale=gain)]

        def operand_lo(m, gain):
            k = stt(XO.lo[:, m, :], hs[m], gain, XO.hi[:, m, :].bitcast(F32), ALU.mult, ALU.subtract, XO.ready[m],
                    XO.war[m])
            XO.ready[m] = [k]

        def pre_norm(name):
            st = Stats()
            for m in range(KD):
                operand_hi(m, col(name, m), h_tok[m])
                operand_lo(m, col(name, m))
                st.tile(m)
            return st

        class Post(Sums):

            def __init__(self):
                Sums.__init__(self)
                self.toks = [None] * KD

            def tile(self, j, tok):
                self.toks[j] = tok
                if j >= 4:
                    self.square(fs[j], tok)
                    self.add()

            def hooks(self):
                def sq(*ms):
                    for m in ms:
                        self.square(fs[m], self.toks[m])

                def first():
                    self.add()
                    sq(2, 3)
                return {(0, 0): lambda: sq(0, 1), (2, 1): first, (4, 1): self.add}

            def end(self, gain, then):
                self.factor()
                self.diagonal()
                k = self.spread()
                st = Stats()
                for m in range(KD):
                    s = stt(fs[m], fs[m], gain(m), X[1][:, :], ALU.mult, ALU.mult, k, self.toks[m], k_half)
                    h_tok[m] = tt(pool if m in (2, 4, 6) else dve, hs[m], hs[m], fs[m], ALU.add, s, h_tok[m])
                    f_tok[m] = [h_tok[m]]
                    operand_hi(m, col(then, m), h_tok[m])
                    st.tile(m)
                    if m:
                        operand_lo(m - 1, col(then, m - 1))
                operand_lo(KD - 1, col(then, KD - 1))
                xfree[1] = [s]
                return st

        def ffn(name, st, post_n, then, pumps=()):
            hid = lambda i: (AO, i) if i < 8 else (BO, i - 8)
            toks = [None] * KD
            post = Post()
            for hf, (g0, g1) in enumerate(((0, 6), (6, 11))):
                for g in range(g0, g1):
                    done = gemm(plan[name, "gu", g], XO, 4, order=[0, 2, 1, 3], hooks=st.hooks() if g == 0 else None,
                                pumps=pumps if g else ())
                    for p in range(2):
                        si, s, fr = acts.take()
                        k = tt(dve, s, G[p][:, :], rpre[:, :], ALU.mult, st.k, done[p], fr)
                        gfree[p] = [k]
                        k1 = act(s, s, ACT.Silu, k)
                        i, t, fr = tmps.take()
                        k = tt(dve, t, G[2 + p][:, :], rpre[:, :], ALU.mult, done[2 + p], fr)
                        gfree[2 + p] = [k]
                        k = tt(pool, t, t, s, ALU.mult, k1, k)
                        acts.free[si] = [k]
                        split_tile(i, t, k, *hid(2 * (g - g0) + p))
                nk = 2 * (g1 - g0)
                both = Both(AO, BO, nk)
                for c in range(2):
                    done = gemm(plan[name, "dn", hf, c], both, 4, hooks=post.hooks() if hf and c else None)
                    if hf and c:
                        sqrt_soon()
                    for m in range(4):
                        j = 4 * c + m
                        if hf == 0:
                            toks[j] = act(fs[j], G[m][:, :], ACT.Copy, done[m], f_tok[j])
                        else:
                            toks[j] = tt(dve, fs[j], G[m][:, :], fs[j], ALU.add, done[m], toks[j])
                            post.tile(j, toks[j])
                        gfree[m] = [toks[j]]
                both.close()
            return post.end(lambda m: half[:, 8 * post_n + m:8 * post_n + m + 1], then)

        class Both:

            def __init__(self, p, q, n):
                self.p, self.q, self.n, self.first = p, q, n, 0
                self.ready = p.ready + q.ready
                self.war = [None] * 16
                self.hi, self.lo = Pair(p.hi, q.hi), Pair(p.lo, q.lo)

            def close(self):
                for k in range(self.n):
                    (self.p if k < 8 else self.q).war[k % 8] = self.war[k]

        class Pair:
            def __init__(self, p, q):
                self.p, self.q = p, q

            def __getitem__(self, at):
                return self.p[at] if at[1] < 8 else self.q[:, at[1] - 8, :]

        def sgu_weights():
            for g in range(4):
                t = tr(X[2][:, g * 128:(g + 1) * 128], wsr[:, g, :], ident[:, :], k_ws, xfree[2], inc=(g == 3))
            wst_tok.append(copy(dve, wst[:, :, :].rearrange("p g s -> p (g s)"), X[2][:, :], t))
            xfree[2] = wst_tok[:]
            BO.war[0] = [t]
            yield

        wst_tok = []
        background.append(sgu_weights())
        st = ffn("ffn1", pre_norm("ffn1_pre_g"), 0, "mix_pre_g", pumps=(3,))
        k_wst = wst_tok[0]

        k_ln = [None] * 4
        v_tok = [[None, None] for _ in range(4)]
        for c in range(2):
            done = gemm(plan["v", c], XO, 4, by_token=True, hooks=st.hooks() if c == 0 else None)
            for i in range(4):
                v = vtok[:, i, c * 512:(c + 1) * 512]
                v_tok[i][c] = act(v, G[i][:, :], ACT.Gelu_apprx_tanh, done[i], f_tok, st.rt, scale=rtok[:, i:i + 1])
                gfree[i] = [v_tok[i][c]]
                k_bn = dve.put(lambda e, i=i, c=c, v=v: e.bn_stats(bnst[:, i, c, :], v), v_tok[i][c])
        rtok_free[0] = now(rtok_free, v_tok)
        for i in range(4):
            k_ag = dve.put(lambda e, i=i: e.bn_aggr(mv[:, i, :], bnst[:, i, :, :]), k_bn)
        k = act(lnr[:, :], mv[:, :, 1], ACT.Sqrt, k_ag, k_eps, bias=eps[:, 0:1])
        k_lr = rec(lnr[:, :], lnr[:, :], k)
        for i in range(4):
            k_ln[i] = ts(dve, vtok[:, i, :], vtok[:, i, :], mv[:, i, 0:1], lnr[:, i:i + 1], ALU.subtract, ALU.mult,
                         k_lr, v_tok[i])

        def sgu(j, si, u, k_u):
            b = 1 + j % 2
            for i in range(4):
                t = mm(X[b][:, i * 128:(i + 1) * 128], vtok[:, i, j * 128:(j + 1) * 128], wst[:, j // 2, :],
                       True, True, k_ln, k_wst, xfree[b], inc=(i == 3))
            ti, s, fr = tmps.take()
            bb = sgub[:, j // 2, :].unsqueeze(1).to_broadcast([128, 4, 128])
            k = stt(s.rearrange("p (i t) -> p i t", i=4), X[b][:, :].rearrange("p (i t) -> p i t", i=4),
                    col("sgu_norm_g", j), bb, ALU.mult, ALU.add, t, sgb_t, fr)
            xfree[b] = [k]
            k = tt(pool, s, s, u, ALU.mult, k, k_u)
            acts.free[si] = [k]
            split_tile(ti, s, k, AO, j)
            k_sgu[0] = t
            yield

        k_sgu = [None]
        for c in range(2):
            done = gemm(plan["u", c], XO, 4, pumps=(1, 3))
            drain_background()
            for m in range(4):
                j = 4 * c + m
                si, u, fr = acts.take()
                k = tt(dve, u, G[m][:, :], rpre[:, :], ALU.mult, st.k, done[m], fr)
                gfree[m] = [k]
                background.append(sgu(j, si, u, act(u, u, ACT.Gelu_apprx_tanh, k)))

        def pooled(gi):
            got = []
            for n in range(2):
                for kk in range(2):
                    t = mm(X[2 + n][:, :], poolw[:, gi, kk, n * 128:n * 128 + 128], diff[:, 2 * gi + kk, :], kk == 0,
                           kk == 1, k_diff[2 * gi + kk], pw_t, xfree[2 + n], inc=(kk == 1))
                got.append(t)
            for n in range(2):
                di = 2 * gi + n
                ti, s, fr = tmps.take()
                k = act(s, X[2 + n][:, :], ACT.Copy, got[n], fr, scale=col("pool_scale", di))
                xfree[2 + n] = [k]
                BO.war[di] = now(b_war, t)
                split_tile(ti, s, k, BO, di)
            yield

        b_war = now(BO.war)
        k_diff = [None] * KD
        k_c = [None, None]
        k_csum = None
        for c in range(2):
            done = gemm(plan["c", c], XO, 4, pumps=(1, 3))
            drain_background()
            if c == 0:
                k_pad = pool.put(lambda e: e.memset(cpad[:, :, 0:16], 0.0), k_sgu)
                k_c = [k_pad, k_pad]
            for m in range(4):
                j = 4 * c + m
                gi, b = j // 2, j % 2
                w = 2 << gi
                cur = cpad[:, b, :]
                k0 = tt(dve, cpad[:, b, 16:528], G[m][:, :], rpre[:, :], ALU.mult, st.k, done[m], k_c[b], k_sgu)
                gfree[m] = [k0]
                lo, src, k = 0, cur, [k0, k_csum]
                for n in range(gi + 1):
                    dst, sh = csum[:, n % 2, :], 1 << n
                    lo += sh
                    k = [tt(pool, dst[:, lo:528], src[:, lo:528], src[:, lo - sh:528 - sh], ALU.add, k)]
                    src = dst
                t = diff[:, j, :]
                k2 = stt(t, src[:, 16:528], 1.0 / w, cpad[:, b, 16:528], ALU.mult, ALU.subtract, k, b_war)
                k3 = tt(dve, src[:, 16:15 + w], src[:, 16:15 + w], inv[:, 0:w - 1], ALU.mult, k2, k_inv)
                k4 = tt(dve, t[:, 0:w - 1], src[:, 16:15 + w], cpad[:, b, 16:15 + w], ALU.subtract, k3)
                k_csum = k_c[b] = k_diff[j] = k4
                if b:
                    background.append(pooled(gi))
        k_cend = now(k_c, k_csum)

        y_tok = [None] * KD

        def gated(gname, oname, x, use, st, hooks=({}, {}), soon=False):
            for c in range(2):
                done = gemm(plan[gname, c], XO, 4, pumps=(1, 3), hooks=hooks[c])
                drain_background()
                sg = []
                for m in range(4):
                    si, s, fr = acts.take()
                    if st:
                        k = tt(dve, s, G[m][:, :], rpre[:, :], ALU.mult, st.k, done[m], fr)
                        gfree[m] = [k]
                        k = act(s, s, ACT.Sigmoid, k)
                    else:
                        k = act(s, G[m][:, :], ACT.Sigmoid, done[m], fr)
                        gfree[m] = [k]
                    sg.append((si, s, k))
                done = gemm(plan[oname, c], x, 4)
                if soon and c == 1:
                    sqrt_soon()
                for m in range(4):
                    si, s, k = sg[m]
                    k = use(4 * c + m, G[m][:, :], s, [k, done[m]])
                    gfree[m] = [k]
                    acts.free[si] = [k]

        def use_a(j, ps, s, toks):
            y_tok[j] = tt(dve, fs[j], ps, s, ALU.mult, toks, k_cend, k_sgu)
            return y_tok[j]

        def use_b(j, ps, s, toks):
            ti, t, fr = tmps.take()
            k0 = tt(dve, t, ps, s, ALU.mult, toks, fr)
            k = tt(pool, t, t, fs[j], ALU.add, k0, y_tok[j])
            f_tok[j] = [k]
            split_tile(ti, t, k, AO, j)
            return k0

        gated("ga", "oa", AO, use_a, st)
        gated("gb", "ob", BO, use_b, st)
        post = Post()
        for c in range(2):
            done = gemm(plan["wo", c], AO, 4, hooks=post.hooks() if c else None)
            if c:
                sqrt_soon()
            for m in range(4):
                j = 4 * c + m
                k = copy(dve, fs[j], G[m][:, :], done[m], f_tok)
                gfree[m] = [k]
                post.tile(j, k)
        st = post.end(lambda m: col("mix_post_g", m), "ffn2_pre_g")

        def embed(k_p, *after):
            for k in range(2):
                for i in range(4):
                    t = tr(X[3][:, i * 128:(i + 1) * 128], prow[:, i, k * 128:(k + 1) * 128], ident[:, :],
                           k_p, xfree[3], inc=(i == 3))
                ti, s, fr = tmps.take()
                kc = copy(dve, s, X[3][:, :], t, fr)
                xfree[3] = [kc]
                PO.war[4 + k] = now(*after)
                split_tile(ti, s, kc, PO, 4 + k)
                yield
            BO.war[6] = BO.war[7] = [t]

        k_p = load(pool, prow[:, :, :], A["p"][0, 0].rearrange("(i p) c -> p i c", p=128), now(BO.war))
        background.append(embed(k_p, now(BO.war)))
        st = ffn("ffn2", st, 1, "ple_pre_g", pumps=(3,))

        post = Post()

        def use_p(j, ps, s, tk):
            k = tt(dve, fs[j], ps, s, ALU.mult, tk, f_tok)
            post.tile(j, k)
            return k

        gated("pg", "pp", PO, use_p, st, hooks=(st.hooks(), post.hooks()), soon=True)
        st = post.end(lambda m: col("ple_post_g", m), "norm_mix_2")

        k_b2 = now(PO.war, BO.war, AO.war)

        def store(done, dst, *after, scale=None):
            got = []
            for m, d in enumerate(dst):
                got.append(stt(d, G[m][:, :], scale[m] if scale else 1.0, rpre[:, :], ALU.mult, ALU.mult, st.k, done[m],
                               *after))
                gfree[m] = [got[-1]]
            return got

        k_dq = store(gemm(plan["dq"], XO, 3, hooks=st.hooks()), [dq[:, m, :] for m in range(3)], k_b2,
                     scale=[0.125] * 3)
        k_dk = store(gemm(plan["dk"], XO, 3), [dk[:, m, :] for m in range(3)], k_b2)
        done = gemm(plan["dv"], XO, 4, by_token=True)
        k_dv = []
        for i in range(4):
            k_dv.append(act(dv[:, i, :], G[i][:, 0:384], ACT.Copy, done[i], k_b2, st.rt, scale=rtok[:, i:i + 1]))
            gfree[i] = [k_dv[i]]

        ptrs = Ring([ptr[:, i, :] for i in range(3)])
        prbs = Ring([prb[:, i, :] for i in range(4)])
        for r_ in (ptrs, prbs):
            r_.free = [now(f_tok) for _ in r_.aps]
        n_stat = [0]
        k_stat = [pool.put(lambda e: e.memset(stat[:, :], 0.0), f_tok)]

        def stats(n):
            o = n_stat[0]
            n_stat[0] += n
            assert o + n <= 256
            return stat[:, o:o + n]

        class Bank:
            def __init__(self, ap, free, i):
                self.ap, self.of, self.i = ap, free, i

            @property
            def free(self):
                return self.of[self.i]

            @free.setter
            def free(self, toks):
                self.of[self.i] = toks

        s_banks = [Bank(X[0], xfree, 0), Bank(X[1], xfree, 1)]
        t_banks = [Bank(X[2], xfree, 2)]
        o_banks = [Bank(X[3], xfree, 3)]
        turns = {"s": 0, "t": 0}

        def turn(name, banks):
            turns[name] += 1
            return banks[turns[name] % len(banks)]

        def qk(q, k, k0, i, masks, nm, den, *after):
            bank = turn("s", s_banks)
            n = (i + 1) * 128 - k0
            qt = q[:, i * 128:(i + 1) * 128]
            mm(bank.ap[:, 0:n], qt, k[:, k0:k0 + n], True, False, bank.free, *after)
            for mi, (o, mw, m) in enumerate(masks):
                t = mm(bank.ap[:, o:o + mw], identb[:, :], m, False, mi == len(masks) - 1,
                       k_idb, k_mc, k_mb, k_md, inc=(mi == len(masks) - 1))
            k1 = red(nm, bank.ap[:, 0:n], ALU.max, t, k_stat, negate=True)
            pi, p, fr = prbs.take()
            k2 = act(p[:, 0:n], bank.ap[:, 0:n], ACT.Exp, k1, fr, bias=nm, accum_out=den)
            bank.free = [k2]
            return pi, p[:, 0:n], n // 128, k2

        def turn_p(pi, p, nb, k, q):
            bank = turn("t", t_banks)
            for b in range(nb):
                t = tr(bank.ap[:, b * 128:(b + 1) * 128], p[:, b * 128:(b + 1) * 128], ident[:, :], k, bank.free,
                       inc=(b == nb - 1))
            prbs.free[pi] = [t]
            ti, o, fr = ptrs.take()
            kc = copy(q, o[:, 0:nb * 128], bank.ap[:, 0:nb * 128], t, fr)
            bank.free = [kc]
            return ti, o, kc

        k_od = [None] * 4

        def dilated():
            items = [(i, j, gi) for i in range(4) for j in range(2) for gi in range(3)]
            state, turned = {}, {}

            def scores(n):
                i, j, gi = items[n]
                if gi == 0:
                    state[n // 3] = {"nm": stats(3), "den": stats(3), "w": stats(3), "dw": stats(3), "s": stats(2),
                                     "p": [], "k": []}
                st = state[n // 3]
                q, k = (v[64 * j:64 * j + 64, gi, :] for v in (dq, dk))
                if gi == 0:
                    k0 = 128 * max(i - 1, 0)
                    masks = [(0, 256, mband[:, :, :].rearrange("p a c -> p (a c)"))] if i else [(0, 128, mband[:, 1, :])]
                else:
                    k0 = 0
                    md = md4 if gi == 1 else md16
                    masks = [(128 * b, 128, md[:, 0, :]) for b in range(i)] + [(128 * i, 128, md[:, 1, :])]
                st["p"].append(qk(q, k, k0, i, masks, st["nm"][:, gi:gi + 1], st["den"][:, gi:gi + 1], k_dq, k_dk))

            def combine(s):
                st = state[s]
                nM, r_ = st["s"][:, 0:1], st["s"][:, 1:2]
                k = red(nM, st["nm"], ALU.min, [p[3] for p in st["p"]])
                k = act(st["w"], st["nm"], ACT.Exp, k, bias=nM, scale=-1.0)
                k = tt(dve, st["dw"], st["den"], st["w"], ALU.mult, k)
                k = red(r_, st["dw"], ALU.add, k)
                k = rec(r_, r_, k)
                k = ts(dve, st["w"], st["w"], r_, None, ALU.mult, None, k)
                st["k"] = [ts(dve, p[1], p[1], st["w"][:, gi:gi + 1], None, ALU.mult, None, k)
                           for gi, p in enumerate(st["p"])]

            def weigh(n):
                i, j, gi = items[n]
                bank = o_banks[i % len(o_banks)]
                ti, o, kc = turned.pop(n)
                nb = state[n // 3]["p"][gi][2]
                for b in range(nb):
                    kt = i + 1 - nb + b
                    t = mm(bank.ap[64 * j:64 * j + 64, gi * 128:gi * 128 + 128],
                           dv[:, kt, 128 * gi + 64 * j:128 * gi + 64 * j + 64], o[:, b * 128:(b + 1) * 128],
                           b == 0, b == nb - 1, kc, k_dv, bank.free if j == 0 else None, inc=(b == nb - 1))
                ptrs.free[ti] = [t]
                if j == 1 and gi == 2:
                    k_od[i] = copy(sca, odil[:, :, i * 128:(i + 1) * 128],
                                   bank.ap[:, 0:384].rearrange("p (g t) -> p g t", g=3), t, k_b2)
                    bank.free = [k_od[i]]

            for n in range(4):
                scores(n)
                yield
            combine(0)
            for n in range(len(items)):
                s, gi = n // 3, n % 3
                if gi == 2 and s + 1 < 8:
                    combine(s + 1)
                pi, p, nb, _ = state[s]["p"][gi]
                turned[n] = turn_p(pi, p, nb, state[s]["k"][gi], dve if n % 2 else sca)
                if n + 4 < len(items):
                    scores(n + 4)
                if n:
                    weigh(n - 1)
                yield
            weigh(len(items) - 1)

        k_w1 = [load(pool, w1s[64 * g:64 * g + 64, kv, :, :], A["cmp_w1_2"][0, kv].rearrange("(l e) o -> e l o", e=64),
                     k_b2) for kv in range(2) for g in range(2)]
        k_w2 = [load(pool, w2s[64 * g:64 * g + 64, :, :], A["cmp_w2_2"][0].rearrange("v e o -> e v o"), k_b2)
                for g in range(2)]
        k_pe = [load(pool, perow[:, :, g, :], A["cmp_pe_2"][0].rearrange("v l e -> l v e"), k_b2) for g in range(2)]
        k_pc = [None]
        k_q, k_kv, k_nz = [None] * 3, [None] * 4, [None] * 3

        def compress():
            b0, b1 = s_banks
            b2 = t_banks[0]
            for kv in range(2):
                t = tr(b2.ap[:, kv * 32:kv * 32 + 32], perow[:, kv, :, :].rearrange("l g e -> l (g e)"),
                       ident[0:32, 0:32], k_pe, b2.free, inc=True)
            k = copy(dve, pes[:, :, :].rearrange("p v l -> p (v l)"), b2.ap[:, 0:64], t, k_b2)
            b2.free = [k]
            t2 = None
            for kv in range(2):
                assert k_kv[kv]
                src = kvn[:, kv, :]
                win_ = bass.AP(tensor=src.tensor, offset=src.offset, ap=[list(src.ap[0]), [16, 31], [1, 32]])
                kb = tt(dve, blk[:, :, :], win_, pes[:, kv, :].unsqueeze(1).to_broadcast([128, 31, 32]), ALU.add,
                        k, k_kv[kv], t2)
                yield
                for l in range(32):
                    for g in range(2):
                        sl = slice(64 * g, 64 * g + 64)
                        t = mm(b0.ap[sl, 0:31], w1s[sl, kv, l, :], blk[sl, :, l], l == 0, l == 31, kb, k_w1, b0.free,
                               inc=(l == 31 and g == 1))
                    if l % 16 == 15:
                        yield
                t2 = t
                kh = act(hcs[:, 0:31], b0.ap[:, 0:31], ACT.Silu, t, k_pc[0])
                b0.free = [kh]
                yield
                for g in range(2):
                    sl = slice(64 * g, 64 * g + 64)
                    if kv == 0:
                        t = mm(b1.ap[sl, 0:31], w2s[sl, kv, :], hcs[sl, 0:31], True, True, kh, k_w2, b1.free,
                               inc=True)
                    else:
                        t = mm(b1.ap[0:31, 64 * g:64 * g + 64], hcs[sl, 0:31], w2s[sl, kv, :], True, True, kh, k_w2,
                               b1.free, t, inc=True)
                    if g == 1 and kv == 0:
                        k_pc[0] = copy(dve, kcs[:, 0:31], b1.ap[:, 0:31], t)
                        b1.free = [k_pc[0]]
                if kv == 1:
                    k_vc = copy(dve, vcs[:, :], b1.ap[0:31, 0:128], t)
                    b1.free = [k_vc]
            k_s = []
            for g in range(2):
                bank = s_banks[g]
                v = bank.ap[:, 0:384].rearrange("p (a n) -> p a n", n=32)
                sl = slice(64 * g, 64 * g + 64)
                for i in range(4):
                    for r_ in range(3):
                        t = mm(v[:, i * 3 + r_, 0:31], qn[sl, r_, i * 128:(i + 1) * 128], kcs[sl, 0:31], True, True,
                               k_q, k_pc[0], bank.free, inc=(i == 3 and r_ == 2))
                for i in range(4):
                    k = tt(dve, pcmp[:, i * 6 + g * 3:i * 6 + g * 3 + 3, 0:31], v[:, i * 3:i * 3 + 3, 0:31],
                           mcmp[:, i, :].unsqueeze(1).to_broadcast([128, 3, 31]), ALU.add, t, t2, k_cm)
                    k_s.append(k)
                bank.free = [k]
                yield
            pc = pcmp[:, :, 0:31]
            mx, dn = pcs[:, 0, :], pcs[:, 1, :]
            bc = lambda v: v.unsqueeze(2).to_broadcast([128, 24, 31])
            k = red(mx, pc, ALU.max, k_s)
            k = ts(dve, mx, mx, -1.0e20, None, ALU.max, None, k)
            k = tt(dve, pc, pc, bc(mx), ALU.subtract, k)
            k = act(pc, pc, ACT.Exp, k)
            yield
            k = red(dn, pc, ALU.add, k)
            k = ts(dve, dn, dn, 1e-30, None, ALU.max, None, k)
            k = rec(dn, dn, k)
            gc = gates[:, :, :].rearrange("p i (n b) -> p (i n) b", b=3)[:, :, 0]
            k = tt(dve, dn, dn, gc, ALU.mult, k, k_gt)
            k_pc[0] = [tt(dve, pc, pc, bc(dn), ALU.mult, k), k_vc]
            for k in range(KD):
                AO.war[k] = now(k_od, k_b2, k_pe, k_pc[0])

        def sparse():
            items = [(r_, i, g, b) for r_ in range(3) for i in range(4) for g in range(2) for b in range(2)]
            state, scaled, turned = {}, {}, {}
            pct_free = [now(sqs.free), now(sqs.free)]
            pct_tok = [None, None]

            def scores(n):
                r_, i, g, b = items[n]
                nm, den = stats(1), stats(1)
                sl = slice(64 * g, 64 * g + 64)
                state[n] = (den, *qk(qn[sl, r_, :], kvn[sl, 2 + b, :], 0, i, [(128 * i, 128, mcaus[:, :])], nm, den,
                                     k_q, k_kv))

            def scale(n):
                r_, i, g, b = items[n]
                den, pi, p, nb, k = state[n]
                c = (g * 3 + r_) * 3 + 1 + b
                k = rec(den, den, k)
                scaled[n] = ts(dve, p, p, den, gates[:, i, c:c + 1], ALU.mult, ALU.mult, k, k_gt)

            def coarse(n):
                r_, _, g, _ = items[n]
                bank = turn("t", t_banks)
                for i in range(4):
                    t = tr(bank.ap[0:31, i * 128:(i + 1) * 128], pcmp[:, i * 6 + g * 3 + r_, 0:31], ident[:, :],
                           k_pc[0], bank.free, inc=(i == 3))
                pct_tok[g] = copy(sca, sq_t[0:31, g, :], bank.ap[0:31, :], t, pct_free[g])
                bank.free = [pct_tok[g]]

            def weigh(n):
                r_, i, g, b = items[n]
                bank = o_banks[r_ % 2]
                o = bank.ap[64 * g:64 * g + 64, i * 128:(i + 1) * 128]
                sl = slice(64 * g, 64 * g + 64)
                if b == 0:
                    t = mm(o, vcs[:, sl], sq_t[0:31, g, i * 128:(i + 1) * 128], True, False, k_pc[0], pct_tok[g],
                           bank.free if i == 0 else None, inc=True)
                    if i == 3:
                        pct_free[g] = [t]
                ti, p, kc = turned.pop(n)
                for j in range(i + 1):
                    t = mm(o, vnt[:, j, 128 * b + 64 * g:128 * b + 64 * g + 64], p[:, j * 128:(j + 1) * 128], False,
                           b == 1 and j == i, kc, k_v, inc=(j == i))
                ptrs.free[ti] = [t]
                if i == 3 and g == 1 and b == 1:
                    assert k_nz[r_]
                    ti, y, fr = tmps.take()
                    k = tt(dve, y, bank.ap[:, :], nz[:, r_, :], ALU.mult, t, k_nz[r_], fr)
                    bank.free = [k]
                    split_tile(ti, y, k, AO, 2 + r_)

            assert all(k_q + k_kv)
            n_stat[0] = 0
            k_stat[0] = pool.put(lambda e: e.memset(stat[:, :], 0.0), now(prbs.free, k_pc[0]))
            coarse(0)
            for n in range(3):
                scores(n)
                yield
            scale(0)
            for n in range(len(items)):
                if n + 1 < len(items):
                    scale(n + 1)
                if n + 2 < len(items) and items[n + 2][1] == 0 and items[n + 2][3] == 0:
                    coarse(n + 2)
                turned[n] = turn_p(*state.pop(n)[1:4], scaled.pop(n), dve if n % 2 else sca)
                if n + 3 < len(items):
                    scores(n + 3)
                if n:
                    weigh(n - 1)
                yield
            weigh(len(items) - 1)
            sqs.free = [pct_free[0], pct_free[1]]

        def attention():
            yield from dilated()
            yield from compress()
            yield from sparse()

        background.append(attention())

        done = gemm(plan["vg"], XO, 4, by_token=True, pumps=(1, 3))
        k_v, k_gt = [], []
        for i in range(4):
            k_v.append(act(vnt[:, i, :], G[i][:, 0:256], ACT.Copy, done[i], st.rt, scale=rtok[:, i:i + 1]))
            k_gt.append(ts(dve, gates[:, i, :], G[i][:, 256:274], rtok[:, i:i + 1], None, ALU.mult, None, k_v[i]))
            gfree[i] = [k_v[i], k_gt[i]]
        rtok_free[0] = now(rtok_free, k_dv, k_v, k_gt)
        k_gt = act(gates[:, :, :], gates[:, :, :], ACT.Sigmoid, k_gt)

        t_banks.append(Bank(G[2], gfree, 2))
        o_banks.append(Bank(G[3], gfree, 3))
        kept = {}

        def store_tile(n, dst, *after, scale=1.0):
            b, t = gemm_tile(n)
            gfree[b] = [stt(dst, G[b][:, :], scale, rpre[:, :], ALU.mult, ALU.mult, st.k, t, *after)]
            return gfree[b][0]

        for (name, m), n in tiles_in:
            if name == "q":
                k_q[m] = store_tile(n, qn[:, m, :], k_b2, scale=0.125)
            elif name == "kv":
                k_kv[m] = store_tile(n, kvn[:, m, :], k_b2)
            elif name == "nz":
                k_nz[m] = store_tile(n, nz[:, m, :], k_b2)
                if m == 2:
                    k_nz[:] = [act(nz[:, r_, :], nz[:, r_, :], ACT.Silu, k_nz[r_]) for r_ in range(3)]
            elif name in "bc":
                assert all(k_od)
                kept[name, m] = store_tile(n, (cab if name == "b" else cac)[:, m, :], k_b2, k_od)
            elif name == "h":
                u, cv = cac[:, m, :], ccv[:, m, :]
                w = lambda n, m=m: cols[:, colat["conv_w_2"] + 2 * n + m:colat["conv_w_2"] + 2 * n + m + 1]
                si, s, fr = acts.take()
                k0 = store_tile(n, s, fr)
                k0 = tt(dve, u, s, u, ALU.mult, kept["c", m], k0)
                acts.free[si] = [k0]
                k = ts(dve, cv, u, w(2), col("conv_b_2", m), ALU.mult, ALU.add, k0, k_b2, k_od)
                k = stt(cv[:, 1:], u[:, :T - 1], w(1), cv[:, 1:], ALU.mult, ALU.add, k)
                k = stt(cv[:, 2:], u[:, :T - 2], w(0), cv[:, 2:], ALU.mult, ALU.add, k)
                kept["h", m] = tt(pool, cv, cv, cab[:, m, :], ALU.mult, k, kept["b", m])
            else:
                si, s, fr = acts.take()
                kept[name, m] = (si, s, store_tile(n, s, fr))
                acts.free[si] = [kept[name, m][2]]
            for last_tile, other, first in ((("z", 1), "h", 0), (("dz", 2), None, 5)):
                if (name, m) == last_tile:
                    assert AO.war[0]
                    sil = [(kept[name, j], act(kept[name, j][1], kept[name, j][1], ACT.Silu, kept[name, j][2]))
                           for j in range(m + 1)]
                    for j, ((si, s, _), k) in enumerate(sil):
                        ti, t, fr = tmps.take()
                        o, ko = (ccv[:, j, :], kept["h", j]) if other else (odil[:, j, :], k_od)
                        k = tt(pool, t, s, o, ALU.mult, k, ko, fr)
                        acts.free[si] = [k]
                        split_tile(ti, t, k, AO, first + j)
        drain_background()

        k_all = now(k_pc[0], AO.ready, list(kept[n, m] for n in "bch" for m in range(2)))
        k_p = load(pool, prow[:, :, :], A["p_2"][0, 0].rearrange("(i p) c -> p i c", p=128), k_all)
        background.append(embed(k_p, k_all))

        for c in range(2):
            done = gemm(plan["out2", c], AO, 4, pumps=(3,) if c else (), ks=out2_k)
            for m in range(4):
                j = 4 * c + m
                h_tok[j] = tt(dve, hs[j], G[m][:, :], hs[j], ALU.add, done[m], h_tok[j])
                gfree[m] = [h_tok[j]]
                split_tile(None, hs[j], h_tok[j], XO, j)

        drain_background()
        k_att = now(f_tok, ptrs.free, prbs.free)

        class Final(Sums):

            def __init__(self):
                Sums.__init__(self)
                self.gained = []

            def tile(self, j):
                if j >= 4:
                    self.square(hs[j], h_tok[j])
                    self.add()
                self.gained.append(ts(dve if j == KD - 1 else pool, fs[j], hs[j], col("norm_final_2", j), None, ALU.mult,
                                      None, h_tok[j], k_att))

            def hooks(self):
                def sq(*ms):
                    for m in ms:
                        self.square(hs[m], h_tok[m])

                def first():
                    self.add()
                    sq(2, 3)
                return {(0, 0): lambda: sq(0, 1), (2, 1): first, (4, 1): self.add}

        last = Final()

        def use_p2(j, ps, s, tk):
            ti, t, fr = tmps.take()
            k0 = tt(dve, t, ps, s, ALU.mult, tk, fr)
            h_tok[j] = tt(dve if j > 5 else pool, hs[j], hs[j], t, ALU.add, k0, h_tok[j], XO.ready[j])
            tmps.free[ti] = [h_tok[j]]
            last.tile(j)
            return k0

        gated("pg2", "pp2", PO, use_p2, None, hooks=({}, last.hooks()), soon=True)
        last.factor()
        orow = out[0].rearrange("(i p) c -> p i c", p=128)
        banks = [(X[1], xfree, 1), (X[2], xfree, 2), (X[3], xfree, 3)] + [(G[i], gfree, i) for i in range(4)]
        for n in range(8):
            hf, i = n // 4, n % 4
            bank, free, b = banks[n % 7]
            for j in range(4):
                q = tr(bank[:, j * 128:(j + 1) * 128], fs[4 * hf + j][:, i * 128:(i + 1) * 128], ident[:, :],
                       last.gained[4 * hf + j], free[b], inc=(j == 3))
            ri, r, fr = (acts, tmps)[n % 2].take()
            if n % 2:
                k = ts(dve, r, bank[:, :], rtok[:, i:i + 1], None, ALU.mult, None, q, last.rt, fr)
            else:
                k = act(r, bank[:, :], ACT.Copy, q, last.rt, fr, scale=rtok[:, i:i + 1])
            free[b] = [k]
            sp.put(lambda e, i=i, hf=hf, r=r: e.dma_start(orow[:, i, hf * 512:hf * 512 + 512], r).then_inc(s_out, 16), k,
                   inc=False)

        block = ctx.enter_context(nc.Block())

        @block.sync
        def _(e):
            sp.run(e)
            e.wait_ge(s_out, 16 * KD)

        @block.gpsimd
        def _(e):
            pool.run(e)

        @block.vector
        def _(e):
            dve.run(e)

        @block.scalar
        def _(e):
            sca.run(e)

        @block.tensor
        def _(e):
            pe.run(e)


_INS = ["x", "p", "ffn1_pre_g", "ffn1_w_gate", "ffn1_w_up", "ffn1_w_down", "ffn1_post_g", "mix_pre_g", "w_in",
        "sgu_norm_g", "sgu_w", "sgu_b", "pool_w", "pool_scale", "w_out_a", "w_out_b", "w_o", "mix_post_g", "ffn2_pre_g",
        "ffn2_w_gate", "ffn2_w_up", "ffn2_w_down", "ffn2_post_g", "ple_pre_g", "ple_w_gate", "ple_w_proj",
        "ple_post_g", "p_2", "norm_mix_2", "w_in_2", "conv_w_2", "conv_b_2", "cmp_pe_2", "cmp_w1_2", "cmp_w2_2",
        "w_out_2", "w_ple_gate_2", "w_ple_proj_2", "norm_final_2"]
_OUTS = [((1, 512, 1024), "float32")]


def kernel(**inputs):
    import numpy as _np
    import concourse.bacc as _bacc
    from concourse import mybir as _mybir
    from concourse.bass_utils import run_bass_kernel_spmd as _run

    nc = _bacc.Bacc("TRN2", target_bir_lowering=False, num_devices=1)
    arrays, args = {}, {}
    for name in _INS:
        v = _np.ascontiguousarray(inputs[name])
        arrays[f"in_{name}_dram"] = v
        args[name] = nc.dram_tensor(f"in_{name}_dram", v.shape, _mybir.dt.from_np(v.dtype), kind="ExternalInput").ap()
    outs = []
    for i, (shape, dtype) in enumerate(_OUTS):
        dt = _mybir.dt.from_np(_np.dtype(dtype))
        outs.append(nc.dram_tensor(f"out_{i}_dram", shape, dt, kind="ExternalOutput").ap())
    two_blocks(nc, args, outs[0])
    r = _run(nc, [arrays], core_ids=[0])
    return r.results[0]["out_0_dram"]
```

```python
from contextlib import ExitStack

import concourse.bass as bass
from concourse import mybir

F32 = mybir.dt.float32
F32R = mybir.dt.float32r
BF16 = mybir.dt.bfloat16
ALU = mybir.AluOpType
ACT = mybir.ActivationFunctionType
AX = mybir.AxisListType.X

T = 512
D = 1024
KD = D // 128
NEG = -1.0e30
EPS = 1e-6
NRAW = 3
NSPLIT = 3
AHEAD = 2

COLS = [("ffn1_pre_g", 8), ("ffn1_post_g", 8), ("mix_pre_g", 8), ("sgu_norm_g", 8), ("pool_scale", 8),
        ("mix_post_g", 8), ("ffn2_pre_g", 8), ("ffn2_post_g", 8), ("ple_pre_g", 8), ("ple_post_g", 8),
        ("norm_mix_2", 8), ("norm_final_2", 8), ("conv_w_2", 6), ("conv_b_2", 2)]


class Queue:

    def __init__(self, sem):
        self.sem, self.count, self.items, self.met = sem, 0, [], {}

    def put(self, make, *after, inc=True):
        waits = []
        for tok in flat(after):
            key = tok[0].name
            if self.met.get(key, 0) < tok[1]:
                self.met[key] = tok[1]
                waits.append(tok)
        self.items.append((waits, make, self.sem if inc else None))
        if inc:
            self.count += 1
            return (self.sem, self.count)
        return None

    def run(self, eng):
        for waits, make, sem in self.items:
            for s, v in waits:
                eng.wait_ge(s, v)
            ins = make(eng)
            if sem is not None:
                ins.then_inc(sem, 1)


def flat(toks):
    for t in toks:
        if t is None:
            continue
        if isinstance(t, list):
            yield from flat(t)
        else:
            yield t


def now(*toks):
    last = {}
    for s, v in flat(toks):
        if s.name not in last or last[s.name][1] < v:
            last[s.name] = (s, v)
    return list(last.values())


class Ring:

    def __init__(self, aps):
        self.aps, self.free, self.at = aps, [[] for _ in aps], 0

    def take(self):
        i = self.at % len(self.aps)
        self.at += 1
        return i, self.aps[i], self.free[i]


class Operand:

    def __init__(self, hi, lo, first=0):
        self.hi, self.lo, self.first = hi, lo, first
        n = hi.shape[1]
        self.ready = [[] for _ in range(n)]
        self.early = [[] for _ in range(n)]
        self.war = [[] for _ in range(n)]


def two_blocks(nc, a, out):
    ctx = ExitStack()
    with ctx:
        def sem(name):
            return ctx.enter_context(nc.semaphore(name))

        base, top = 16512, 229344
        place = {"at": base}

        def at(name, shape, dt, offset):
            return nc.alloc_sbuf_tensor_at(name, shape, dt, offset=offset)

        def sb(name, shape, dt):
            n = 1
            for s in shape[1:]:
                n *= s
            n *= 2 if dt == BF16 else 4
            o = place["at"]
            place["at"] = o + (n + 31) // 32 * 32
            assert place["at"] <= top, (name, place["at"] - top)
            return at(name, shape, dt, o), o

        h, _ = sb("h", [128, KD, T], F32)
        xh, _ = sb("xh", [128, KD, T], F32R)
        xl, _ = sb("xl", [128, KD, T], F32R)
        ah, ah_o = sb("ah", [128, KD, T], F32R)
        al, al_o = sb("al", [128, KD, T], F32R)
        bh, bh_o = sb("bh", [128, KD, T], F32R)
        bl, bl_o = sb("bl", [128, KD, T], F32R)
        f, f_o = sb("f", [128, KD, T], F32)
        raw, _ = sb("raw", [128, NRAW, 1024], F32)
        whi, _ = sb("whi", [128, NSPLIT, 1024], F32R)
        wlo, _ = sb("wlo", [128, NSPLIT, 1024], F32R)
        act_t, _ = sb("act_t", [128, 4, T], F32)
        tmp_t, _ = sb("tmp_t", [128, 4, T], F32)
        sq_t, _ = sb("sq_t", [128, 2, T], F32)
        rpre, _ = sb("rpre", [128, T], F32)
        rtok, _ = sb("rtok", [128, 4], F32)
        m_o = place["at"]
        place["at"] += 12 * 1024
        vnt, _ = sb("vnt", [128, 4, 256], F32)
        ident, _ = sb("ident", [128, 128], F32)
        identb, _ = sb("identb", [128, 128], BF16)
        ones, _ = sb("ones", [128, 128], F32)
        cols, _ = sb("cols", [128, 104], F32)
        half, _ = sb("half", [128, 16], F32)
        mcaus, _ = sb("mcaus", [128, 128], BF16)
        mband, _ = sb("mband", [128, 2, 128], BF16)
        md4, _ = sb("md4", [128, 2, 128], BF16)
        md16, _ = sb("md16", [128, 2, 128], BF16)
        mcmp, _ = sb("mcmp", [128, 4, 31], F32)
        eps, _ = sb("eps", [128, 1], F32)
        inv, _ = sb("inv", [128, 16], F32)
        gates, _ = sb("gates", [128, 4, 18], F32)
        mv, _ = sb("mv", [128, 4, 2], F32)
        bnst, _ = sb("bnst", [128, 4, 2, 6], F32)
        lnr, _ = sb("lnr", [128, 4], F32)
        poolw = at("poolw", [128, 4, 2, 256], F32, m_o)
        wst = at("wst", [128, 4, 128], F32, m_o + 8192)
        sgub = at("sgub", [128, 4, 128], F32, m_o + 10240)
        scr = at("scr", [128, 2, T], F32, bl_o)
        emb = at("emb", [128, 4, T], F32, ah_o)
        wsr = at("wsr", [128, 4, 128], F32, bh_o)
        vtok = f[:, :, :].rearrange("p k t -> p (k t)").rearrange("p (i c) -> p i c", i=4)
        cpad = at("cpad", [128, 4, 528], F32, f_o)
        csum = at("csum", [128, 2, 528], F32, f_o + 8448)
        diff = at("diff", [128, KD, T], F32, bl_o)
        prow = at("prow", [128, 4, 256], F32, bh_o + 6 * 2048)
        qn = at("qn", [128, 3, T], F32, bh_o)
        kvn = at("kvn", [128, 4, T], F32, bh_o + 6144)
        dq = at("dq", [128, 3, T], F32, bh_o + 14336)
        dk = at("dk", [128, 3, T], F32, bh_o + 20480)
        cab = at("cab", [128, 2, T], F32, bh_o + 14336)
        cac = at("cac", [128, 2, T], F32, bh_o + 18432)
        ccv = at("ccv", [128, 2, T], F32, bh_o + 22528)
        blk = at("blk", [128, 31, 32], F32, bh_o + 26624)
        pcmp = at("pcmp", [128, 24, 32], F32, bh_o + 26624)
        vcs = at("vcs", [31, 128], F32, bh_o + 26624 + 4096)
        kcs = at("kcs", [128, 32], F32, bh_o + 26624 + 4608)
        hcs = at("hcs", [128, 32], F32, bh_o + 26624 + 4736)
        pes = at("pes", [128, 2, 32], F32, bh_o + 26624 + 4864)
        pcs = at("pcs", [128, 3, 24], F32, bh_o + 26624 + 5120)
        w2s = at("w2s", [128, 2, 64], F32, bh_o + 26624 + 5408)
        dv = at("dv", [128, 4, 384], F32, ah_o)
        odil = at("odil", [128, 3, T], F32, m_o)
        nz = at("nz", [128, 3, T], F32, m_o + 6144)
        ptr = at("ptr", [128, 3, T], F32, f_o)
        prb = at("prb", [128, 4, T], F32, f_o + 6144)
        stat = at("stat", [128, 256], F32, f_o + 14336)
        w1s = at("w1s", [128, 2, 32, 64], F32, al_o)
        perow = at("perow", [32, 2, 2, 64], F32, ah_o + 8192)

        G = [ctx.enter_context(nc.psum_tensor(f"G{i}", [128, T], F32)) for i in range(4)]
        X = [ctx.enter_context(nc.psum_tensor(f"X{i}", [128, T], F32)) for i in range(4)]
        gfree = [[] for _ in range(4)]
        xfree = [[] for _ in range(4)]

        pe, dve, sca, pool, sp = (Queue(sem(n)) for n in ("s_pe", "s_dve", "s_act", "s_pool", "s_sp"))
        raw_sem = [sem(f"s_raw{i}") for i in range(NRAW)]
        s_out = sem("s_out")
        n_sem = [0]

        def load(q, dst, src, *after):
            n_sem[0] += 1
            s = sem(f"s_ld{n_sem[0]}")
            q.put(lambda e: e.dma_start(dst, src).then_inc(s, 16), *after, inc=False)
            return (s, 16)

        def mm(o, lhs, rhs, start, stop, *after, inc=False):
            return pe.put(lambda e: e.matmul(o, lhs, rhs, start=start, stop=stop), *after, inc=inc)

        def tr(o, i, idn, *after, inc=False):
            return pe.put(lambda e: e.transpose(o, i, idn), *after, inc=inc)

        def act(o, i, fn, *after, **kw):
            return sca.put(lambda e: e.activation(o, i, fn, **kw), *after)

        def copy(q, o, i, *after):
            if q is sca:
                return act(o, i, ACT.Copy, *after)
            return q.put(lambda e: e.tensor_copy(o, i), *after)

        def tt(q, o, i0, i1, op, *after):
            return q.put(lambda e: e.tensor_tensor(o, i0, i1, op), *after)

        def stt(o, i0, s, i1, op0, op1, *after):
            return dve.put(lambda e: e.scalar_tensor_tensor(o, i0, s, i1, op0, op1), *after)

        def ts(q, o, i, s1, s2, op0, op1, *after):
            if s2 is None:
                return q.put(lambda e: e.tensor_scalar(o, i, s1, None, op0), *after)
            return q.put(lambda e: e.tensor_scalar(o, i, s1, s2, op0, op1), *after)

        def red(o, i, op, *after, **kw):
            return dve.put(lambda e: e.tensor_reduce(o, i, AX, op, **kw), *after)

        def rec(o, i, *after):
            return dve.put(lambda e: e.reciprocal(o, i), *after)

        acts = Ring([act_t[:, i, :] for i in range(4)])
        tmps = Ring([tmp_t[:, i, :] for i in range(4)])
        sqs = Ring([sq_t[:, i, :] for i in range(2)])

        units = []
        split_done, pe_done = [], []
        sent = [0]
        raw_count = [0] * NRAW
        raw_tok = []

        def add_units(pieces_of, nk, wid):
            first = len(units)
            for k0 in range(0, nk, 2):
                units.append((pieces_of(k0, min(2, nk - k0)), min(2, nk - k0), wid))
            return (first, nk, wid)

        def plain(w, parts, row0=0):
            def pieces(k0, n):
                o, got = 0, []
                for c0, c1 in parts:
                    src = w[row0 + k0 * 128:row0 + (k0 + n) * 128, c0:c1].rearrange("(k p) c -> p k c", p=128)
                    got.append((0, 128, 0, n, o, c1 - c0, src))
                    o += c1 - c0
                return got
            return pieces

        def send(j):
            pieces, nk, wid = units[j]
            s = j % NRAW
            after = split_done[j - NRAW] if j >= NRAW else []
            v = raw[:, s, 0:nk * wid].rearrange("p (k c) -> p k c", k=nk)
            for p0, p1, k0, n, o, c, src in pieces:
                dst = v[p0:p1, k0:k0 + n, o:o + c] if o is not None else c(v[p0:p1, k0])
                sp.put(lambda e, dst=dst, src=src: e.dma_start(dst, src).then_inc(raw_sem[s], 16), after, inc=False)
                raw_count[s] += 16
            raw_tok.append((raw_sem[s], raw_count[s]))

        def split(j):
            pieces, nk, wid = units[j]
            n = nk * wid
            r, d = j % NRAW, j % NSPLIT
            used = pe_done[j - NSPLIT] if j >= NSPLIT else None
            hi = act(whi[:, d, 0:n], raw[:, r, 0:n], ACT.Copy, raw_tok[j], used)
            split_done.append([hi])
            lows.append((j, wlo[:, d, 0:n], raw[:, r, 0:n], whi[:, d, 0:n].bitcast(F32), [hi, raw_tok[j], used]))

        lows = []

        def low_parts():
            while lows:
                j, o, w, hi, after = lows.pop(0)
                split_done[j].append(tt(dve, o, w, hi, ALU.subtract, after))

        reach = [0]

        def ahead(n):
            low_parts()
            while len(split_done) <= min(n + reach[0], len(units) - 1):
                while sent[0] <= min(len(split_done) + NRAW - 1, len(units) - 1):
                    low_parts()
                    send(sent[0])
                    sent[0] += 1
                split(len(split_done))

        background = []

        def pump():
            while background:
                try:
                    next(background[0])
                    return
                except StopIteration:
                    background.pop(0)

        def drain_background():
            while background:
                pump()

        def gemm(group, x, tiles, by_token=False, order=None, pumps=(), hooks=None, ks=None):
            first, nk, wid = group
            done = [None] * tiles
            order = order or list(range(tiles))
            for u in range(0, nk, 2):
                n = first + u // 2
                ahead(n)
                if lows and lows[0][0] <= n:
                    low_parts()
                d = n % NSPLIT
                kn = min(2, nk - u)
                tok = None
                for ti, m in enumerate(order):
                    for kk in range(kn):
                        k = ks[u + kk] if ks else u + kk
                        wv = [w[:, d, kk * wid:(kk + 1) * wid] for w in (whi, wlo)]
                        xv = [v[:, x.first + k, :] for v in (x.hi, x.lo)]
                        for wi, xi in ((0, 0), (1, 0), (0, 1)):
                            if by_token:
                                o, lhs, rhs = G[m][:, 0:wid], xv[xi][:, m * 128:(m + 1) * 128], wv[wi]
                            else:
                                lhs = wv[wi][:, m * 128:(m + 1) * 128]
                                o, rhs = G[m][:, :], xv[xi]
                            s, e = u + kk == 0 and wi + xi == 0, u + kk == nk - 1 and xi == 1
                            inc = (kk == kn - 1 and xi == 1) and (u + kk == nk - 1 or ti == tiles - 1)
                            tok = mm(o, lhs, rhs, s, e, split_done[n], (x.ready if xi else x.early)[x.first + k],
                                     gfree[m] if s else None, inc=inc)
                            if e:
                                done[m] = tok
                    low_parts()
                    if ti in pumps:
                        pump()
                    if hooks and (u, ti) in hooks:
                        hooks[u, ti]()
                pe_done.append(tok)
            for k in range(nk):
                x.war[x.first + k] = [pe_done[-1]]
            return done

        at_bank = [0]

        def gemm_tile(n):
            b = at_bank[0] % 2
            at_bank[0] += 1
            ahead(n)
            d = n % NSPLIT
            for k in range(KD):
                for wi, xi in ((0, 0), (1, 0), (0, 1)):
                    w, x = (whi, wlo)[wi][:, d, k * 128:(k + 1) * 128], (XO.hi, XO.lo)[xi][:, k, :]
                    s, e = k == 0 and wi + xi == 0, k == KD - 1 and xi == 1
                    t = mm(G[b][:, :], w, x, s, e, split_done[n], (XO.ready if xi else XO.early)[k],
                           gfree[b] if s else None, inc=e)
                if k % 2:
                    pump()
                if k == 3:
                    low_parts()
            pe_done.append(t)
            for k in range(KD):
                XO.war[k] = [t]
            return b, t

        def split_tile(i, t, tok, x, k):
            hi = act(x.hi[:, k, :], t, ACT.Copy, tok, x.war[k])
            lo = tt(dve, x.lo[:, k, :], t, x.hi[:, k, :].bitcast(F32), ALU.subtract, hi, x.war[k])
            x.early[k], x.ready[k] = [hi], [hi, lo]
            if i is not None:
                tmps.free[i] = [lo]

        XO, AO, BO = Operand(xh, xl), Operand(ah, al), Operand(bh, bl)
        PO = Operand(bh, bl, 4)

        A = a
        plan = {}

        def ffn_units(name, wg, wu, wd):
            for hf, (g0, g1) in enumerate(((0, 6), (6, 11))):
                for g in range(g0, g1):
                    c = g * 256

                    def pieces(k0, n, c=c):
                        return [(0, 128, 0, n, o, 256,
                                 w[k0 * 128:(k0 + n) * 128, c:c + 256].rearrange("(k p) c -> p k c", p=128))
                                for o, w in ((0, wg), (256, wu))]
                    plan[name, "gu", g] = add_units(pieces, KD, 512)
                for c in range(2):
                    plan[name, "dn", hf, c] = add_units(plain(wd, [(c * 512, c * 512 + 512)], g0 * 256),
                                                        2 * (g1 - g0), 512)

        def two(name, w, nk, c0=0):
            for c in range(2):
                plan[name, c] = add_units(plain(w, [(c0 + c * 512, c0 + c * 512 + 512)]), nk, 512)

        def inter(names):
            for c in range(2):
                for name, w, nk, c0 in names:
                    plan[name, c] = add_units(plain(w, [(c0 + c * 512, c0 + c * 512 + 512)]), nk, 512)

        ffn_units("ffn1", A["ffn1_w_gate"][0], A["ffn1_w_up"][0], A["ffn1_w_down"][0])
        win = A["w_in"][0]
        two("v", win, KD, D)
        two("u", win, KD, 0)
        two("c", win, KD, 2 * D)
        inter([("ga", win, KD, 3 * D), ("oa", A["w_out_a"][0], KD, 0)])
        inter([("gb", win, KD, 4 * D), ("ob", A["w_out_b"][0], KD, 0)])
        two("wo", A["w_o"][0], KD)
        ffn_units("ffn2", A["ffn2_w_gate"][0], A["ffn2_w_up"][0], A["ffn2_w_down"][0])
        for name, c in (("pp", 0), ("pg", 0), ("pg", 1), ("pp", 1)):
            w, nk = (A["ple_w_proj"][0], 2) if name == "pp" else (A["ple_w_gate"][0], KD)
            plan[name, c] = add_units(plain(w, [(c * 512, c * 512 + 512)]), nk, 512)
        w2 = A["w_in_2"][0]

        for name, parts in (("dv", [(3346, 3730)]), ("dq", [(2578, 2962)]), ("dk", [(2962, 3346)]),
                            ("vg", [(1792, 1920), (2048, 2194)])):
            plan[name] = add_units(plain(w2, parts), KD, sum(c1 - c0 for c0, c1 in parts))

        def column(*parts):
            o, got = 0, []
            for c0, c1 in parts:
                got.append((0, 128, 0, KD, o, c1 - c0, w2[:, c0:c1].rearrange("(k p) c -> p k c", p=128)))
                o += c1 - c0
            units.append((got, KD, 128))
            return len(units) - 1

        def pair_column(c0, r_):
            return column(*[(c0 + 192 * g + 64 * r_, c0 + 192 * g + 64 * r_ + 64) for g in range(2)])

        tiles_in = [(("q", r_), pair_column(1024, r_)) for r_ in range(3)]
        tiles_in += [(("kv", n), column((c, c + 128))) for n, c in enumerate((1408, 1536, 1664, 1920))]
        tiles_in += [(("nz", r_), pair_column(2194, r_)) for r_ in range(3)]
        tiles_in += [((n, m), column((c + 128 * m, c + 128 * m + 128))) for n, c in (("b", 0), ("c", 256))
                     for m in range(2)]
        tiles_in += [((n, m), column((c + 128 * m, c + 128 * m + 128))) for m in range(2)
                     for n, c in (("h", 512), ("z", 768))]
        tiles_in += [(("dz", m), column((3730 + 128 * m, 3858 + 128 * m))) for m in range(3)]
        wout2 = A["w_out_2"][0]

        out2_k = [0, 1, 2, 3, 5, 6, 7, 4]

        def wout_pieces(c0):
            def rows(p0, p1, k, r0):
                return (p0, p1, k, 1, 0, 512, wout2[r0:r0 + p1 - p0, c0:c0 + 512].rearrange("p (k c) -> p k c", k=1))

            def pieces(k0, n):
                got = []
                for i, k in enumerate(out2_k[k0:k0 + n]):
                    if 2 <= k < 5:
                        got += [rows(64 * g, 64 * g + 64, i, 256 + 192 * g + 64 * (k - 2)) for g in range(2)]
                    else:
                        got.append(rows(0, 128, i, k * 128))
                return got
            return pieces

        for c in range(2):
            plan["out2", c] = add_units(wout_pieces(c * 512), KD, 512)
        inter([("pg2", A["w_ple_gate_2"][0], KD, 0), ("pp2", A["w_ple_proj_2"][0], 2, 0)])

        xrow = f[:, :, :].rearrange("p k t -> p (k t)").rearrange("p (i c) -> p i c", i=4)
        grow = tmp_t[0:8, 3, 0:128]
        g_tok = load(sp, grow, A["ffn1_pre_g"][0].rearrange("(a c) -> a c", c=128))
        x_tok = []
        for n in range(4):
            x_tok.append(load(sp, xrow[:, :, n * 256:(n + 1) * 256],
                              A["x"][0].rearrange("(i p) c -> p i c", p=128)[:, :, n * 256:(n + 1) * 256]))
            if n < 3:
                send(n)
                sent[0] += 1
        colat, r = {}, 0
        for name, n in COLS:
            colat[name] = r
            r += n

        def col(name, m):
            return cols[:, colat[name] + m:colat[name] + m + 1]

        k1 = pool.put(lambda e: e.memset(ident[:, :], 0.0))
        k_id = pool.put(lambda e: e.affine_select(out=ident[:, :], in_=ident[:, :], compare_op=ALU.not_equal, fill=1.0,
                                                  base=0, pattern=[[-1, 128]], channel_multiplier=1), k1)
        k_ones = pool.put(lambda e: e.memset(ones[:, :], 1.0))
        k_eps = pool.put(lambda e: e.memset(eps[:, :], EPS))
        k_g = tr(X[2][:, 0:8], grow, ident[0:8, 0:8], g_tok, k_id, inc=True)
        k_cols = copy(dve, cols[:, 0:8], X[2][:, 0:8], k_g)
        xfree[2] = [k_cols]
        tmps.free[3] = [k_g]

        def lo(k):
            XO.ready[k] = [stt(XO.lo[:, k, :], h[:, k, :], col("ffn1_pre_g", k), XO.hi[:, k, :].bitcast(F32), ALU.mult,
                               ALU.subtract, XO.early[k])]

        h_tok = [None] * KD
        f_tok = [None] * KD

        def refill():
            low_parts()
            while sent[0] < len(split_done) + NRAW:
                send(sent[0])
                sent[0] += 1

        def turn(k):
            b = k % 2
            for i in range(4):
                t = tr(X[b][:, i * 128:(i + 1) * 128], xrow[:, i, k * 128:(k + 1) * 128], ident[:, :],
                       x_tok[k // 2], k_id, xfree[b], inc=(i == 3))
            h_tok[k] = copy(dve, h[:, k, :], X[b][:, :], t)
            xfree[b] = [h_tok[k]]
            XO.early[k] = [act(XO.hi[:, k, :], h[:, k, :], ACT.Copy, h_tok[k], k_cols, scale=col("ffn1_pre_g", k))]
            f_tok[:] = [[t] for _ in range(KD)]

        for k in range(4):
            turn(k)
            if k:
                lo(k - 1)
            if k in (1, 3):
                split(len(split_done))
            if k == 2:
                refill()
        lo(3)
        refill()

        hs = [h[:, m, :] for m in range(KD)]
        fs = [f[:, m, :] for m in range(KD)]

        def sqrt_soon():
            act(lnr[:, 0:1], eps[:, 0:1], ACT.Sqrt, k_eps)

        class Sums:

            def __init__(self):
                self.first, self.acc, self.k_acc = True, None, None

            def gather(self, tile, tok):
                if self.acc is None:
                    self.ai, self.acc, fr = acts.take()
                    self.k_acc = act(self.acc, tile, ACT.Square, tok, fr)
                    return
                i, s, fr = sqs.take()
                k = act(s, tile, ACT.Square, tok, fr)
                self.k_acc = tt(pool, self.acc, self.acc, s, ALU.add, k, self.k_acc)
                sqs.free[i] = [self.k_acc]

            def gathered(self, last=False):
                acts.free[self.ai] = [self.total(self.acc, self.k_acc, last)]

            def add(self, tile, tok, last=False, ring=sqs):
                i, s, fr = ring.take()
                ring.free[i] = [self.total(s, act(s, tile, ACT.Square, tok, fr), last)]

            def total(self, s, k, last):
                for i in range(4):
                    self.t = mm(X[0][:, i:i + 1], s[:, i * 128:(i + 1) * 128], ones[:, 0:1], self.first and i == 0,
                                last and i == 3, k, k_ones, xfree[0] if self.first else None, inc=(i == 3))
                self.first = False
                return self.t

            def factor(self):
                k = act(rtok[:, :], X[0][:, 0:4], ACT.Sqrt, self.t, k_eps, rtok_free[0], bias=eps[:, 0:1],
                        scale=1.0 / D)
                xfree[0] = [k]
                self.rt = rec(rtok[:, :], rtok[:, :], k)
                rtok_free[0] = [self.rt]

            def diagonal(self):
                self.si, self.s, fr = sqs.take()
                self.dg = []
                for i in range(4):
                    o, r = self.s[:, i * 128:(i + 1) * 128], rtok[:, i:i + 1]
                    if i % 2:
                        self.dg.append(act(o, ident[:, :], ACT.Copy, self.rt, fr, scale=r))
                    else:
                        self.dg.append(ts(dve, o, ident[:, :], r, None, ALU.mult, None, self.rt, fr))
                rtok_free[0] = now(self.dg)

            def spread(self):
                for i in range(4):
                    t = mm(X[1][:, i * 128:(i + 1) * 128], ones[:, :], self.s[:, i * 128:(i + 1) * 128], True, True,
                           self.dg[i], xfree[1], inc=(i == 3))
                sqs.free[self.si] = [t]
                return t

        rtok_free = [None]

        class Stats(Sums):

            def tile(self, m):
                self.gather(hs[m], h_tok[m])

            def hooks(self):
                def last():
                    self.gathered(True)
                    self.factor()
                    self.diagonal()

                def end():
                    t = self.spread()
                    self.k = copy(dve, rpre[:, :], X[1][:, :], t)
                    xfree[1] = [self.k]
                return {(6, 0): last, (6, 2): end}

        def operand_hi(m, gain, tok):
            XO.early[m] = [act(XO.hi[:, m, :], hs[m], ACT.Copy, tok, k_cols, XO.war[m], scale=gain)]

        def operand_lo(m, gain):
            k = stt(XO.lo[:, m, :], hs[m], gain, XO.hi[:, m, :].bitcast(F32), ALU.mult, ALU.subtract, XO.early[m],
                    XO.war[m])
            XO.ready[m] = [k]

        class First(Stats):

            def pair(self, k):
                turn(k)
                turn(k + 1)
                lo(k)
                split(len(split_done))
                lo(k + 1)
                refill()
                for m in range(4) if k == 4 else range(4, KD):
                    self.tile(m)

            def all(self):
                self.pair(6)
                reach[0] = AHEAD

            def hooks(self):
                return {(0, 0): lambda: self.pair(4), (2, 1): self.all, **Stats.hooks(self)}

        class Post(Sums):

            def __init__(self):
                Sums.__init__(self)
                self.toks = [None] * KD
                self.between = lambda: None
                self.k = None

            def tile(self, j, tok):
                self.toks[j] = tok
                if j < 4:
                    self.gather(fs[j], tok)
                else:
                    self.add(fs[j], tok, j == KD - 1, sqs if j < 6 else acts)

            def hooks(self):
                return {(6, 0): self.gathered}

            def factors(self):
                self.factor()
                self.diagonal()

            def along(self):
                self.k = self.spread()

            def end(self, gain, then):
                if self.k is None:
                    self.factors()
                    self.along()
                k = self.k
                st = Stats()
                for m in range(KD):
                    s = stt(fs[m], fs[m], gain(m), X[1][:, :], ALU.mult, ALU.mult, k, self.toks[m], k_half)
                    h_tok[m] = tt(dve, hs[m], hs[m], fs[m], ALU.add, s, h_tok[m])
                    f_tok[m] = [h_tok[m]]
                    operand_hi(m, col(then, m), h_tok[m])
                    st.tile(m)
                    if m == 0:
                        self.between()
                    if m:
                        operand_lo(m - 1, col(then, m - 1))
                    if m == 4:
                        ahead(len(split_done) - AHEAD)
                    if m == 5:
                        low_parts()
                operand_lo(KD - 1, col(then, KD - 1))
                xfree[1] = [s]
                return st

        def ffn(name, st, post_n, then, pumps=(), fill=None):
            hid = lambda i: (AO, i) if i < 8 else (BO, i - 8)
            toks = [None] * KD
            post = Post()
            for hf, (g0, g1) in enumerate(((0, 6), (6, 11))):
                for g in range(g0, g1):
                    done = gemm(plan[name, "gu", g], XO, 4, order=[0, 2, 1, 3], hooks=st.hooks() if g == 0 else None,
                                pumps=pumps if g else ())
                    made = []
                    for p in range(2):
                        si, s, fr = acts.take()
                        k = tt(dve, s, G[p][:, :], rpre[:, :], ALU.mult, st.k, done[p], fr)
                        gfree[p] = [k]
                        k1 = act(s, s, ACT.Silu, k)
                        i, t, fr = tmps.take()
                        k = tt(dve, t, G[2 + p][:, :], rpre[:, :], ALU.mult, done[2 + p], fr)
                        gfree[2 + p] = [k]
                        k = tt(pool, t, t, s, ALU.mult, k1, k)
                        acts.free[si] = [k]
                        made.append((i, t, k))
                    for p, (i, t, k) in enumerate(made):
                        split_tile(i, t, k, *hid(2 * (g - g0) + p))
                nk = 2 * (g1 - g0)
                both = Both(AO, BO, nk)
                for c in range(2):
                    done = gemm(plan[name, "dn", hf, c], both, 4, hooks=post.hooks() if hf and c else None)
                    if hf and c:
                        sqrt_soon()
                    def take(m, hf=hf, c=c, done=done):
                        j = 4 * c + m
                        if hf == 0:
                            toks[j] = act(fs[j], G[m][:, :], ACT.Copy, done[m], f_tok[j])
                        else:
                            toks[j] = tt(dve, fs[j], G[m][:, :], fs[j], ALU.add, done[m], toks[j])
                        gfree[m] = [toks[j]]
                        if hf:
                            post.tile(j, toks[j])
                    if fill and hf and c:
                        fill(take, post)
                    else:
                        for m in range(4):
                            take(m)
                both.close()
            return post.end(lambda m: half[:, 8 * post_n + m:8 * post_n + m + 1], then)

        class Both:

            def __init__(self, p, q, n):
                self.p, self.q, self.n, self.first = p, q, n, 0
                self.early, self.ready = p.early + q.early, p.ready + q.ready
                self.war = [None] * 16
                self.hi, self.lo = Pair(p.hi, q.hi), Pair(p.lo, q.lo)

            def close(self):
                for k in range(self.n):
                    (self.p if k < 8 else self.q).war[k % 8] = self.war[k]

        class Pair:
            def __init__(self, p, q):
                self.p, self.q = p, q

            def __getitem__(self, at):
                return self.p[at] if at[1] < 8 else self.q[:, at[1] - 8, :]

        k_idb = k_inv = k_mc = k_mb = k_md = k_cm = k_half = k_wst = sgb_t = pw_t = None

        def prepare():
            nonlocal k_idb, k_inv, k_mc, k_mb, k_md, k_cm, k_half, k_wst, sgb_t, pw_t, k_cols
            ti, rows, fr = tmps.take()
            g_toks = []
            for name, n in COLS:
                src = A[name][0].rearrange("k (a c) -> (k a) c", c=128) if name == "conv_w_2" else \
                    (A[name] if name == "norm_final_2" else A[name][0]).rearrange("(a c) -> a c", c=128)
                g_toks.append(load(sp, rows[colat[name]:colat[name] + n, 0:128], src, fr))
            ws_t = load(pool, wsr[:, :, :], A["sgu_w"][0].rearrange("g t s -> t g s"))
            sgb_t = load(pool, sgub[:, :, :].rearrange("p g t -> p (g t)"),
                         A["sgu_b"].rearrange("a g t -> a (g t)").partition_broadcast(128))
            pw_t = load(pool, poolw[:, :, :, :], A["pool_w"][0].rearrange("g (k p) d -> p g k d", p=128))
            for g in range(4):
                k_ws = pool.put(lambda e, g=g: e.affine_select(out=wsr[:, g, :], in_=wsr[:, g, :], pattern=[[-1, 128]],
                                                               channel_multiplier=1, compare_op=ALU.is_ge, fill=0.0,
                                                               base=0), ws_t)
            k_idb = copy(pool, identb[:, :], ident[:, :], k_id)
            for t in range(15):
                k_inv = pool.put(lambda e, t=t: e.memset(inv[:, t:t + 1], 1.0 / (t + 1)))
            yield
            yield
            yield
            k_g = tr(X[2][:, 0:104], rows[0:104, 0:128], ident[0:104, 0:104], g_toks, xfree[2], inc=True)
            k_cols = copy(dve, cols[:, :], X[2][:, 0:104], k_g)
            xfree[2] = [k_cols]
            tmps.free[ti] = [k_g]
            k_half = [ts(dve, half[:, 8 * n:8 * n + 8], cols[:, colat[w]:colat[w] + 8], 0.5, None, ALU.mult, None,
                         k_cols) for n, w in enumerate(("ffn1_post_g", "ffn2_post_g"))]
            yield
            for g in range(4):
                t = tr(X[2][:, g * 128:(g + 1) * 128], wsr[:, g, :], ident[:, :], k_ws, xfree[2], inc=(g == 3))
            k_wst = copy(dve, wst[:, :, :].rearrange("p g s -> p (g s)"), X[2][:, :], t)
            xfree[2] = [k_wst]
            yield
            zero = scr[:, 0, 0:128]
            k_z = pool.put(lambda e: e.memset(zero, 0.0))
            keep = dict(compare_op=ALU.is_ge, fill=NEG, base=0)
            k_mc = pool.put(lambda e: e.affine_select(out=mcaus[:, :], in_=zero, pattern=[[-1, 128]],
                                                      channel_multiplier=1, **keep), k_z)
            k_mb = pool.put(lambda e: e.affine_select(out=mband[:, 0, :], in_=zero, pattern=[[1, 128]],
                                                      channel_multiplier=-1, **keep), k_z)
            k_mb = copy(pool, mband[:, 1, :], mcaus[:, :], k_mc)
            zc = scr[:, 0, 0:124].rearrange("p (i n) -> p i n", i=4)
            k_cm = pool.put(lambda e: e.affine_select(out=mcmp[:, :, :], in_=zc, pattern=[[128, 4], [-16, 31]],
                                                      channel_multiplier=1, compare_op=ALU.is_ge, fill=NEG, base=-31), k_z)
            k_oh, k_md = [], []
            for n, d in enumerate((4, 16)):
                o = scr[0:d, 1, n * 128:n * 128 + 128].rearrange("p (a b) -> p a b", b=d)
                k = pool.put(lambda e, o=o: e.memset(o, 0.0))
                k_oh.append(pool.put(lambda e, o=o, d=d: e.affine_select(
                    out=o, in_=o, compare_op=ALU.not_equal, fill=1.0, base=0, pattern=[[0, 128 // d], [1, d]],
                    channel_multiplier=-1), k))
            yield
            yield
            for n, (d, md) in enumerate(((4, md4), (16, md16))):
                oh = scr[0:d, 1, n * 128:n * 128 + 128]
                kp = mm(X[3][:, n * 128:n * 128 + 128], oh, oh, True, True, k_oh[n], xfree[3], inc=True)
                mt = scr[:, 0, 128 + n * 128:256 + n * 128]
                kd = ts(dve, mt, X[3][:, n * 128:n * 128 + 128], -1.0, -NEG, ALU.add, ALU.mult, kp)
                copy(pool, md[:, 0, :], mt, kd)
                k_md.append(pool.put(lambda e, md=md, mt=mt: e.affine_select(
                    out=md[:, 1, :], in_=mt, pattern=[[-1, 128]], channel_multiplier=1, **keep), kd))
                xfree[3] = [kd]
            for k in range(4):
                BO.war[k] = now(t, k_md, k_cm, kp)
            yield

        background.append(prepare())
        st = ffn("ffn1", First(), 0, "mix_pre_g", pumps=(3,))

        k_ln = [None] * 4
        v_tok = [[None, None] for _ in range(4)]
        for c in range(2):
            done = gemm(plan["v", c], XO, 4, by_token=True, hooks=st.hooks() if c == 0 else None)
            for i in range(4):
                v = vtok[:, i, c * 512:(c + 1) * 512]
                v_tok[i][c] = act(v, G[i][:, :], ACT.Gelu_apprx_tanh, done[i], f_tok, st.rt, scale=rtok[:, i:i + 1])
                gfree[i] = [v_tok[i][c]]
                k_bn = dve.put(lambda e, i=i, c=c, v=v: e.bn_stats(bnst[:, i, c, :], v), v_tok[i][c])
        rtok_free[0] = now(rtok_free, v_tok)
        for i in range(4):
            k_ag = dve.put(lambda e, i=i: e.bn_aggr(mv[:, i, :], bnst[:, i, :, :]), k_bn)
        k = act(lnr[:, :], mv[:, :, 1], ACT.Sqrt, k_ag, k_eps, bias=eps[:, 0:1])
        k_lr = rec(lnr[:, :], lnr[:, :], k)
        for i in range(4):
            k_ln[i] = ts(dve, vtok[:, i, :], vtok[:, i, :], mv[:, i, 0:1], lnr[:, i:i + 1], ALU.subtract, ALU.mult,
                         k_lr, v_tok[i])

        def sgu(j, si, u, k_u):
            b = 1 + j % 2
            for i in range(4):
                t = mm(X[b][:, i * 128:(i + 1) * 128], vtok[:, i, j * 128:(j + 1) * 128], wst[:, j // 2, :],
                       True, True, k_ln, k_wst, xfree[b], inc=(i == 3))
            ti, s, fr = tmps.take()
            bb = sgub[:, j // 2, :].unsqueeze(1).to_broadcast([128, 4, 128])
            k = stt(s.rearrange("p (i t) -> p i t", i=4), X[b][:, :].rearrange("p (i t) -> p i t", i=4),
                    col("sgu_norm_g", j), bb, ALU.mult, ALU.add, t, sgb_t, fr)
            xfree[b] = [k]
            k = tt(pool, s, s, u, ALU.mult, k, k_u)
            acts.free[si] = [k]
            split_tile(ti, s, k, AO, j)
            k_sgu[0] = t
            yield

        k_sgu = [None]
        for c in range(2):
            done = gemm(plan["u", c], XO, 4, pumps=(1, 3))
            drain_background()
            for m in range(4):
                j = 4 * c + m
                si, u, fr = acts.take()
                k = tt(dve, u, G[m][:, :], rpre[:, :], ALU.mult, st.k, done[m], fr)
                gfree[m] = [k]
                background.append(sgu(j, si, u, act(u, u, ACT.Gelu_apprx_tanh, k)))

        def pooled(gi):
            got = []
            for n in range(2):
                for kk in range(2):
                    t = mm(X[2 + n][:, :], poolw[:, gi, kk, n * 128:n * 128 + 128], diff[:, 2 * gi + kk, :], kk == 0,
                           kk == 1, k_diff[2 * gi + kk], pw_t, xfree[2 + n], inc=(kk == 1))
                got.append(t)
            for n in range(2):
                di = 2 * gi + n
                ti, s, fr = tmps.take()
                k = act(s, X[2 + n][:, :], ACT.Copy, got[n], fr, scale=col("pool_scale", di))
                xfree[2 + n] = [k]
                BO.war[di] = now(b_war, t)
                split_tile(ti, s, k, BO, di)
            yield

        b_war = now(BO.war)
        k_diff = [None] * KD
        k_c, k_csum = [None] * 4, [None]
        k_cend = []

        def windows(c):
            for m in range(4):
                j = 4 * c + m
                gi = j // 2
                w = 2 << gi
                lo, src, k = 0, cpad[:, m, :], [k_c[m], k_csum[0]]
                for n in range(gi + 1):
                    dst, sh = csum[:, n % 2, :], 1 << n
                    lo += sh
                    k = [tt(pool, dst[:, lo:528], src[:, lo:528], src[:, lo - sh:528 - sh], ALU.add, k)]
                    src = dst
                yield
                if c:
                    yield
                t = diff[:, j, :]
                k2 = stt(t, src[:, 16:528], 1.0 / w, cpad[:, m, 16:528], ALU.mult, ALU.subtract, k, b_war)
                k3 = tt(dve, src[:, 16:15 + w], src[:, 16:15 + w], inv[:, 0:w - 1], ALU.mult, k2, k_inv)
                k4 = tt(dve, t[:, 0:w - 1], src[:, 16:15 + w], cpad[:, m, 16:15 + w], ALU.subtract, k3)
                k_csum[0] = k_c[m] = k_diff[j] = k4
            if c:
                k_cend.append(k4)
            yield

        for c in range(2):
            done = gemm(plan["c", c], XO, 4, pumps=(1, 3))
            drain_background()
            if c == 0:
                k_pad = pool.put(lambda e: e.memset(cpad[:, :, 0:16], 0.0), k_sgu)
                k_c = [k_pad] * 4
            for m in range(4):
                k_c[m] = tt(dve, cpad[:, m, 16:528], G[m][:, :], rpre[:, :], ALU.mult, st.k, done[m], k_c[m], k_sgu)
                gfree[m] = [k_c[m]]
            background.append(windows(c))
        pools = [pooled(gi) for gi in range(4)]

        y_tok = [None] * KD

        def gated(gname, oname, x, use, st, hooks=({}, {}), soon=False):
            for c in range(2):
                done = gemm(plan[gname, c], XO, 4, pumps=(1, 3), hooks=hooks[c])
                if not pools:
                    drain_background()
                sg = []
                for m in range(4):
                    si, s, fr = acts.take()
                    if st:
                        k = tt(dve, s, G[m][:, :], rpre[:, :], ALU.mult, st.k, done[m], fr)
                        gfree[m] = [k]
                        k = act(s, s, ACT.Sigmoid, k)
                    else:
                        k = act(s, G[m][:, :], ACT.Sigmoid, done[m], fr)
                        gfree[m] = [k]
                    sg.append((si, s, k))
                if pools:
                    background.extend(pools[0:2])
                    del pools[0:2]
                done = None
                if (oname, c) != ("pp", 0):
                    done = gemm(plan[oname, c], x, 4, pumps=(3,))
                drain_background()
                if soon and c == 1:
                    sqrt_soon()
                for m in range(4):
                    si, s, k = sg[m]
                    k = use(4 * c + m, G[m][:, :] if done else None, s, [k, done and done[m]])
                    if done:
                        gfree[m] = [k]
                    acts.free[si] = [k]
                while later:
                    later.pop(0)()

        later = []

        def use_a(j, ps, s, toks):
            y_tok[j] = tt(dve, fs[j], ps, s, ALU.mult, toks, k_cend, k_sgu)
            return y_tok[j]

        def use_b(j, ps, s, toks):
            ti, t, fr = tmps.take()
            k0 = tt(dve, t, ps, s, ALU.mult, toks, fr)
            k = tt(pool, t, t, fs[j], ALU.add, k0, y_tok[j])
            f_tok[j] = [k]
            tmps.free[ti] = None
            later.append(lambda: split_tile(ti, t, k, AO, j))
            return k0

        gated("ga", "oa", AO, use_a, st)
        gated("gb", "ob", BO, use_b, st)
        post = Post()
        for c in range(2):
            done = gemm(plan["wo", c], AO, 4, hooks=post.hooks() if c else None)
            if c:
                sqrt_soon()
            for m in range(4):
                j = 4 * c + m
                k = copy(dve, fs[j], G[m][:, :], done[m], f_tok)
                gfree[m] = [k]
                post.tile(j, k)
        st = post.end(lambda m: col("mix_post_g", m), "ffn2_pre_g")

        def embed(k_p, *after):
            for k in range(2):
                for i in range(4):
                    t = tr(X[3][:, i * 128:(i + 1) * 128], prow[:, i, k * 128:(k + 1) * 128], ident[:, :],
                           k_p, xfree[3], inc=(i == 3))
                ti, s, fr = tmps.take()
                kc = copy(dve, s, X[3][:, :], t, fr)
                xfree[3] = [kc]
                PO.war[4 + k] = now(*after)
                split_tile(ti, s, kc, PO, 4 + k)
                yield
            BO.war[6] = BO.war[7] = [t]

        k_p = load(pool, prow[:, :, :], A["p"][0, 0].rearrange("(i p) c -> p i c", p=128), now(BO.war))
        background.append(embed(k_p, now(BO.war)))
        k_e = [None] * 4

        def project(take, post):
            def rest():
                take(2)
                take(3)
                post.factors()

            take(0)
            take(1)
            done = gemm(plan["pp", 0], PO, 4, hooks={(0, 0): rest, (0, 3): post.along})

            def store_e():
                for m in range(4):
                    k_e[m] = act(emb[:, m, :], G[m][:, :], ACT.Copy, done[m])
                    gfree[m] = [k_e[m]]
            post.between = store_e

        st = ffn("ffn2", st, 1, "ple_pre_g", pumps=(3,), fill=project)
        post = Post()

        def use_p(j, ps, s, tk):
            if ps is None:
                ps = emb[:, j, :]
            k = tt(dve, fs[j], ps, s, ALU.mult, tk, f_tok, k_e)
            post.tile(j, k)
            return k

        gated("pg", "pp", PO, use_p, st, hooks=(st.hooks(), post.hooks()), soon=True)
        AO.war = [now(AO.war, post.toks) for _ in range(KD)]
        st = post.end(lambda m: col("ple_post_g", m), "norm_mix_2")

        k_b2 = now(PO.war, BO.war, AO.war)

        def store(done, dst, *after, scale=None):
            got = []
            for m, d in enumerate(dst):
                got.append(stt(d, G[m][:, :], scale[m] if scale else 1.0, rpre[:, :], ALU.mult, ALU.mult, st.k, done[m],
                               *after))
                gfree[m] = [got[-1]]
            return got

        done = gemm(plan["dv"], XO, 4, by_token=True, hooks=st.hooks())
        k_dv = []
        for i in range(4):
            k_dv.append(act(dv[:, i, :], G[i][:, 0:384], ACT.Copy, done[i], k_b2, st.rt, scale=rtok[:, i:i + 1]))
            gfree[i] = [k_dv[i]]
        k_dq = store(gemm(plan["dq"], XO, 3), [dq[:, m, :] for m in range(3)], k_b2,
                     scale=[0.125] * 3)
        k_dk = store(gemm(plan["dk"], XO, 3), [dk[:, m, :] for m in range(3)], k_b2)

        ptrs = Ring([ptr[:, i, :] for i in range(3)])
        prbs = Ring([prb[:, i, :] for i in range(4)])
        for r_ in (ptrs, prbs):
            r_.free = [now(f_tok) for _ in r_.aps]
        n_stat = [0]
        k_stat = [pool.put(lambda e: e.memset(stat[:, :], 0.0), f_tok)]

        def stats(n):
            o = n_stat[0]
            n_stat[0] += n
            assert o + n <= 256
            return stat[:, o:o + n]

        class Bank:
            def __init__(self, ap, free, i):
                self.ap, self.of, self.i = ap, free, i

            @property
            def free(self):
                return self.of[self.i]

            @free.setter
            def free(self, toks):
                self.of[self.i] = toks

        s_banks = [Bank(X[0], xfree, 0), Bank(X[1], xfree, 1)]
        t_banks = [Bank(X[2], xfree, 2)]
        o_banks = [Bank(X[3], xfree, 3)]
        turns = {"s": 0, "t": 0}

        def turn(name, banks):
            turns[name] += 1
            return banks[turns[name] % len(banks)]

        def qk(q, k, k0, i, masks, nm, den, *after):
            bank = turn("s", s_banks)
            n = (i + 1) * 128 - k0
            qt = q[:, i * 128:(i + 1) * 128]
            mm(bank.ap[:, 0:n], qt, k[:, k0:k0 + n], True, False, bank.free, *after)
            for mi, (o, mw, m) in enumerate(masks):
                t = mm(bank.ap[:, o:o + mw], identb[:, :], m, False, mi == len(masks) - 1,
                       k_idb, k_mc, k_mb, k_md, inc=(mi == len(masks) - 1))
            k1 = red(nm, bank.ap[:, 0:n], ALU.max, t, k_stat, negate=True)
            pi, p, fr = prbs.take()
            k2 = act(p[:, 0:n], bank.ap[:, 0:n], ACT.Exp, k1, fr, bias=nm, accum_out=den)
            bank.free = [k2]
            return pi, p[:, 0:n], n // 128, k2

        def turn_p(pi, p, nb, k, q):
            bank = turn("t", t_banks)
            for b in range(nb):
                t = tr(bank.ap[:, b * 128:(b + 1) * 128], p[:, b * 128:(b + 1) * 128], ident[:, :], k, bank.free,
                       inc=(b == nb - 1))
            prbs.free[pi] = [t]
            ti, o, fr = ptrs.take()
            kc = copy(q, o[:, 0:nb * 128], bank.ap[:, 0:nb * 128], t, fr)
            bank.free = [kc]
            return ti, o, kc

        k_od = [None] * 4

        def dilated():
            items = [(i, j, gi) for i in range(4) for j in range(2) for gi in range(3)]
            state, turned = {}, {}

            def scores(n):
                i, j, gi = items[n]
                if gi == 0:
                    state[n // 3] = {"nm": stats(3), "den": stats(3), "w": stats(3), "dw": stats(3), "s": stats(2),
                                     "p": [], "k": []}
                st = state[n // 3]
                q, k = (v[64 * j:64 * j + 64, gi, :] for v in (dq, dk))
                if gi == 0:
                    k0 = 128 * max(i - 1, 0)
                    masks = [(0, 256, mband[:, :, :].rearrange("p a c -> p (a c)"))] if i else [(0, 128, mband[:, 1, :])]
                else:
                    k0 = 0
                    md = md4 if gi == 1 else md16
                    masks = [(128 * b, 128, md[:, 0, :]) for b in range(i)] + [(128 * i, 128, md[:, 1, :])]
                st["p"].append(qk(q, k, k0, i, masks, st["nm"][:, gi:gi + 1], st["den"][:, gi:gi + 1], k_dq, k_dk))

            def combine(s):
                st = state[s]
                nM, r_ = st["s"][:, 0:1], st["s"][:, 1:2]
                k = red(nM, st["nm"], ALU.min, [p[3] for p in st["p"]])
                k = act(st["w"], st["nm"], ACT.Exp, k, bias=nM, scale=-1.0)
                k = tt(dve, st["dw"], st["den"], st["w"], ALU.mult, k)
                k = red(r_, st["dw"], ALU.add, k)
                k = rec(r_, r_, k)
                k = ts(dve, st["w"], st["w"], r_, None, ALU.mult, None, k)
                st["k"] = [ts(dve, p[1], p[1], st["w"][:, gi:gi + 1], None, ALU.mult, None, k)
                           for gi, p in enumerate(st["p"])]

            def weigh(n):
                i, j, gi = items[n]
                bank = o_banks[i % len(o_banks)]
                ti, o, kc = turned.pop(n)
                nb = state[n // 3]["p"][gi][2]
                for b in range(nb):
                    kt = i + 1 - nb + b
                    t = mm(bank.ap[64 * j:64 * j + 64, gi * 128:gi * 128 + 128],
                           dv[:, kt, 128 * gi + 64 * j:128 * gi + 64 * j + 64], o[:, b * 128:(b + 1) * 128],
                           b == 0, b == nb - 1, kc, k_dv, bank.free if j == 0 else None, inc=(b == nb - 1))
                ptrs.free[ti] = [t]
                if j == 1 and gi == 2:
                    k_od[i] = copy(sca, odil[:, :, i * 128:(i + 1) * 128],
                                   bank.ap[:, 0:384].rearrange("p (g t) -> p g t", g=3), t, k_b2)
                    bank.free = [k_od[i]]

            for n in range(4):
                scores(n)
                yield
            combine(0)
            yield
            for n in range(len(items)):
                s, gi = n // 3, n % 3
                if gi == 2 and s + 1 < 8:
                    combine(s + 1)
                pi, p, nb, _ = state[s]["p"][gi]
                turned[n] = turn_p(pi, p, nb, state[s]["k"][gi], dve if n % 2 else sca)
                if n + 4 < len(items):
                    scores(n + 4)
                if n:
                    weigh(n - 1)
                yield
            weigh(len(items) - 1)

        def sigmoid(dst, src, *after):
            k = act(dst, src, ACT.Exp, *after, scale=-1.0)
            return rec(dst, dst, ts(dve, dst, dst, 1.0, None, ALU.add, None, k))

        k_w1 = [load(pool, w1s[64 * g:64 * g + 64, kv, :, :], A["cmp_w1_2"][0, kv].rearrange("(l e) o -> e l o", e=64),
                     k_b2) for kv in range(2) for g in range(2)]
        k_w2 = [load(pool, w2s[64 * g:64 * g + 64, :, :], A["cmp_w2_2"][0].rearrange("v e o -> e v o"), k_b2)
                for g in range(2)]
        k_pe = [load(pool, perow[:, :, g, :], A["cmp_pe_2"][0].rearrange("v l e -> l v e"), k_b2) for g in range(2)]
        k_pc = [None]
        k_q, k_kv, k_nz = [None] * 3, [None] * 4, [None] * 3

        def compress():
            b0, b1 = s_banks
            b2 = t_banks[0]
            for kv in range(2):
                t = tr(b2.ap[:, kv * 32:kv * 32 + 32], perow[:, kv, :, :].rearrange("l g e -> l (g e)"),
                       ident[0:32, 0:32], k_pe, b2.free, inc=True)
            k = copy(dve, pes[:, :, :].rearrange("p v l -> p (v l)"), b2.ap[:, 0:64], t, k_b2)
            b2.free = [k]
            t2 = None
            for kv in range(2):
                assert k_kv[kv]
                src = kvn[:, kv, :]
                win_ = bass.AP(tensor=src.tensor, offset=src.offset, ap=[list(src.ap[0]), [16, 31], [1, 32]])
                kb = tt(dve, blk[:, :, :], win_, pes[:, kv, :].unsqueeze(1).to_broadcast([128, 31, 32]), ALU.add,
                        k, k_kv[kv], t2)
                yield
                for l in range(32):
                    for g in range(2):
                        sl = slice(64 * g, 64 * g + 64)
                        t = mm(b0.ap[sl, 0:31], w1s[sl, kv, l, :], blk[sl, :, l], l == 0, l == 31, kb, k_w1, b0.free,
                               inc=(l == 31 and g == 1))
                    if l % 16 == 15:
                        yield
                t2 = t
                kh = sigmoid(hcs[:, 0:31], b0.ap[:, 0:31], t, k_pc[0])
                kh = tt(dve, hcs[:, 0:31], b0.ap[:, 0:31], hcs[:, 0:31], ALU.mult, kh)
                b0.free = [kh]
                yield
                for g in range(2):
                    sl = slice(64 * g, 64 * g + 64)
                    if kv == 0:
                        t = mm(b1.ap[sl, 0:31], w2s[sl, kv, :], hcs[sl, 0:31], True, True, kh, k_w2, b1.free,
                               inc=True)
                    else:
                        t = mm(b1.ap[0:31, 64 * g:64 * g + 64], hcs[sl, 0:31], w2s[sl, kv, :], True, True, kh, k_w2,
                               b1.free, t, inc=True)
                    if g == 1 and kv == 0:
                        k_pc[0] = copy(dve, kcs[:, 0:31], b1.ap[:, 0:31], t)
                        b1.free = [k_pc[0]]
                if kv == 1:
                    k_vc = copy(dve, vcs[:, :], b1.ap[0:31, 0:128], t)
                    b1.free = [k_vc]
            k_s = []
            for g in range(2):
                bank = s_banks[g]
                v = bank.ap[:, 0:384].rearrange("p (a n) -> p a n", n=32)
                sl = slice(64 * g, 64 * g + 64)
                for i in range(4):
                    for r_ in range(3):
                        t = mm(v[:, i * 3 + r_, 0:31], qn[sl, r_, i * 128:(i + 1) * 128], kcs[sl, 0:31], True, True,
                               k_q, k_pc[0], bank.free, inc=(i == 3 and r_ == 2))
                for i in range(4):
                    k = tt(dve, pcmp[:, i * 6 + g * 3:i * 6 + g * 3 + 3, 0:31], v[:, i * 3:i * 3 + 3, 0:31],
                           mcmp[:, i, :].unsqueeze(1).to_broadcast([128, 3, 31]), ALU.add, t, t2, k_cm)
                    k_s.append(k)
                bank.free = [k]
                yield
            pc = pcmp[:, :, 0:31]
            mx, dn = pcs[:, 0, :], pcs[:, 1, :]
            bc = lambda v: v.unsqueeze(2).to_broadcast([128, 24, 31])
            k = red(mx, pc, ALU.max, k_s)
            k = ts(dve, mx, mx, -1.0e20, None, ALU.max, None, k)
            k = tt(dve, pc, pc, bc(mx), ALU.subtract, k)
            k = act(pc, pc, ACT.Exp, k)

            def finish():
                k1 = red(dn, pc, ALU.add, k)
                k1 = ts(dve, dn, dn, 1e-30, None, ALU.max, None, k1)
                k1 = rec(dn, dn, k1)
                gc = gates[:, :, :].rearrange("p i (n b) -> p (i n) b", b=3)[:, :, 0]
                k1 = tt(dve, dn, dn, gc, ALU.mult, k1, k_gt)
                k_pc[0] = [tt(dve, pc, pc, bc(dn), ALU.mult, k1), k_vc]
                for n in range(KD):
                    AO.war[n] = now(k_od, k_b2, k_pe, k_pc[0])
            k_pc.append(finish)

        def sparse():
            items = [(r_, i, g, b) for r_ in range(3) for i in range(4) for g in range(2) for b in range(2)]
            state, scaled, turned = {}, {}, {}
            pct_free = [now(sqs.free), now(sqs.free)]
            pct_tok = [None, None]

            def scores(n):
                r_, i, g, b = items[n]
                nm, den = stats(1), stats(1)
                sl = slice(64 * g, 64 * g + 64)
                state[n] = (den, *qk(qn[sl, r_, :], kvn[sl, 2 + b, :], 0, i, [(128 * i, 128, mcaus[:, :])], nm, den,
                                     k_q, k_kv))

            def scale(n):
                r_, i, g, b = items[n]
                den, pi, p, nb, k = state[n]
                c = (g * 3 + r_) * 3 + 1 + b
                k = rec(den, den, k)
                scaled[n] = ts(dve, p, p, den, gates[:, i, c:c + 1], ALU.mult, ALU.mult, k, k_gt)

            def coarse(n):
                r_, _, g, _ = items[n]
                bank = turn("t", t_banks)
                for i in range(4):
                    t = tr(bank.ap[0:31, i * 128:(i + 1) * 128], pcmp[:, i * 6 + g * 3 + r_, 0:31], ident[:, :],
                           k_pc[0], bank.free, inc=(i == 3))
                pct_tok[g] = copy(sca, sq_t[0:31, g, :], bank.ap[0:31, :], t, pct_free[g])
                bank.free = [pct_tok[g]]

            def weigh(n):
                r_, i, g, b = items[n]
                bank = o_banks[r_ % 2]
                o = bank.ap[64 * g:64 * g + 64, i * 128:(i + 1) * 128]
                sl = slice(64 * g, 64 * g + 64)
                if b == 0:
                    t = mm(o, vcs[:, sl], sq_t[0:31, g, i * 128:(i + 1) * 128], True, False, k_pc[0], pct_tok[g],
                           bank.free if i == 0 else None, inc=True)
                    if i == 3:
                        pct_free[g] = [t]
                ti, p, kc = turned.pop(n)
                for j in range(i + 1):
                    t = mm(o, vnt[:, j, 128 * b + 64 * g:128 * b + 64 * g + 64], p[:, j * 128:(j + 1) * 128], False,
                           b == 1 and j == i, kc, k_v, inc=(j == i))
                ptrs.free[ti] = [t]
                if i == 3 and g == 1 and b == 1:
                    assert k_nz[r_]
                    ti, y, fr = tmps.take()
                    k = tt(dve, y, bank.ap[:, :], nz[:, r_, :], ALU.mult, t, k_nz[r_], fr)
                    bank.free = [k]
                    split_tile(ti, y, k, AO, 2 + r_)

            assert all(k_q + k_kv)
            scores(0)
            yield
            k_pc.pop()()
            scores(1)
            yield
            coarse(0)
            scores(2)
            scale(0)
            yield
            for n in range(len(items)):
                if n + 1 < len(items):
                    scale(n + 1)
                if n + 2 < len(items) and items[n + 2][1] == 0 and items[n + 2][3] == 0:
                    coarse(n + 2)
                turned[n] = turn_p(*state.pop(n)[1:4], scaled.pop(n), dve if n % 2 else sca)
                if n + 3 < len(items):
                    scores(n + 3)
                if n:
                    weigh(n - 1)
                yield
            weigh(len(items) - 1)
            sqs.free = [pct_free[0], pct_free[1]]

        def attention():
            yield from dilated()
            yield from compress()
            yield from sparse()

        background.append(attention())

        done = gemm(plan["vg"], XO, 4, by_token=True, pumps=(1, 3))
        k_v, k_gt = [], []
        for i in range(4):
            k_v.append(act(vnt[:, i, :], G[i][:, 0:256], ACT.Copy, done[i], st.rt, scale=rtok[:, i:i + 1]))
            k_gt.append(ts(dve, gates[:, i, :], G[i][:, 256:274], rtok[:, i:i + 1], None, ALU.mult, None, k_v[i]))
            gfree[i] = [k_v[i], k_gt[i]]
        rtok_free[0] = now(rtok_free, k_dv, k_v, k_gt)
        k_gt = sigmoid(gates[:, :, :], gates[:, :, :], k_gt)

        t_banks.append(Bank(G[2], gfree, 2))
        o_banks.append(Bank(G[3], gfree, 3))
        kept = {}

        def store_tile(n, dst, *after, scale=1.0):
            b, t = gemm_tile(n)
            gfree[b] = [stt(dst, G[b][:, :], scale, rpre[:, :], ALU.mult, ALU.mult, st.k, t, *after)]
            return gfree[b][0]

        for (name, m), n in tiles_in:
            if name == "q":
                k_q[m] = store_tile(n, qn[:, m, :], k_b2, scale=0.125)
            elif name == "kv":
                k_kv[m] = store_tile(n, kvn[:, m, :], k_b2)
            elif name == "nz":
                k_nz[m] = store_tile(n, nz[:, m, :], k_b2)
                if m == 2:
                    k_nz[:] = [act(nz[:, r_, :], nz[:, r_, :], ACT.Silu, k_nz[r_]) for r_ in range(3)]
            elif name in "bc":
                assert all(k_od)
                kept[name, m] = store_tile(n, (cab if name == "b" else cac)[:, m, :], k_b2, k_od)
            elif name == "h":
                u, cv = cac[:, m, :], ccv[:, m, :]
                w = lambda n, m=m: cols[:, colat["conv_w_2"] + 2 * n + m:colat["conv_w_2"] + 2 * n + m + 1]
                si, s, fr = acts.take()
                k0 = store_tile(n, s, fr)
                k0 = tt(dve, u, s, u, ALU.mult, kept["c", m], k0)
                acts.free[si] = [k0]
                k = ts(dve, cv, u, w(2), col("conv_b_2", m), ALU.mult, ALU.add, k0, k_b2, k_od)
                k = stt(cv[:, 1:], u[:, :T - 1], w(1), cv[:, 1:], ALU.mult, ALU.add, k)
                k = stt(cv[:, 2:], u[:, :T - 2], w(0), cv[:, 2:], ALU.mult, ALU.add, k)
                kept["h", m] = tt(pool, cv, cv, cab[:, m, :], ALU.mult, k, kept["b", m])
            else:
                si, s, fr = acts.take()
                kept[name, m] = (si, s, store_tile(n, s, fr))
                acts.free[si] = [kept[name, m][2]]
            for last_tile, other, first in ((("z", 1), "h", 0), (("dz", 2), None, 5)):
                if (name, m) == last_tile:
                    assert AO.war[0]
                    sil = [(kept[name, j], act(kept[name, j][1], kept[name, j][1], ACT.Silu, kept[name, j][2]))
                           for j in range(m + 1)]
                    for j, ((si, s, _), k) in enumerate(sil):
                        ti, t, fr = tmps.take()
                        o, ko = (ccv[:, j, :], kept["h", j]) if other else (odil[:, j, :], k_od)
                        k = tt(pool, t, s, o, ALU.mult, k, ko, fr)
                        acts.free[si] = [k]
                        later.append(lambda ti=ti, t=t, k=k, n=first + j: split_tile(ti, t, k, AO, n))
                elif other and (name, m) == ("dz", 0):
                    while later:
                        later.pop(0)()
        drain_background()
        while later:
            later.pop(0)()

        k_all = now(k_pc[0], AO.ready, list(kept[n, m] for n in "bch" for m in range(2)))
        k_p = load(pool, prow[:, :, :], A["p_2"][0, 0].rearrange("(i p) c -> p i c", p=128), k_all)
        background.append(embed(k_p, k_all))

        for c in range(2):
            done = gemm(plan["out2", c], AO, 4, pumps=(3,) if c else (), ks=out2_k)
            for m in range(4):
                j = 4 * c + m
                h_tok[j] = tt(dve, hs[j], G[m][:, :], hs[j], ALU.add, done[m], h_tok[j])
                gfree[m] = [h_tok[j]]
                split_tile(None, hs[j], h_tok[j], XO, j)

        drain_background()
        k_att = now(f_tok, ptrs.free, prbs.free)

        class Final(Sums):

            def __init__(self):
                Sums.__init__(self)
                self.gained = []

            def tile(self, j):
                if j < 4:
                    self.gather(hs[j], h_tok[j])
                else:
                    self.add(hs[j], h_tok[j], j == KD - 1, sqs if j < 6 else acts)
                self.gained.append(ts(dve, fs[j], hs[j], col("norm_final_2", j), None, ALU.mult,
                                      None, h_tok[j], k_att))

            def hooks(self):
                return {(6, 0): self.gathered}

        last = Final()

        def use_p2(j, ps, s, tk):
            ti, t, fr = tmps.take()
            k0 = tt(dve, t, ps, s, ALU.mult, tk, fr)
            h_tok[j] = tt(dve, hs[j], hs[j], t, ALU.add, k0, h_tok[j], XO.ready[j])
            tmps.free[ti] = [h_tok[j]]
            last.tile(j)
            return k0

        gated("pg2", "pp2", PO, use_p2, None, hooks=({}, last.hooks()), soon=True)
        last.factor()
        orow = out[0].rearrange("(i p) c -> p i c", p=128)
        banks = [(X[1], xfree, 1), (X[2], xfree, 2), (X[3], xfree, 3)] + [(G[i], gfree, i) for i in range(4)]
        for n in range(8):
            hf, i = n // 4, n % 4
            bank, free, b = banks[n % 7]
            for j in range(4):
                q = tr(bank[:, j * 128:(j + 1) * 128], fs[4 * hf + j][:, i * 128:(i + 1) * 128], ident[:, :],
                       last.gained[4 * hf + j], free[b], inc=(j == 3))
            _, r, fr = (acts, tmps)[n % 2].take()
            if n % 2:
                k = ts(dve, r, bank[:, :], rtok[:, i:i + 1], None, ALU.mult, None, q, last.rt, fr)
            else:
                k = act(r, bank[:, :], ACT.Copy, q, last.rt, fr, scale=rtok[:, i:i + 1])
            free[b] = [k]
            sp.put(lambda e, i=i, hf=hf, r=r: e.dma_start(orow[:, i, hf * 512:hf * 512 + 512], r).then_inc(s_out, 16), k,
                   inc=False)

        block = ctx.enter_context(nc.Block())

        @block.sync
        def _(e):
            sp.run(e)
            e.wait_ge(s_out, 16 * KD)

        @block.gpsimd
        def _(e):
            pool.run(e)

        @block.vector
        def _(e):
            dve.run(e)

        @block.scalar
        def _(e):
            sca.run(e)

        @block.tensor
        def _(e):
            pe.run(e)


_INS = ["x", "p", "ffn1_pre_g", "ffn1_w_gate", "ffn1_w_up", "ffn1_w_down", "ffn1_post_g", "mix_pre_g", "w_in",
        "sgu_norm_g", "sgu_w", "sgu_b", "pool_w", "pool_scale", "w_out_a", "w_out_b", "w_o", "mix_post_g", "ffn2_pre_g",
        "ffn2_w_gate", "ffn2_w_up", "ffn2_w_down", "ffn2_post_g", "ple_pre_g", "ple_w_gate", "ple_w_proj",
        "ple_post_g", "p_2", "norm_mix_2", "w_in_2", "conv_w_2", "conv_b_2", "cmp_pe_2", "cmp_w1_2", "cmp_w2_2",
        "w_out_2", "w_ple_gate_2", "w_ple_proj_2", "norm_final_2"]
_OUTS = [((1, 512, 1024), "float32")]


def kernel(**inputs):
    import numpy as _np
    import concourse.bacc as _bacc
    from concourse import mybir as _mybir
    from concourse.bass_utils import run_bass_kernel_spmd as _run

    nc = _bacc.Bacc("TRN2", target_bir_lowering=False, num_devices=1)
    arrays, args = {}, {}
    for name in _INS:
        v = _np.ascontiguousarray(inputs[name])
        arrays[f"in_{name}_dram"] = v
        args[name] = nc.dram_tensor(f"in_{name}_dram", v.shape, _mybir.dt.from_np(v.dtype), kind="ExternalInput").ap()
    outs = []
    for i, (shape, dtype) in enumerate(_OUTS):
        dt = _mybir.dt.from_np(_np.dtype(dtype))
        outs.append(nc.dram_tensor(f"out_{i}_dram", shape, dt, kind="ExternalOutput").ap())
    two_blocks(nc, args, outs[0])
    r = _run(nc, [arrays], core_ids=[0])
    return r.results[0]["out_0_dram"]
```
